# Optimizing a Trainium2 kernel written in Bass

```python
import jax, jax.numpy as jnp
from jax import lax
import numpy as np
import math
import jax
import jax.numpy as jnp

D_MODEL = 1024
BATCH = 1
SEQ = 256
DEPTH = 2

N_MIXERS = 2
SB_HEADS = 16
SB_HEAD_DIM = D_MODEL // SB_HEADS
SB_BLOCK = 128
RET_HEADS = 4
RET_QK_DIM = D_MODEL // RET_HEADS
RET_V_DIM = 2 * D_MODEL // RET_HEADS
RET_CHUNK = 128
ROPE_BASE = 10000.0
MLP_HIDDEN = 4 * D_MODEL
RMS_EPS = 1e-6
GN_EPS = 1e-6
N_SB_LAYERS = (DEPTH + N_MIXERS - 1) // N_MIXERS
N_RET_LAYERS = DEPTH // N_MIXERS


F32 = jnp.float32

def rms_norm(x, g):
    xf = x.astype(F32)
    y = xf * lax.rsqrt(jnp.mean(xf * xf, axis=-1, keepdims=True) + RMS_EPS)
    return (y * g.astype(F32)).astype(x.dtype)

def stick_breaking_attention(h, w_in, w_out):
    b, s, _ = h.shape
    q, k, v = jnp.split(h @ w_in, 3, axis=-1)

    def heads(t):
        return t.reshape(b, s, SB_HEADS, SB_HEAD_DIM).transpose(0, 2, 1, 3).astype(F32)

    q, k, v = heads(q), heads(k), heads(v)
    scale = SB_HEAD_DIM ** -0.5
    outs = []
    for blk in range(s // SB_BLOCK):
        start = blk * SB_BLOCK
        end = start + SB_BLOCK
        qb = q[:, :, start:end]
        kp = k[:, :, :end]
        vp = v[:, :, :end]
        z = jnp.einsum('bhqd,bhkd->bhqk', qb, kp) * scale
        t_idx = start + jnp.arange(SB_BLOCK)[:, None]
        s_idx = jnp.arange(end)[None, :]
        mask = s_idx < t_idx
        log_keep = jnp.where(mask, jax.nn.log_sigmoid(-z), 0.0)
        later = lax.cumsum(log_keep, axis=3, reverse=True) - log_keep
        a = jnp.where(mask, jnp.exp(jax.nn.log_sigmoid(z) + later), 0.0)
        outs.append(jnp.einsum('bhqk,bhkd->bhqd', a, vp))
    o = jnp.concatenate(outs, axis=2)
    o = o.transpose(0, 2, 1, 3).reshape(b, s, D_MODEL).astype(h.dtype)
    return o @ w_out

def rotary(x, pos):
    half = x.shape[-1] // 2
    inv_freq = 1.0 / (ROPE_BASE ** jnp.linspace(0.0, 1.0, half, dtype=F32))
    ang = pos.astype(F32)[:, None] * inv_freq[None, :]
    cos, sin = jnp.cos(ang), jnp.sin(ang)
    x1, x2 = x[..., :half], x[..., half:]
    return jnp.concatenate([x1 * cos - x2 * sin, x1 * sin + x2 * cos], axis=-1)

def retention(h, w_in, w_out):
    b, s, _ = h.shape
    c = RET_CHUNK
    nc = s // c
    q, k, v, g = jnp.split(h @ w_in, [D_MODEL, 2 * D_MODEL, 4 * D_MODEL], axis=-1)
    q = q.reshape(b, s, RET_HEADS, RET_QK_DIM).transpose(0, 2, 1, 3).astype(F32)
    k = k.reshape(b, s, RET_HEADS, RET_QK_DIM).transpose(0, 2, 1, 3).astype(F32)
    v = v.reshape(b, s, RET_HEADS, RET_V_DIM).transpose(0, 2, 1, 3).astype(F32)
    pos = jnp.arange(s)
    q = rotary(q, pos)
    k = rotary(k, pos) * (RET_QK_DIM ** -0.5)

    log_gamma = jnp.log1p(-jnp.exp2(-5.0 - jnp.arange(RET_HEADS, dtype=F32)))
    idx = jnp.arange(c, dtype=F32)
    rel = idx[:, None] - idx[None, :]
    decay_in = jnp.where(rel >= 0, jnp.exp(log_gamma[:, None, None] * jnp.maximum(rel, 0.0)), 0.0)
    q_decay = jnp.exp(log_gamma[:, None] * (idx + 1.0))[None, :, :, None]
    k_decay = jnp.exp(log_gamma[:, None] * (c - 1.0 - idx))[None, :, :, None]
    chunk_decay = jnp.exp(log_gamma * c)[None, :, None, None]

    qc = q.reshape(b, RET_HEADS, nc, c, RET_QK_DIM)
    kc = k.reshape(b, RET_HEADS, nc, c, RET_QK_DIM)
    vc = v.reshape(b, RET_HEADS, nc, c, RET_V_DIM)

    scores = jnp.einsum('bhnid,bhnjd->bhnij', qc, kc) * decay_in[None, :, None]
    inner = jnp.einsum('bhnij,bhnje->bhnie', scores, vc)

    def step(state, xs):
        q_n, k_n, v_n = xs
        cross = jnp.einsum('bhid,bhde->bhie', q_n, state) * q_decay
        state = state * chunk_decay + jnp.einsum('bhjd,bhje->bhde', k_n * k_decay, v_n)
        return state, cross

    state0 = jnp.zeros((b, RET_HEADS, RET_QK_DIM, RET_V_DIM), F32)
    xs = (qc.transpose(2, 0, 1, 3, 4), kc.transpose(2, 0, 1, 3, 4), vc.transpose(2, 0, 1, 3, 4))
    _, cross = lax.scan(step, state0, xs)
    o = (inner + cross.transpose(1, 2, 0, 3, 4)).reshape(b, RET_HEADS, s, RET_V_DIM)

    mu = jnp.mean(o, axis=-1, keepdims=True)
    var = jnp.mean(jnp.square(o - mu), axis=-1, keepdims=True)
    o = (o - mu) * lax.rsqrt(var + GN_EPS)
    o = o.transpose(0, 2, 1, 3).reshape(b, s, RET_HEADS * RET_V_DIM)
    y = jax.nn.silu(g.astype(F32)) * o
    return y.astype(h.dtype) @ w_out

def squared_relu_mlp(h, w_up, w_down):
    u = jax.nn.relu(h @ w_up)
    return (u * u) @ w_down

def first_inputs(seed: int = 0) -> dict:
    key = jax.random.key(seed)
    ks = jax.random.split(key, 11)

    def w(k, shape, fan_in):
        return jax.random.normal(k, shape, F32) * (fan_in ** -0.5)

    def gain(k, shape):
        return 1.0 + 0.05 * jax.random.normal(k, shape, F32)

    return {
        "x": jax.random.normal(ks[0], (BATCH, SEQ, D_MODEL), F32),
        "w_sb_in": w(ks[1], (N_SB_LAYERS, D_MODEL, 3 * D_MODEL), D_MODEL),
        "w_sb_out": w(ks[2], (N_SB_LAYERS, D_MODEL, D_MODEL), D_MODEL),
        "w_ret_in": w(ks[3], (N_RET_LAYERS, D_MODEL, 6 * D_MODEL), D_MODEL),
        "w_ret_out": w(ks[4], (N_RET_LAYERS, 2 * D_MODEL, D_MODEL), 2 * D_MODEL),
        "g_mix": gain(ks[5], (DEPTH, D_MODEL)),
        "g_mlp": gain(ks[6], (DEPTH, D_MODEL)),
        "w_mlp_up": w(ks[7], (DEPTH, D_MODEL, MLP_HIDDEN), D_MODEL),
        "w_mlp_down": w(ks[8], (DEPTH, MLP_HIDDEN, D_MODEL), MLP_HIDDEN),
        "g_final": gain(ks[9], (D_MODEL,)),
    }

def first_block(x, w_sb_in, w_sb_out, w_ret_in, w_ret_out, g_mix, g_mlp, w_mlp_up, w_mlp_down, g_final):
    h = x
    for layer in range(DEPTH):
        hn = rms_norm(h, g_mix[layer])
        i = layer // N_MIXERS
        if layer % N_MIXERS == 0:
            h = h + stick_breaking_attention(hn, w_sb_in[i], w_sb_out[i])
        else:
            h = h + retention(hn, w_ret_in[i], w_ret_out[i])
        h = h + squared_relu_mlp(rms_norm(h, g_mlp[layer]), w_mlp_up[layer], w_mlp_down[layer])
    return rms_norm(h, g_final)


DEPTH_2 = 1

N_META = 16
BLOCK = 128
PAD = BLOCK - N_META
EPS = 1e-6
NEG_INF = -1e30
H_A = 8
DK_A = 128
DV_A = 128
CONV_K = 4
CHUNK = 64
H_B = 8
DH_B = 128
FORGET_BIAS = 2.0
N_KEYS = 128
N_EXPERTS = N_KEYS * N_KEYS
H_P = 8
D_QP = 256
TOPK = 16
PEER_BLOCK = 256

A_QK = H_A * DK_A
A_V = H_A * DV_A
B_W = H_B * DH_B
BRANCH_W = A_V
CONV_CH = 2 * A_QK + A_V
IN_SIZES = (CONV_CH, A_V, H_A, H_A, 3 * B_W, H_B, 2 * D_MODEL)
IN_COLS = 2 * A_QK + 2 * A_V + 2 * H_A + 3 * B_W + H_B + 2 * D_MODEL


def rms_norm_2(x, w):
    xf = x.astype(jnp.float32)
    y = xf * lax.rsqrt(jnp.mean(xf * xf, axis=-1, keepdims=True) + EPS)
    return (y * w.astype(jnp.float32)).astype(x.dtype)

def l2_norm(x):
    xf = x.astype(jnp.float32)
    return (xf * lax.rsqrt(jnp.sum(xf * xf, axis=-1, keepdims=True) + EPS)).astype(x.dtype)

def pad_front(t):
    return jnp.pad(t, [(0, 0), (PAD, 0)] + [(0, 0)] * (t.ndim - 2))

def split_cols(t, sizes):
    return jnp.split(t, [int(s) for s in np.cumsum(sizes)[:-1]], axis=-1)

def causal_dwconv_silu(x, w):
    y = lax.conv_general_dilated(x, w.astype(x.dtype)[:, None, :], window_strides=(1,),
                                 padding=[(CONV_K - 1, 0)],
                                 dimension_numbers=('NWC', 'WIO', 'NWC'),
                                 feature_group_count=x.shape[-1])
    return jax.nn.silu(y)

def gated_delta_rule(q, k, v, beta, g):
    out_dtype = v.dtype
    B_, Lp, H, _ = k.shape
    DV = v.shape[-1]
    N = Lp // CHUNK

    def to_chunks(t):
        t = t.astype(jnp.float32).reshape((B_, N, CHUNK, H) + t.shape[3:])
        return jnp.swapaxes(t, 2, 3)

    q, k, v, beta, g = (to_chunks(t) for t in (q, k, v, beta, g))
    G = jnp.cumsum(g, axis=-1)
    incl = jnp.tril(jnp.ones((CHUNK, CHUNK), bool))
    strict = jnp.tril(jnp.ones((CHUNK, CHUNK), bool), -1)
    diff = G[..., :, None] - G[..., None, :]
    gamma = jnp.where(incl, jnp.exp(jnp.where(incl, diff, 0.0)), 0.0)
    k_beta = k * beta[..., None]
    a_mat = jnp.where(strict, jnp.einsum('bnhcd,bnhsd->bnhcs', k_beta, k) * gamma, 0.0) \
        + jnp.eye(CHUNK, dtype=jnp.float32)
    rhs = jnp.concatenate([v * beta[..., None], k_beta * jnp.exp(G)[..., None]], axis=-1)
    sol = lax.linalg.triangular_solve(a_mat, rhs, left_side=True, lower=True, unit_diagonal=True)
    u, w = sol[..., :DV], sol[..., DV:]
    attn = jnp.einsum('bnhcd,bnhsd->bnhcs', q, k) * gamma
    q_dec = q * jnp.exp(G)[..., None]
    k_tail = k * jnp.exp(G[..., -1:] - G)[..., None]
    chunk_dec = jnp.exp(G[..., -1])

    def step(S, inp):
        qd, w_c, u_c, at, kt, dec = inp
        v_new = u_c - jnp.einsum('bhcd,bhde->bhce', w_c, S)
        o = jnp.einsum('bhcd,bhde->bhce', qd, S) + jnp.einsum('bhcs,bhse->bhce', at, v_new)
        S = S * dec[..., None, None] + jnp.einsum('bhcd,bhce->bhde', kt, v_new)
        return S, o

    xs = tuple(jnp.moveaxis(t, 1, 0) for t in (q_dec, w, u, attn, k_tail, chunk_dec))
    S0 = jnp.zeros((B_, H, k.shape[-1], DV), jnp.float32)
    _, o = lax.scan(step, S0, xs)
    o = jnp.swapaxes(jnp.moveaxis(o, 0, 1), 2, 3).reshape(B_, Lp, H, DV)
    return o.astype(out_dtype)

def forgetting_attention(q, k, v, log_f):
    Lp = q.shape[1]
    scale = DH_B ** -0.5
    cum = jnp.swapaxes(jnp.cumsum(log_f, axis=1), 1, 2)
    pos = jnp.arange(Lp)
    outs = []
    for i in range(Lp // BLOCK):
        lo, hi = i * BLOCK, (i + 1) * BLOCK
        s = jnp.einsum('bthd,bshd->bhts', q[:, lo:hi], k[:, :hi]).astype(jnp.float32) * scale
        bias = cum[:, :, lo:hi, None] - cum[:, :, None, :hi]
        allowed = (pos[None, :hi] <= pos[lo:hi, None]) & (pos[None, :hi] >= PAD)
        p = jax.nn.softmax(jnp.where(allowed, s + bias, NEG_INF), axis=-1).astype(v.dtype)
        outs.append(jnp.einsum('bhts,bshd->bthd', p, v[:, :hi]))
    return jnp.concatenate(outs, axis=1)

def hybrid_mixer(h, w_in, conv_w, a_log, dt_bias, o_norm_a, q_norm_b, k_norm_b, f_bias,
                 w_branch, w_out):
    B_, L, _ = h.shape
    proj = h @ w_in
    qkv_a, z_a, b_a, a_a, qkv_b, f_b, gates = split_cols(proj, IN_SIZES)
    qkv_a = causal_dwconv_silu(pad_front(qkv_a), conv_w)
    Lp = qkv_a.shape[1]
    qa, ka, va = split_cols(qkv_a, (A_QK, A_QK, A_V))
    qa = l2_norm(qa.reshape(B_, Lp, H_A, DK_A)) * (DK_A ** -0.5)
    ka = l2_norm(ka.reshape(B_, Lp, H_A, DK_A))
    va = va.reshape(B_, Lp, H_A, DV_A)
    beta = pad_front(jax.nn.sigmoid(b_a))
    g = pad_front(-jnp.exp(a_log) * jax.nn.softplus(a_a + dt_bias))
    o_a = gated_delta_rule(qa, ka, va, beta, g)[:, PAD:]
    o_a = rms_norm_2(o_a, o_norm_a) * jax.nn.silu(z_a.reshape(B_, L, H_A, DV_A))
    qb, kb, vb = split_cols(qkv_b, (B_W, B_W, B_W))
    qb = rms_norm_2(qb.reshape(B_, L, H_B, DH_B), q_norm_b)
    kb = rms_norm_2(kb.reshape(B_, L, H_B, DH_B), k_norm_b)
    vb = vb.reshape(B_, L, H_B, DH_B)
    log_f = jax.nn.log_sigmoid((f_b + f_bias).astype(jnp.float32))
    o_b = forgetting_attention(pad_front(qb), pad_front(kb), pad_front(vb), pad_front(log_f))[:, PAD:]
    o = jnp.stack([o_a.reshape(B_, L, BRANCH_W), o_b.reshape(B_, L, BRANCH_W)], axis=2)
    y = jnp.einsum('blgc,gcd->blgd', o, w_branch)
    gate = jax.nn.sigmoid(gates.reshape(B_, L, 2, D_MODEL))
    return jnp.sum(gate * y, axis=2) @ w_out

def peer_ffn(h, wq, sub_keys, expert_u, expert_v):
    B_, L, D = h.shape
    T = B_ * L
    n_blk = -(-T // PEER_BLOCK)
    tokens = jnp.pad(h.reshape(T, D), [(0, n_blk * PEER_BLOCK - T), (0, 0)])
    tokens = tokens.reshape(n_blk, PEER_BLOCK, D)

    def one_block(xb):
        qh = (xb @ wq).reshape(PEER_BLOCK, H_P, 2, D_QP // 2)
        s1 = jnp.einsum('thd,hnd->thn', qh[:, :, 0], sub_keys[0]).astype(jnp.float32)
        s2 = jnp.einsum('thd,hnd->thn', qh[:, :, 1], sub_keys[1]).astype(jnp.float32)
        v1, i1 = lax.top_k(s1, TOPK)
        v2, i2 = lax.top_k(s2, TOPK)
        cand = (v1[..., :, None] + v2[..., None, :]).reshape(PEER_BLOCK, H_P, TOPK * TOPK)
        sc, ci = lax.top_k(cand, TOPK)
        idx = jnp.take_along_axis(i1, ci // TOPK, axis=-1) * N_KEYS \
            + jnp.take_along_axis(i2, ci % TOPK, axis=-1)
        gate_w = jax.nn.softmax(sc, axis=-1)
        act = jax.nn.gelu(jnp.einsum('thkd,td->thk', expert_u[idx], xb).astype(jnp.float32),
                          approximate=False)
        coef = (gate_w * act).astype(xb.dtype)
        return jnp.einsum('thk,thkd->td', coef, expert_v[idx])

    out = lax.map(one_block, tokens)
    return out.reshape(n_blk * PEER_BLOCK, D)[:T].reshape(B_, L, D)

def second_inputs(seed: int = 0) -> dict:
    key = jax.random.key(seed)
    ks = jax.random.split(key, 18)

    def nrm(k, shape, scale):
        return scale * jax.random.normal(k, shape, jnp.float32)

    dt = jnp.exp(jax.random.uniform(ks[6], (DEPTH_2, H_A), jnp.float32,
                                    math.log(1e-3), math.log(1e-1)))
    return {
        'x': nrm(ks[0], (BATCH, SEQ, D_MODEL), 1.0),
        'meta_tokens': nrm(ks[1], (N_META, D_MODEL), 1.0),
        'norm_mix': 1.0 + nrm(ks[2], (DEPTH_2, D_MODEL), 0.02),
        'w_in': nrm(ks[3], (DEPTH_2, D_MODEL, IN_COLS), D_MODEL ** -0.5),
        'conv_w': nrm(ks[4], (DEPTH_2, CONV_K, CONV_CH), CONV_K ** -0.5),
        'a_log': jnp.log(jax.random.uniform(ks[5], (DEPTH_2, H_A), jnp.float32, 1.0, 16.0)),
        'dt_bias': dt + jnp.log(-jnp.expm1(-dt)),
        'o_norm_a': 1.0 + nrm(ks[7], (DEPTH_2, DV_A), 0.02),
        'q_norm_b': 1.0 + nrm(ks[8], (DEPTH_2, DH_B), 0.02),
        'k_norm_b': 1.0 + nrm(ks[9], (DEPTH_2, DH_B), 0.02),
        'f_bias': FORGET_BIAS + nrm(ks[10], (DEPTH_2, H_B), 0.1),
        'w_branch': nrm(ks[11], (DEPTH_2, 2, BRANCH_W, D_MODEL), BRANCH_W ** -0.5),
        'w_out': nrm(ks[12], (DEPTH_2, D_MODEL, D_MODEL), D_MODEL ** -0.5),
        'norm_ffn': 1.0 + nrm(ks[13], (DEPTH_2, D_MODEL), 0.02),
        'peer_wq': nrm(ks[14], (DEPTH_2, D_MODEL, H_P * D_QP), D_MODEL ** -0.5),
        'peer_sub_keys': nrm(ks[15], (DEPTH_2, 2, H_P, N_KEYS, D_QP // 2), (D_QP // 2) ** -0.5),
        'expert_u': nrm(ks[16], (DEPTH_2, N_EXPERTS, D_MODEL), D_MODEL ** -0.5),
        'expert_v': nrm(ks[17], (DEPTH_2, N_EXPERTS, D_MODEL), D_MODEL ** -0.5),
    }

def second_block(x, meta_tokens, norm_mix, w_in, conv_w, a_log, dt_bias, o_norm_a, q_norm_b,
              k_norm_b, f_bias, w_branch, w_out, norm_ffn, peer_wq, peer_sub_keys,
              expert_u, expert_v):
    B_ = x.shape[0]
    meta = jnp.broadcast_to(meta_tokens.astype(x.dtype)[None], (B_, N_META, D_MODEL))
    res = jnp.concatenate([meta, x], axis=1)
    for layer in range(DEPTH_2):
        res = res + hybrid_mixer(rms_norm_2(res, norm_mix[layer]), w_in[layer], conv_w[layer],
                                 a_log[layer], dt_bias[layer], o_norm_a[layer],
                                 q_norm_b[layer], k_norm_b[layer], f_bias[layer],
                                 w_branch[layer], w_out[layer])
        res = res + peer_ffn(rms_norm_2(res, norm_ffn[layer]), peer_wq[layer],
                             peer_sub_keys[layer], expert_u[layer], expert_v[layer])
    return res[:, N_META:]


def setup_inputs(seed=0):
    out = dict(first_inputs(seed))
    for name, value in second_inputs(seed + 1).items():
        if name != "x":
            out[name + "_2"] = value
    return out


def reference(
    x, w_sb_in, w_sb_out, w_ret_in, w_ret_out, g_mix, g_mlp, w_mlp_up, w_mlp_down, g_final,
    meta_tokens_2, norm_mix_2, w_in_2, conv_w_2, a_log_2, dt_bias_2, o_norm_a_2, q_norm_b_2,
    k_norm_b_2, f_bias_2, w_branch_2, w_out_2, norm_ffn_2, peer_wq_2, peer_sub_keys_2,
    expert_u_2, expert_v_2,
):
    x = first_block(
        x, w_sb_in, w_sb_out, w_ret_in, w_ret_out, g_mix, g_mlp, w_mlp_up, w_mlp_down, g_final,
    )
    return second_block(
        x, meta_tokens_2, norm_mix_2, w_in_2, conv_w_2, a_log_2, dt_bias_2, o_norm_a_2,
        q_norm_b_2, k_norm_b_2, f_bias_2, w_branch_2, w_out_2, norm_ffn_2, peer_wq_2,
        peer_sub_keys_2, expert_u_2, expert_v_2,
    )


_drawn_inputs = setup_inputs


def setup_inputs(seed=0):
    import zlib

    import numpy as np

    out = dict(_drawn_inputs(seed))
    spreads = {}
    factors = {'norm_mix_2': 4.606,
     'o_norm_a_2': 8.0,
     'q_norm_b_2': 8.0,
     'k_norm_b_2': 8.0,
     'f_bias_2': 4.861,
     'norm_ffn_2': 8.0,
     'peer_wq_2': 4.04,
     'peer_sub_keys_2': 3.98,
     'expert_u_2': 4.446,
     'expert_v_2': 4.003}
    for name, (base, spread) in spreads.items():
        noise = np.random.default_rng([zlib.crc32(name.encode()), seed]).standard_normal(out[name].shape)
        drawn = base * np.exp(spread * noise) if base else spread * noise
        out[name] = jnp.asarray(drawn.astype(out[name].dtype))
    for name, factor in factors.items():
        out[name] = (out[name] * factor).astype(out[name].dtype)
    return out
```

```python
from contextlib import ExitStack, contextmanager

import numpy as np

import concourse.bass as bass
from concourse import mybir

F32 = mybir.dt.float32
I32 = mybir.dt.int32
U32 = mybir.dt.uint32
ALU = mybir.AluOpType
ACT = mybir.ActivationFunctionType
AX = mybir.AxisListType.X
ENG = mybir.EngineType

P = 128
D = 1024
KD = D // P
S = 256
NT = S // P
META = 16
SM = META + S
HID = 4096
SB_H, SB_D = 16, 64
RET_H, RET_QK, RET_V = 4, 256, 512
H2, DH = 8, 128
CONV_K = 4
CONV_CH = 3 * H2 * DH
KEYS, TOPK, PEER_H = 128, 16, 8
EPS = 1e-6
BANK = 512
BLK = 2048
RING = 4
NEG = -1.0e30
COLS_W = BLK // KD
ROWS_K = BLK // BANK
TILES = [(0, META), (META, P), (META + P, P)]


FIRST_BLOCK = {"c_sb_keep", "c_sb_cap", "c_cos", "c_sin", "c_decay", "c_g_final"}
PEER_ONLY = {"c_g_peer", "c_keys"}


def cols_blocks(w):
    k, n = w.shape
    return w.reshape(KD, P, n // COLS_W, COLS_W).transpose(2, 1, 0, 3).reshape(-1, P, BLK)


def rows_blocks(w):
    k, n = w.shape
    w = w.reshape(k // (ROWS_K * P), ROWS_K, P, n // BANK, BANK)
    return w.transpose(3, 0, 2, 1, 4).reshape(-1, P, BLK)


def per_partition(v):
    return v.reshape(-1, P).T


def weight_stream(a):
    w_in = a["w_in_2"][0]
    at = np.cumsum([0, CONV_CH, D, H2, H2, CONV_CH, H2, 2 * D])
    sb, ret = a["w_sb_in"][0], a["w_ret_in"][0]
    parts = [
        cols_blocks(sb[:, :2 * D]), rows_blocks(sb[:, 2 * D:]), rows_blocks(a["w_sb_out"][0]),
        cols_blocks(a["w_mlp_up"][0]), rows_blocks(a["w_mlp_down"][0]),
        cols_blocks(ret[:, :2 * D]), rows_blocks(ret[:, 2 * D:]), rows_blocks(a["w_ret_out"][0]),
        cols_blocks(a["w_mlp_up"][1]), rows_blocks(a["w_mlp_down"][1]),
        cols_blocks(w_in[:, at[0]:at[1]]), cols_blocks(w_in[:, at[1]:at[2]]),
        cols_blocks(w_in[:, at[4]:at[5]]), cols_blocks(w_in[:, at[6]:at[7]]),
        cols_blocks(a["w_branch_2"][0, 0]), cols_blocks(a["w_branch_2"][0, 1]),
        rows_blocks(a["w_out_2"][0]), cols_blocks(a["peer_wq_2"][0]),
    ]
    small = np.concatenate([w_in[:, at[2]:at[4]], w_in[:, at[5]:at[6]]], axis=1)
    small = small.reshape(KD, P, 3 * H2).transpose(1, 0, 2).reshape(P, -1)
    return np.concatenate(parts), small


def shape_constants():
    p, f = np.arange(P)[:, None], np.arange(P)[None, :]
    c = {}
    c["ident"] = (p == f)
    c["ones"] = np.ones((P, P))
    c["from_here"] = (p >= f)
    before = (p < f)
    c["sb_keep"] = np.concatenate([before, np.ones((P, P)), before], 1)
    c["sb_cap"] = np.where(c["sb_keep"] > 0, 0.0, NEG)
    inv = (1.0 / (np.float32(10000.0) ** np.linspace(0, 1, P, dtype=np.float32))).astype(np.float32)
    ang = (np.arange(S, dtype=np.float32)[None, :] * inv[:, None]).astype(np.float32)
    c["cos"], c["sin"] = np.cos(ang), np.sin(ang)
    lg = np.log1p(-np.exp2(-5.0 - np.arange(RET_H)))
    rel = np.concatenate([f - p, f + P - p, f - p], 1).astype(np.float64)
    c["decay"] = np.concatenate([np.where(rel >= 0, np.exp(g * np.maximum(rel, 0)), 0) for g in lg], 1)
    c["earlier"] = (p < f)
    c["not_later"] = (p <= f)
    c["merge"] = np.concatenate([((p >> l) == (f >> l) + 1) & ((p >> l) % 2 == 1)
                                 for l in range(7)], 1)
    c["causal"] = np.concatenate([np.zeros((P, SM - P)), np.where(f <= p, 0.0, NEG)], 1)
    head = np.zeros((P, H2 * P))
    for h in range(H2):
        head[h, h * P:(h + 1) * P] = 1.0
    c["pick"] = head
    c["iota"] = np.broadcast_to(np.arange(TOPK), (P, TOPK))
    return {k: np.ascontiguousarray(v, dtype=np.float32) for k, v in c.items()}


def vectors(a):
    conv = a["conv_w_2"][0].reshape(CONV_K, CONV_CH // P, P).transpose(2, 1, 0).reshape(P, -1)
    v = {
        "g_mix0": per_partition(a["g_mix"][0]), "g_mix1": per_partition(a["g_mix"][1]),
        "g_mlp0": per_partition(a["g_mlp"][0]), "g_mlp1": per_partition(a["g_mlp"][1]),
        "g_mixer": per_partition(a["norm_mix_2"][0]), "conv": conv,
        "o_norm": a["o_norm_a_2"][0][:, None], "q_norm": a["q_norm_b_2"][0][:, None],
        "k_norm": a["k_norm_b_2"][0][:, None],
    }
    for n in ("a_log", "dt_bias", "f_bias"):
        v[n] = a[n + "_2"][0][:, None]
    rows = {"g_final": a["g_final"], "g_peer": a["norm_ffn_2"][0]}
    v.update({k: np.broadcast_to(x, (P, D)) for k, x in rows.items()})
    v["keys"] = a["peer_sub_keys_2"][0].transpose(3, 1, 0, 2).reshape(P, -1)
    return {k: np.ascontiguousarray(x) for k, x in v.items()}


class Mark:

    def __init__(self, counter, value, loop=None):
        self.counter, self.value, self.loop = counter, value, loop

    def at(self):
        if self.loop is None:
            return self.value
        i, per = self.loop
        return i * per[self.counter] + self.value

    def back(self, turns=1):
        value = self.value - turns * self.loop[1][self.counter]
        assert value >= 1, "a wait needs a positive value"
        return Mark(self.counter, value, self.loop)


class Counter:

    def __init__(self, sem, step=1):
        self.sem, self.step, self.value, self.loop = sem, step, 0, None

    def mark(self, ins):
        ins.then_inc(self.sem, self.step)
        self.value += self.step
        return Mark(self, self.value, self.loop)

    def now(self):
        return Mark(self, self.value, self.loop)


@contextmanager
def loop(nc, turns, engines, per):
    entry = {c: c.value for c in per}
    with nc.Fori(0, turns, engines=engines) as i:
        for c in per:
            c.loop = (i, per)
        yield i
        for c in per:
            assert c.value - entry[c] == per[c], (c.sem, c.value - entry[c], per[c])
    for c in per:
        c.value, c.loop = entry[c] + turns * per[c], None


def wait(engine, *marks):
    best = {}
    for m in marks:
        if m is None:
            continue
        o = best.get(m.counter)
        if o is None or o.loop is not m.loop and m.loop is not None or o.loop is m.loop and m.value > o.value:
            best[m.counter] = m
    for m in best.values():
        if m.loop is not None or m.value > 0:
            engine.wait_ge(m.counter.sem, m.at())


class Program:
    def __init__(self, nc, ins, out, stop=None):
        self.nc, self.ins, self.out, self.stop = nc, ins, out, stop
        self.pe, self.dve, self.act, self.pool, self.sp = nc.tensor, nc.vector, nc.scalar, nc.gpsimd, nc.sync
        self.c_pe = Counter(nc.alloc_semaphore("tensor_done"))
        self.c_dve = Counter(nc.alloc_semaphore("vector_done"))
        self.c_act = Counter(nc.alloc_semaphore("scalar_done"))
        self.c_pool = Counter(nc.alloc_semaphore("gpsimd_done"))
        self.blocks = Counter(nc.alloc_semaphore("blocks_read"))
        self.block_full = [nc.alloc_semaphore(f"block_full{s}") for s in range(RING)]
        self.n_block = 0
        self.first_block = ExitStack()

    def sb(self, name, shape, dt=F32):
        return self.nc.alloc_sbuf_tensor(name, shape, dt)

    def V(self, ins): return self.c_dve.mark(ins)
    def A(self, ins): return self.c_act.mark(ins)
    def G(self, ins): return self.c_pool.mark(ins)
    def T(self, ins): return self.c_pe.mark(ins)

    def meet(self):
        all_marks = [c.now() for c in (self.c_pe, self.c_dve, self.c_act, self.c_pool, self.blocks)]
        for e in (self.pe, self.dve, self.act, self.pool):
            wait(e, *all_marks)

    def bank(self, b, width=BANK, count=1):
        return self.psum[:, b * BANK:b * BANK + width]

    def dense_cols(self, n_blocks, x, width, evac, steps=1):
        nc, pe = self.nc, self.pe
        wait(pe, self.c_dve.now(), self.c_act.now())
        assert self.n_block % RING == 0 and n_blocks % RING == 0
        first = self.n_block // RING
        def turn(i, full_at, earlier):
            for s in range(RING):
                pe.wait_ge(self.block_full[s], full_at)
                w = self.ring[s][:, :].rearrange("p (k n) -> p k n", k=KD)
                for sub in range(2):
                    q = 2 * s + sub
                    wait(pe, earlier[q])
                    for k in range(KD):
                        mm = pe.matmul(self.bank(q, width), w[:, k, sub * P:(sub + 1) * P], x[:, k, 0:width],
                                       start=(k == 0), stop=(k == KD - 1))
                read = self.blocks.mark(mm)
                for sub in range(2):
                    q = 2 * s + sub
                    eng, mark = (self.dve, self.V) if sub == 0 else (self.act, self.A)
                    wait(eng, read)
                    mark(evac(eng, i, q, self.bank(q, width)))

        per = {self.blocks: RING, self.c_dve: RING * steps, self.c_act: RING * steps}
        with loop(nc, n_blocks // RING, [ENG.PE, ENG.DVE, ENG.Activation], per) as i:
            base_v, base_a = self.c_dve.value, self.c_act.value
            earlier = []
            for q in range(8):
                c, b = (self.c_dve, base_v) if q % 2 == 0 else (self.c_act, base_a)
                earlier.append(Mark(c, b + (q // 2 + 1 - RING) * steps, c.loop))
            turn(i, i * 16 + (first + 1) * 16, earlier)
        self.n_block += n_blocks

    def dense_rows(self, n_k, halves, x, evac):
        nc, pe = self.nc, self.pe
        per_half = n_k // ROWS_K
        unroll = max(1, RING // per_half)
        wait(pe, self.c_dve.now(), self.c_act.now())
        assert self.n_block % RING == 0 and (per_half * unroll) % RING == 0 and halves % unroll == 0
        first = self.n_block // RING
        n_dve = unroll * NT
        turns = halves // unroll
        per = {self.blocks: per_half * unroll, self.c_dve: n_dve}
        slots_turn = per_half * unroll // RING
        with loop(nc, turns, [ENG.PE, ENG.DVE], per) as i:
            base = self.c_dve.value
            for u in range(unroll):
                for kb in range(per_half):
                    b = u * per_half + kb
                    s = b % RING
                    pe.wait_ge(self.block_full[s], i * (16 * slots_turn) + 16 * (first + b // RING + 1))
                    w = self.ring[s][:, :].rearrange("p (k n) -> p k n", k=ROWS_K)
                    for t in range(NT):
                        if kb == 0:
                            wait(pe, Mark(self.c_dve, base + u * NT + t + 1 - n_dve, self.c_dve.loop))
                        for k in range(ROWS_K):
                            kk = kb * ROWS_K + k
                            mm = pe.matmul(self.bank(u * NT + t), x[:, kk, t * P:(t + 1) * P], w[:, k, :],
                                           start=(kk == 0), stop=(kk == n_k - 1))
                    read = self.blocks.mark(mm)
                wait(self.dve, read)
                for t in range(NT):
                    self.V(evac(i, u, t, self.bank(u * NT + t)))
        self.n_block += per_half * halves

    def rms_scale(self, tiles, width, rstd, junk):
        r = self.stat
        for j, (ap, n) in enumerate(tiles):
            sq = self.A(self.act.activation(junk[0:n, 0:width], ap, ACT.Square, accum_out=r[0:n, j:j + 1]))
            wait(self.act, sq)
        for j, (ap, n) in enumerate(tiles):
            wait(self.dve, sq)
            m = self.V(self.dve.tensor_scalar(r[0:n, 4 + j:5 + j], r[0:n, j:j + 1], 1.0 / width, EPS, ALU.mult, ALU.add))
            wait(self.act, m)
            m = self.A(self.act.activation(r[0:n, 8 + j:9 + j], r[0:n, 4 + j:5 + j], ACT.Sqrt))
            wait(self.dve, m)
            m = self.V(self.dve.reciprocal(rstd[0:n, j:j + 1], r[0:n, 8 + j:9 + j]))
        return m

    def norm_cols(self, tiles, gain, out):
        self.meet()
        ready = self.rms_scale([(ap, n) for ap, n, _ in tiles], D, self.rstd, self.junk)
        wait(self.dve, ready)
        for j, (ap, n, _) in enumerate(tiles):
            ready = self.V(self.dve.tensor_scalar(self.hn[0:n, j, :], ap, self.rstd[0:n, j:j + 1], None, ALU.mult))
        wait(self.pe, ready)
        self.turn_cols(tiles, [self.hn[0:n, j, :] for j, (_, n, _) in enumerate(tiles)], KD, out,
                       lambda k: gain[:, k:k + 1])

    def turn_cols(self, tiles, rows, pieces, out, gain=None):
        width = max(c + n for _, n, c in tiles)
        moved = {}
        for k in range(pieces):
            wait(self.pe, moved.get(k - 8))
            for (_, n, c), r in zip(tiles, rows):
                tr = self.pe.transpose(self.bank(k % 8)[:, c:c + n], r[:, k * P:(k + 1) * P], self.C["ident"][0:n, 0:n])
            tr = self.T(tr)
            src, dst = self.bank(k % 8, width), out[:, k, 0:width]
            if k % 2 == 0:
                wait(self.dve, tr)
                moved[k] = self.V(self.dve.tensor_scalar(dst, src, gain(k), None, ALU.mult) if gain
                                  else self.dve.tensor_copy(dst, src))
            else:
                wait(self.act, tr)
                moved[k] = self.A(self.act.activation(dst, src, ACT.Copy, scale=gain(k)) if gain
                                  else self.act.activation(dst, src, ACT.Copy))
        wait(self.pe, self.c_dve.now(), self.c_act.now())

    def setup(self):
        nc = self.nc
        self.ring = [self.sb(f"weights{s}", [P, BLK]) for s in range(RING)]
        self.psum = nc.alloc_psum_tensor("banks", [P, 8 * BANK], F32)
        self.h = self.sb("h", [P, NT, D])
        self.hn = self.sb("hn", [P, 3, D])
        self.xT = self.sb("xT", [P, KD, SM])
        self.junk = self.sb("junk", [P, D])
        self.stat = self.sb("stat", [P, 16])
        self.rstd = self.sb("rstd", [P, 4])
        self.meta = self.sb("meta_rows", [META, D])
        self.ret_stat = self.sb("ret_stat", [P, NT * RET_H, 12])
        self.C = {}
        self.c_load = Counter(nc.alloc_semaphore("constants_landed"), 16)
        self.x_in = Counter(nc.alloc_semaphore("x_landed"), 16)
        self.x_in.mark(self.sp.dma_start(self.h[:, :, :], self.ins["x"].rearrange("o (t p) d -> p (o t) d", p=P)))
        self.x_in.mark(self.sp.dma_start(self.meta[:, :], self.ins["meta"]))
        names = [n for n in self.ins if n.startswith("c_") and n not in PEER_ONLY]
        for name in sorted(names, key=lambda n: n in FIRST_BLOCK):
            shape = list(self.ins[name].shape)
            if name in FIRST_BLOCK:
                t = self.first_block.enter_context(nc.sbuf_tensor("s" + name, shape, F32))
            else:
                t = self.sb("s" + name, shape)
            self.C[name[2:]] = t
            self.c_load.mark(self.act.dma_start(t[:, :], self.ins[name]))
        w = self.ins["weights"]
        n = {1: 16, 2: 48, 3: 80, 4: 112, 5: 112, 6: 160}.get(self.stop, w.shape[0])
        for s in range(RING):
            self.sp.dma_start(self.ring[s][:, :], w[s]).then_inc(self.block_full[s], 16)
        with nc.Fori(1, n // RING, engines=[ENG.SP]) as i:
            for s in range(RING):
                self.sp.wait_ge(self.blocks.sem, i * RING + (s + 1 - RING))
                self.sp.dma_start(self.ring[s][:, :], w[bass.ds(i * RING + s, 1), :, :].rearrange("o p n -> p (o n)"))\
                    .then_inc(self.block_full[s], 16)
        for k in range(8):
            self.V(self.dve.memset(self.stat[:, k:k + 1], 0.0))
        for e in (self.pe, self.dve, self.act, self.pool):
            wait(e, self.c_load.now(), self.x_in.now())
        for k in range(8):
            self.A(self.act.activation(self.stat[:, 8 + k:9 + k], self.C["ident"][:, 0:1], ACT.Copy))
        self.G(self.pool.memset(self.junk[:, 0:1], 0.0))

    def h_tiles(self):
        return [(self.h[:, t, :], P, t * P) for t in range(NT)]

    def add_to_h(self, i, u, t, ps, turn_halves):
        at = bass.ds((i * turn_halves + u) * BANK, BANK)
        return self.dve.tensor_tensor(self.h[:, t, at], self.h[:, t, at], ps, ALU.add)

    def stick_breaking(self):
        nc, pe, dve, act, pool = self.nc, self.pe, self.dve, self.act, self.pool
        self.norm_cols(self.h_tiles(), self.C["g_mix0"], self.xT)
        with nc.sbuf_tensor("sb_qk", [P, 16, S], F32) as qk, nc.sbuf_tensor("sb_v", [P, NT, D], F32) as v, \
                nc.sbuf_tensor("sb_oT", [P, KD, S], F32) as oT, \
                nc.sbuf_tensor("sb_e", [P, 2, 2, 384], F32) as e, nc.sbuf_tensor("sb_sp", [P, 2, 2, 384], F32) as sp, \
                nc.sbuf_tensor("sb_a", [P, 2, 2, 384], F32) as a, \
                nc.sbuf_tensor("sb_z", [P, 2, 2, 384], F32) as zs:

            def put_qk(eng, i, q, ps):
                dst = qk[:, bass.ds(i * 8 + q, 1), :].rearrange("p o n -> p (o n)")
                return eng.tensor_copy(dst, ps) if eng is dve else act.activation(dst, ps, ACT.Copy)

            self.dense_cols(8, self.xT, S, put_qk)
            self.dense_rows(KD, 2, self.xT, lambda i, u, t, ps: dve.tensor_copy(v[:, t, u * BANK:(u + 1) * BANK], ps))
            self.meet()
            self.V(dve.tensor_scalar(qk[:, 0:8, :], qk[:, 0:8, :], SB_D ** -0.5, None, ALU.mult))
            wait(pe, self.c_dve.now())

            def banks(first, n=384):
                return self.psum[:, first * BANK:(first + 2) * BANK].rearrange("p (b n) -> p b n", b=2)[:, :, 0:n]

            NP_ = SB_H // 2
            z_done, m = {}, {}

            def logits(c):
                wait(pe, m.get(("copy", c - 2)))
                for j in range(2):
                    r = slice(64 * j, 64 * j + 64)
                    z = self.bank(2 * (c % 2) + j)
                    pe.matmul(z[:, 0:S], qk[r, 8 + c, 0:P], qk[r, c, 0:S], start=True, stop=True)
                    mm = pe.matmul(z[:, S:384], qk[r, 8 + c, P:S], qk[r, c, P:S], start=True, stop=True)
                m["z", c] = self.T(mm)

            def softplus(c):
                b = c % 2
                z = zs[:, b]
                wait(act, m["z", c], m.get(("d", c - 2)))
                m["copy", c] = self.A(act.activation(z, banks(2 * b), ACT.Copy))
                wait(dve, m["copy", c])
                m["abs", c] = self.V(dve.scalar_tensor_tensor(e[:, b], z, -1.0, z, ALU.mult, ALU.min))
                wait(act, m["abs", c])
                x = self.A(act.activation(e[:, b], e[:, b], ACT.Exp))
                wait(act, x)
                m["ln", c] = self.A(act.activation(e[:, b], e[:, b], ACT.Ln, bias=1.0))
                wait(dve, m.get(("cum", c - 2)))
                wait(dve, m["ln", c])
                m["sp", c] = self.V(dve.scalar_tensor_tensor(sp[:, b], z, 0.0, e[:, b], ALU.max, ALU.add))
                wait(pool, m["sp", c])
                keep = self.C["sb_keep"][:, None, :].to_broadcast([P, 2, 384])
                m["keep", c] = self.G(pool.tensor_tensor(sp[:, b], sp[:, b], keep, ALU.mult))

            def cumulate(c):
                b = c % 2
                wait(pe, m["keep", c], m.get(("oT", c - 2)))
                for j in range(2):
                    L = self.bank(4 + 2 * b + j)
                    pe.matmul(L[:, 0:S], self.C["from_here"][:, :], sp[:, b, j, 0:S], start=True, stop=False)
                    pe.matmul(L[:, P:S], self.C["ones"][:, :], sp[:, b, j, S:384], start=False, stop=True)
                    mm = pe.matmul(L[:, S:384], self.C["from_here"][:, :], sp[:, b, j, S:384], start=True, stop=True)
                m["cum", c] = self.T(mm)

            def weights(c):
                z, L, b = zs[:, c % 2], banks(4 + 2 * (c % 2)), c % 2
                wait(dve, m["cum", c], m.get(("av", c - 2)))
                m["d", c] = self.V(dve.tensor_tensor(a[:, b], z, L, ALU.subtract))
                wait(pool, m["d", c])
                cap = self.C["sb_cap"][:, None, :].to_broadcast([P, 2, 384])
                m["min", c] = self.G(pool.tensor_tensor(a[:, b], a[:, b], cap, ALU.add))
                wait(act, m["min", c])
                m["a", c] = self.A(act.activation(a[:, b], a[:, b], ACT.Exp))

            def values(c):
                b = c % 2
                wait(pe, m["a", c])
                for j in range(2):
                    o = self.psum[64 * j:64 * j + 64, (4 + 2 * b) * BANK:(4 + 2 * b) * BANK + S]
                    f = slice((2 * c + j) * SB_D, (2 * c + j + 1) * SB_D)
                    pe.matmul(o[:, 0:S], v[:, 0, f], a[:, b, j, 0:S], start=True, stop=False)
                    mm = pe.matmul(o[:, P:S], v[:, 1, f], a[:, b, j, S:384], start=False, stop=True)
                m["av", c] = self.T(mm)
                wait(dve, m["av", c])
                m["oT", c] = self.V(dve.tensor_copy(oT[:, c, :], self.bank(4 + 2 * b, S)))

            for c in range(NP_ + 2):
                if c < NP_:
                    logits(c)
                    softplus(c)
                if 1 <= c <= NP_:
                    cumulate(c - 1)
                    weights(c - 1)
                if c >= 2:
                    values(c - 2)
            self.meet()
            self.dense_rows(KD, 2, oT, lambda i, u, t, ps: self.add_to_h(i, u, t, ps, 2))

    def mlp(self, gain, name):
        nc, dve, act = self.nc, self.dve, self.act
        self.norm_cols(self.h_tiles(), gain, self.xT)
        with nc.sbuf_tensor("uT" + name, [P, HID // P, S], F32) as uT, \
                nc.sbuf_tensor("relu" + name, [P, 8, S], F32) as relu:
            def square(eng, i, q, ps):
                dst = uT[:, bass.ds(i * 8 + q, 1), :].rearrange("p o n -> p (o n)")
                if eng is dve:
                    wait(dve, self.V(dve.tensor_scalar(relu[:, q, :], ps, 0.0, None, ALU.max)))
                    return dve.tensor_tensor(dst, relu[:, q, :], relu[:, q, :], ALU.mult)
                wait(act, self.A(act.activation(relu[:, q, :], ps, ACT.Relu)))
                return act.activation(dst, relu[:, q, :], ACT.Square)

            self.dense_cols(16, self.xT, S, square, steps=2)
            self.meet()
            self.dense_rows(HID // P, 2, uT, lambda i, u, t, ps: self.add_to_h(i, u, t, ps, 1))

    def retention(self):
        nc, pe, dve, act, pool = self.nc, self.pe, self.dve, self.act, self.pool
        self.norm_cols(self.h_tiles(), self.C["g_mix1"], self.xT)
        with nc.sbuf_tensor("ret_qk", [P, 16, S], F32) as qk, nc.sbuf_tensor("ret_rot", [P, 16, S], F32) as rot, \
                nc.sbuf_tensor("ret_tmp", [P, 8, S], F32) as tmp, nc.sbuf_tensor("ret_v", [P, NT, 2 * D], F32) as v, \
                nc.sbuf_tensor("ret_g", [P, NT, 2 * D], F32) as g:

            def put_qk(eng, i, q, ps):
                dst = qk[:, bass.ds(i * 8 + q, 1), :].rearrange("p o n -> p (o n)")
                return eng.tensor_copy(dst, ps) if eng is dve else act.activation(dst, ps, ACT.Copy)

            self.dense_cols(8, self.xT, S, put_qk)
            self.dense_rows(KD, 4, self.xT, lambda i, u, t, ps: dve.tensor_copy(v[:, t, bass.ds((i * 2 + u) * BANK, BANK)], ps))
            self.dense_rows(KD, 4, self.xT, lambda i, u, t, ps: dve.tensor_copy(g[:, t, bass.ds((i * 2 + u) * BANK, BANK)], ps))
            self.meet()
            for t in range(NT):
                self.A(act.activation(g[:, t, :], g[:, t, :], ACT.Silu))
            ready = []
            for e, mark, o in ((dve, self.V, 0), (pool, self.G, 8)):
                x = qk[:, o:o + 8, :].rearrange("p (h two) s -> p two h s", two=2)
                r = rot[:, o:o + 8, :].rearrange("p (h two) s -> p two h s", two=2)
                w = tmp[:, o // 2:o // 2 + 4, :]
                cos, sin = (self.C[n][:, None, :].to_broadcast([P, 4, S]) for n in ("cos", "sin"))
                for half, op in ((0, ALU.subtract), (1, ALU.add)):
                    a = mark(e.tensor_tensor(r[:, half], x[:, half], cos, ALU.mult))
                    b = mark(e.tensor_tensor(w, x[:, 1 - half], sin, ALU.mult))
                    wait(e, b)
                    a = mark(e.tensor_tensor(r[:, half], r[:, half], w, op))
                    wait(e, a)
                if o:
                    a = mark(e.tensor_scalar(rot[:, 8:16, :], rot[:, 8:16, :], RET_QK ** -0.5, None, ALU.mult))
                ready.append(a)
            wait(pe, *ready)
            sc = qk[:, :, :].rearrange("p a b -> p (a b)")
            decay = self.C["decay"][:, :].rearrange("p (h n) -> p h n", h=RET_H)
            m = {}
            for hd in range(RET_H):
                b = self.bank(hd % 2)
                wait(pe, m.get(("sc", hd - 2)))
                for key, (q0, o) in enumerate(((0, 0), (P, S))):
                    for k in range(2):
                        mm = pe.matmul(b[:, o:o + S - q0], rot[:, 8 + 2 * hd + k, key * P:key * P + P],
                                       rot[:, 2 * hd + k, q0:S], start=(k == 0), stop=(k == 1))
                m["s", hd] = self.T(mm)
                wait(dve, m["s", hd])
                s_h = sc[:, hd * 384:hd * 384 + 384]
                m["sc", hd] = self.V(dve.tensor_tensor(s_h, b[:, 0:384], decay[:, hd], ALU.mult))
                wait(pe, m["sc", hd])
                for t in range(NT):
                    n = NT * hd + t
                    o = self.bank(2 + n % 6)
                    wait(pe, m.get(("o", n - 6)))
                    vh = slice(hd * RET_V, (hd + 1) * RET_V)
                    mm = pe.matmul(o, s_h[:, t * P:t * P + P], v[:, 0, vh], start=True, stop=(t == 0))
                    if t:
                        mm = pe.matmul(o, s_h[:, S:384], v[:, 1, vh], start=False, stop=True)
                    m["m", n] = self.T(mm)
                    wait(dve, m["m", n])
                    st = self.ret_stat[:, n, :]
                    wait(dve, self.V(dve.bn_stats(st[:, 0:6], o)))
                    wait(dve, self.V(dve.bn_aggr(st[:, 6:8], st[:, 0:6])))
                    wait(dve, self.V(dve.tensor_scalar(st[:, 8:9], st[:, 7:8], EPS, None, ALU.add)))
                    wait(act, self.c_dve.now())
                    wait(dve, self.A(act.activation(st[:, 9:10], st[:, 8:9], ACT.Sqrt)))
                    wait(dve, self.V(dve.reciprocal(st[:, 10:11], st[:, 9:10])))
                    nrm = self.hn[:, n % 2, 0:RET_V]
                    wait(dve, self.V(dve.tensor_scalar(nrm, o, st[:, 6:7], st[:, 10:11], ALU.subtract, ALU.mult)))
                    m["o", n] = self.V(dve.tensor_tensor(g[:, t, vh], nrm, g[:, t, vh], ALU.mult))
            self.meet()
            self.turn_cols(self.h_tiles(), [g[:, t, :] for t in range(NT)], 2 * KD, rot)
            self.meet()
            self.dense_rows(2 * KD, 2, rot, lambda i, u, t, ps: self.add_to_h(i, u, t, ps, 1))

    def final_norm(self):
        dve = self.dve
        self.meet()
        wait(dve, self.rms_scale([(ap, n) for ap, n, _ in self.h_tiles()], D, self.rstd, self.junk))
        for t in range(NT):
            self.V(dve.scalar_tensor_tensor(self.h[:, t, :], self.h[:, t, :], self.rstd[:, t:t + 1],
                                            self.C["g_final"][:, :], ALU.mult, ALU.mult))
        self.meet()
        self.first_block.close()

    def small_rows(self):
        nc, pe, dve, act = self.nc, self.pe, self.dve, self.act
        small = self.C["small"][:, :].rearrange("p (k n) -> p k n", k=KD)
        for g in range(3):
            for k in range(KD):
                mm = pe.matmul(self.bank(g, SM)[0:H2, :], small[:, k, g * H2:(g + 1) * H2], self.xT[:, k, :],
                               start=(k == 0), stop=(k == KD - 1))
        done = self.T(mm)
        b, a, f = (self.bank(g, SM)[0:H2, :] for g in range(3))
        R = {n: self.lam[:, j, :] for j, n in enumerate(
            ("beta", "G", "nbe", "tail", "eG", "ncum", "y", "t", "u", "g"))}
        C = self.C

        def v(ins):
            wait(dve, self.V(ins))

        def soft(x):
            v(dve.scalar_tensor_tensor(R["t"], x, -1.0, x, ALU.mult, ALU.min))
            wait(act, self.c_dve.now())
            wait(act, self.A(act.activation(R["t"], R["t"], ACT.Exp)))
            wait(dve, self.A(act.activation(R["t"], R["t"], ACT.Ln, bias=1.0)))

        wait(act, done)
        wait(dve, done)
        wait(dve, self.A(act.activation(R["u"], b, ACT.Exp, scale=-1.0)))
        v(dve.tensor_scalar(R["u"], R["u"], 1.0, None, ALU.add))
        v(dve.reciprocal(R["beta"], R["u"]))
        ea = self.stat[0:H2, 0:1]
        self.A(act.activation(ea, C["a_log"][:, :], ACT.Exp))
        v(dve.tensor_scalar(R["y"], a, C["dt_bias"][:, 0:1], None, ALU.add))
        soft(R["y"])
        v(dve.scalar_tensor_tensor(R["t"], R["y"], 0.0, R["t"], ALU.max, ALU.add))
        v(dve.tensor_scalar(R["g"], R["t"], ea, -1.0, ALU.mult, ALU.mult))
        ones = C["ones"][0:H2, :]
        for c, n in TILES:
            v(dve.tensor_tensor_scan(R["G"][:, c:c + n], ones[:, 0:n], R["g"][:, c:c + n], 0.0, ALU.mult, ALU.add))
        wait(act, self.c_dve.now())
        self.A(act.activation(R["eG"], R["G"], ACT.Exp))
        for c, n in TILES:
            self.A(act.activation(R["tail"][:, c:c + n], R["G"][:, c:c + n], ACT.Exp, scale=-1.0,
                                  bias=R["G"][:, c + n - 1:c + n]))
        wait(dve, self.c_act.now())
        v(dve.scalar_tensor_tensor(R["nbe"], R["beta"], -1.0, R["eG"], ALU.mult, ALU.mult))
        v(dve.tensor_scalar(R["y"], f, C["f_bias"][:, 0:1], None, ALU.add))
        soft(R["y"])
        v(dve.tensor_scalar(R["y"], R["y"], -1.0, 0.0, ALU.mult, ALU.max))
        v(dve.tensor_tensor(R["t"], R["t"], R["y"], ALU.add))
        v(dve.memset(R["u"], 1.0))
        v(dve.tensor_tensor_scan(R["ncum"], R["u"], R["t"], 0.0, ALU.mult, ALU.add))
        ps = self.bank(3)
        wait(pe, self.c_dve.now(), self.c_act.now())
        for t, (c, n) in enumerate(TILES):
            for j in range(4):
                o = (4 * t + j) * H2
                tr = pe.transpose(ps[0:n, o:o + H2], self.lam[:, j, c:c + n], C["ident"][0:H2, 0:H2])
        wait(dve, self.T(tr))
        w = 4 * H2
        self.V(dve.tensor_copy(self.tok[0:META, 0:w], ps[0:META, 0:w]))
        v(dve.tensor_copy(self.tok[:, w:3 * w], ps[:, w:3 * w]))
        return R

    def token_scalar(self, t, j, h):
        o = (4 * t + j) * H2 + h
        return self.tok[0:TILES[t][1], o:o + 1]

    def feature_rms(self, x, width, pieces, total, eps, r, sq):
        pe, dve, act = self.pe, self.dve, self.act
        wait(act, self.c_dve.now())
        wait(pe, self.c_dve.now(), self.A(act.activation(sq, x, ACT.Square)))
        for k in range(pieces):
            mm = pe.matmul(self.bank(k, width), self.C["ones"][:, :], sq[:, k, :], start=True, stop=True)
        wait(dve, self.T(mm))
        banks = self.psum[:, :].rearrange("p (b n) -> p b n", b=8)[:, 0:pieces, 0:width]
        wait(act, self.V(dve.tensor_scalar(r, banks, 1.0 / total, eps, ALU.mult, ALU.add)))
        wait(dve, self.A(act.activation(r, r, ACT.Sqrt)))
        wait(dve, self.V(dve.reciprocal(r, r)))

    def mixer(self):
        with self.nc.sbuf_tensor("obT", [P, H2, S], F32) as self.obT, \
                self.nc.sbuf_tensor("oaT", [P, H2, S], F32) as self.oaT, \
                self.nc.sbuf_tensor("lam", [H2, 10, SM], F32) as self.lam:
            self.mixer_stages()

    def mixer_stages(self):
        nc, pe, dve, act, pool, C = self.nc, self.pe, self.dve, self.act, self.pool, self.C
        tiles = [(self.meta[:, :], META, 0)] + [(self.h[:, t, :], P, META + t * P) for t in range(NT)]
        self.norm_cols(tiles, C["g_mixer"], self.xT)
        xs = self.xT[:, :, META:SM]
        with nc.sbuf_tensor("tok", [P, 12 * H2], F32) as tok:
            self.tok = tok
            R = self.small_rows()
            with nc.sbuf_tensor("conv_in", [P, CONV_CH // P, CONV_K - 1 + SM], F32) as cin:
                pad = CONV_K - 1
                self.V(dve.memset(cin[:, :, 0:pad], 0.0))

                def put_conv(eng, i, q, ps):
                    dst = cin[:, bass.ds(i * 8 + q, 1), pad:pad + SM].rearrange("p o n -> p (o n)")
                    return eng.tensor_copy(dst, ps) if eng is dve else act.activation(dst, ps, ACT.Copy)

                self.dense_cols(CONV_CH // COLS_W, self.xT, SM, put_conv)
                for group in range(2):
                    self.meet()
                    self.delta_group(group, cin, R)
            self.meet()
            self.delta_gate(xs)
            self.meet()
            self.forgetting(R)
        self.meet()
        self.merge_branches(xs)

    def delta_group(self, group, cin, R):
        nc, pe, dve, act, pool, C = self.nc, self.pe, self.dve, self.act, self.pool, self.C
        HG = 4
        stack = ExitStack()

        def sb(name, shape):
            return stack.enter_context(nc.sbuf_tensor(f"{name}{group}", shape, F32))

        def four(ap, n=P):
            return ap.rearrange("p (h n) -> p h n", h=HG)[:, :, 0:n]

        y = sb("dy", [P, 3 * HG, SM])
        kb = sb("dkb", [P, HG, SM])
        qe = sb("dqe", [P, HG, S])
        last_decay = sb("dlast", [P, HG, 3])
        w = C["conv"][:, :].rearrange("p (c k) -> p c k", k=CONV_K)
        marks = {}
        for tap in range(CONV_K):
            for j in range(3 * HG):
                piece = (j // HG) * H2 + group * HG + j % HG
                x, wt = cin[:, piece, tap:tap + SM], w[:, piece, tap:tap + 1]
                if tap == 0:
                    marks[j] = self.V(dve.tensor_scalar(y[:, j, :], x, wt, None, ALU.mult))
                else:
                    wait(dve, marks[j])
                    marks[j] = self.V(dve.scalar_tensor_tensor(y[:, j, :], x, wt, y[:, j, :], ALU.mult, ALU.add))
        wait(act, self.c_dve.now())
        wait(dve, self.A(act.activation(y[:, :, :], y[:, :, :], ACT.Silu)))
        wait(act, self.c_act.now())
        with nc.sbuf_tensor(f"l2_{group}", [P, 2 * HG, SM], F32) as r:
            sq = self.hn[:, :, :].rearrange("p a b -> p (a b)")[:, 0:2 * HG * SM].rearrange("p (k n) -> p k n", k=2 * HG)
            self.feature_rms(y[:, 0:2 * HG, :], SM, 2 * HG, 1.0, EPS, r[:, :, :], sq)
            self.V(dve.scalar_tensor_tensor(y[:, 0:HG, :], y[:, 0:HG, :], DH ** -0.5, r[:, 0:HG, :], ALU.mult, ALU.mult))
            self.V(dve.tensor_tensor(y[:, HG:2 * HG, :], y[:, HG:2 * HG, :], r[:, HG:2 * HG, :], ALU.mult))
        self.meet()
        q, k, v = (y[:, HG * j:HG * (j + 1), :] for j in range(3))
        gam = sb("dgam", [P, HG, SM])
        for name, out in (("beta", kb), ("eG", qe), ("G", gam)):
            wait(pe, self.c_dve.now())
            for hh in range(HG):
                h = group * HG + hh
                mm = pe.matmul(self.bank(hh, SM), C["pick"][0:H2, h * P:(h + 1) * P], R[name], start=True, stop=True)
            wait(dve, self.T(mm))
            rows = self.psum[:, 0:HG * BANK].rearrange("p (b n) -> p b n", b=HG)
            if name == "beta":
                self.V(dve.tensor_tensor(kb[:, :, :], k, rows[:, :, 0:SM], ALU.mult))
            elif name == "eG":
                self.V(dve.tensor_tensor(qe[:, :, :], q[:, :, META:SM], rows[:, :, META:SM], ALU.mult))
                for t, (c, n) in enumerate(TILES):
                    self.V(dve.tensor_copy(last_decay[:, :, t:t + 1], rows[:, :, c + n - 1:c + n]))
            else:
                for t, (c, n) in enumerate(TILES):
                    for hh in range(HG):
                        g = self.V(dve.tensor_scalar(gam[0:n, hh, c:c + n], self.bank(hh)[0:n, c:c + n],
                                                     self.token_scalar(t, 1, group * HG + hh), 0.0, ALU.subtract, ALU.min))
                wait(act, g)
                for c, n in TILES:
                    self.A(act.activation(gam[0:n, :, c:c + n], gam[0:n, :, c:c + n], ACT.Exp))
        self.meet()
        A, AT, B, T, TT, M1 = (sb(n, [P, 2, HG * P]) for n in ("dA", "dAT", "dB", "dT", "dTT", "dM"))
        small = {n: sb(n + "m", [META, HG * META]) for n in ("dA", "dAT", "dB", "dT", "dTT", "dM")}
        attn = sb("dattn", [P, 2, HG * P])
        ktail, bv = sb("dkt", [P, 3, HG * P]), sb("dbv", [P, 3, HG * P])

        def of(x, name, t):
            n = TILES[t][1]
            return (small[name][:, :] if t == 0 else x[:, t - 1, :]).rearrange("p (h n) -> p h n", h=HG)

        for t, (c, n) in enumerate(TILES):
            tile = slice(c, c + n)
            kk, qk, kt, vt = (self.bank(b)[0:n, :] for b in range(4))
            wait(pe, self.c_dve.now(), self.c_act.now())
            for hh in range(HG):
                pe.matmul(kk[:, hh * n:(hh + 1) * n], k[:, hh, tile], kb[:, hh, tile], start=True, stop=True)
                if t:
                    pe.matmul(qk[:, hh * n:(hh + 1) * n], k[:, hh, tile], q[:, hh, tile], start=True, stop=True)
                pe.transpose(kt[:, hh * P:(hh + 1) * P], k[:, hh, tile], C["ident"][:, :])
                mm = pe.transpose(vt[:, hh * P:(hh + 1) * P], v[:, hh, tile], C["ident"][:, :])
            done = self.T(mm)
            wait(act, done)
            for hh in range(HG):
                h, f = group * HG + hh, slice(hh * P, (hh + 1) * P)
                self.A(act.activation(ktail[0:n, t, f], kt[:, f], ACT.Copy, scale=self.token_scalar(t, 3, h)))
                self.A(act.activation(bv[0:n, t, f], vt[:, f], ACT.Copy, scale=self.token_scalar(t, 0, h)))
            wait(dve, done)
            at = of(AT, "dAT", t)
            earlier = C["earlier"][0:n, None, 0:n].to_broadcast([n, HG, n])
            wait(dve, self.V(dve.tensor_tensor(at, kk[:, 0:HG * n].rearrange("p (h n) -> p h n", h=HG), gam[0:n, :, tile], ALU.mult)))
            wait(pe, self.V(dve.tensor_tensor(at, at, earlier, ALU.mult)))
            if t:
                x = attn[:, t - 1, :].rearrange("p (h n) -> p h n", h=HG)
                wait(dve, self.V(dve.tensor_tensor(x, qk[:, :].rearrange("p (h n) -> p h n", h=HG), gam[0:n, :, tile], ALU.mult)))
                self.V(dve.tensor_tensor(x, x, C["not_later"][:, None, :].to_broadcast([P, HG, P]), ALU.mult))
            back = self.bank(4 + t)[0:n, :]
            for hh in range(HG):
                mm = pe.transpose(back[:, hh * n:(hh + 1) * n], at[:, hh, :], C["ident"][0:n, 0:n])
            wait(act, self.T(mm))
            self.A(act.activation(of(A, "dA", t), back[:, 0:HG * n].rearrange("p (h n) -> p h n", h=HG), ACT.Copy))
            eye = C["ident"][0:n, None, 0:n].to_broadcast([n, HG, n])
            self.V(dve.tensor_copy(of(T, "dT", t), eye))
            self.V(dve.tensor_copy(of(TT, "dTT", t), eye))
        self.meet()
        levels = {0: 4, 1: 7, 2: 7}
        upd = {}
        for lvl in range(7):
            act_t = [t for t in range(3) if lvl < levels[t]]
            for t in act_t:
                n = TILES[t][1]
                m = C["merge"][0:n, None, lvl * P:lvl * P + n].to_broadcast([n, HG, n])
                wait(pool, upd.get(("M", t)))
                upd["B", t] = self.G(pool.tensor_tensor(of(B, "dB", t), of(A, "dA", t), m, ALU.mult))
            for t in act_t:
                n = TILES[t][1]
                b, tt = of(B, "dB", t), of(TT, "dTT", t)
                ps = self.bank([6, 0, 3][t])[0:n, :]
                wait(pe, upd["B", t], upd.get(("T", t)))
                for hh in range(HG):
                    mm = pe.matmul(ps[:, hh * n:(hh + 1) * n], b[:, hh, :], tt[:, hh, :], start=True, stop=True)
                upd["M", t] = self.T(mm)
                wait(act, upd["M", t])
                upd["M1", t] = self.A(act.activation(of(M1, "dM", t), ps[:, 0:HG * n].rearrange("p (h n) -> p h n", h=HG), ACT.Copy))
            for t in act_t:
                n = TILES[t][1]
                last = lvl == levels[t] - 1
                m1, tm, tt = of(M1, "dM", t), of(T, "dT", t), of(TT, "dTT", t)
                pz, pzt = self.bank([7, 1, 4][t])[0:n, :], self.bank([7, 2, 5][t])[0:n, :]
                if t == 0:
                    pzt = pzt[:, HG * META:]
                wait(pe, upd["M1", t])
                for hh in range(HG):
                    if not last:
                        pe.matmul(pz[:, hh * n:(hh + 1) * n], m1[:, hh, :], tm[:, hh, :], start=True, stop=True)
                    mm = pe.matmul(pzt[:, hh * n:(hh + 1) * n], tm[:, hh, :], m1[:, hh, :], start=True, stop=True)
                wait(dve, self.T(mm))
                if not last:
                    self.V(dve.tensor_tensor(tm, tm, pz[:, 0:HG * n].rearrange("p (h n) -> p h n", h=HG), ALU.subtract))
                upd["T", t] = self.V(dve.tensor_tensor(tt, tt, pzt[:, 0:HG * n].rearrange("p (h n) -> p h n", h=HG), ALU.subtract))
        self.meet()
        St, rhs, vn = sb("dS", [P, HG * P]), sb("drhs", [P, HG * P]), sb("dvn", [P, HG * P])
        H = [slice(hh * P, (hh + 1) * P) for hh in range(HG)]
        for t, (c, n) in enumerate(TILES):
            tile, tt = slice(c, c + n), of(TT, "dTT", t)
            right = bv[0:n, t, :]
            if t:
                ks = self.bank(0)
                for hh in range(HG):
                    mm = pe.matmul(ks[:, H[hh]], k[:, hh, tile], St[:, H[hh]], start=True, stop=True)
                wait(dve, self.T(mm))
                for hh in range(HG):
                    x = self.V(dve.scalar_tensor_tensor(rhs[:, H[hh]], ks[:, H[hh]], self.token_scalar(t, 2, group * HG + hh),
                                                        bv[:, t, H[hh]], ALU.mult, ALU.add))
                wait(pe, x)
                right = rhs[:, :]
            pv = self.bank(1)[0:n, :]
            for hh in range(HG):
                mm = pe.matmul(pv[:, H[hh]], tt[:, hh, :], right[:, H[hh]], start=True, stop=True)
            wait(act, self.T(mm))
            wait(pe, self.A(act.activation(vn[0:n, :], pv, ACT.Copy)))
            ps = self.bank(2)
            for hh in range(HG):
                mm = pe.matmul(ps[:, H[hh]], ktail[0:n, t, H[hh]], vn[0:n, H[hh]], start=True, stop=True)
            s_done = self.T(mm)
            if t:
                po, xc = self.bank(3), slice(c - META, c - META + n)
                for hh in range(HG):
                    pe.matmul(po[:, H[hh]], St[:, H[hh]], qe[:, hh, xc], start=True, stop=False)
                    mm = pe.matmul(po[:, H[hh]], vn[:, H[hh]], attn[:, t - 1, H[hh]], start=False, stop=True)
                o_done = self.T(mm)
                wait(dve, o_done)
                self.V(dve.tensor_copy(self.oaT[:, group * HG:(group + 1) * HG, xc], po[:, :].rearrange("p (h n) -> p h n", h=HG)))
                for hh in range(HG):
                    x = self.V(dve.scalar_tensor_tensor(St[:, H[hh]], St[:, H[hh]], last_decay[:, hh, t:t + 1],
                                                        ps[:, H[hh]], ALU.mult, ALU.add))
            else:
                wait(dve, s_done)
                x = self.V(dve.tensor_copy(St[:, :], ps))
            wait(pe, x)
        stack.close()

    def delta_gate(self, xs):
        nc, dve, act = self.nc, self.dve, self.act
        with nc.sbuf_tensor("zT", [P, H2, S], F32) as z, nc.sbuf_tensor("zr", [P, H2, S], F32) as r, \
                nc.sbuf_tensor("zs", [P, H2, S], F32) as sq:
            def put_z(eng, i, q, ps):
                dst = z[:, bass.ds(i * 8 + q, 1), :].rearrange("p o n -> p (o n)")
                return eng.tensor_copy(dst, ps) if eng is dve else act.activation(dst, ps, ACT.Copy)

            self.dense_cols(4, xs, S, put_z)
            self.meet()
            silu = self.A(act.activation(z[:, :, :], z[:, :, :], ACT.Silu))
            self.feature_rms(self.oaT[:, :, :], S, H2, DH, EPS, r[:, :, :], sq[:, :, :])
            oa = self.oaT[:, :, :].rearrange("p a b -> p (a b)")
            flat = [x[:, :, :].rearrange("p a b -> p (a b)") for x in (r, z)]
            wait(dve, self.V(dve.scalar_tensor_tensor(oa, oa, self.C["o_norm"][:, 0:1], flat[0], ALU.mult, ALU.mult)), silu)
            self.V(dve.tensor_tensor(oa, oa, flat[1], ALU.mult))
            self.meet()

    def forgetting(self, R):
        nc, pe, dve, act, pool, C = self.nc, self.pe, self.dve, self.act, self.pool, self.C
        with ExitStack() as stack:
            def sb(name, shape):
                return stack.enter_context(nc.sbuf_tensor(name, shape, F32))
            qkv = sb("fa_qkv", [P, 3 * H2, SM])
            vb = sb("fa_v", [P, 3, H2 * P])
            r = sb("fa_r", [P, H2, SM])
            sq = sb("fa_sq", [P, H2, SM])

            def put(eng, i, q, ps):
                dst = qkv[:, bass.ds(i * 8 + q, 1), :].rearrange("p o n -> p (o n)")
                return eng.tensor_copy(dst, ps) if eng is dve else act.activation(dst, ps, ACT.Copy)

            self.dense_cols(3 * H2 * P // COLS_W, self.xT, SM, put)
            self.meet()
            ws = self.stat[:, 0:1]
            self.V(dve.tensor_scalar(ws, C["q_norm"][:, 0:1], DH ** -0.5, None, ALU.mult))
            for j, gain in ((0, ws), (1, C["k_norm"][:, 0:1])):
                x = qkv[:, j * H2:(j + 1) * H2, :]
                self.feature_rms(x, SM, H2, DH, EPS, r[:, :, :], sq[:, :, :])
                self.V(dve.scalar_tensor_tensor(x, x, gain, r[:, :, :], ALU.mult, ALU.mult))
            q, k, v = (qkv[:, j * H2:(j + 1) * H2, :] for j in range(3))
            self.meet()
            moved = {}
            j = 0
            for t, (c, n) in enumerate(TILES):
                for half in range(2):
                    ps = self.bank(j)[0:n, :]
                    for hh in range(4):
                        tr = pe.transpose(ps[:, hh * P:(hh + 1) * P], v[:, 4 * half + hh, c:c + n], C["ident"][:, :])
                    tr = self.T(tr)
                    wait(act, tr)
                    self.A(act.activation(vb[0:n, t, half * 512:half * 512 + 512], ps, ACT.Copy))
                    j += 1
            wait(pe, self.c_act.now())
            m = {}
            xs = [sb(f"fa_x{b}", [P, SM]) for b in range(4)]
            pT = [sb(f"fa_p{b}", [P, 3, P]) for b in range(2)]
            st = sb("fa_stat", [P, 16, 4])
            units = [(h, t) for h in range(H2) for t in range(NT)]

            def scores(u):
                h, t = units[u]
                w = META + P * (t + 1)
                ps = self.bank(u % 4, w)
                wait(pe, m.get(("x", u - 4)))
                pe.matmul(ps, q[:, h, META + t * P:META + (t + 1) * P], k[:, h, 0:w], start=True, stop=False)
                m["z", u] = self.T(pe.matmul(ps, C["pick"][0:H2, h * P:(h + 1) * P], R["ncum"][:, 0:w], start=False, stop=True))
                x = xs[u % 4][:, 0:w]
                wait(dve, m["z", u], m.get(("tr", u - 4)))
                m["x", u] = self.V(dve.tensor_tensor(x, ps, C["causal"][:, SM - w:SM], ALU.add))
                wait(dve, m["x", u])
                mx = self.V(dve.tensor_reduce(st[:, u, 0:1], x, AX, ALU.max, negate=True))
                wait(act, mx)
                e = self.A(act.activation(x, x, ACT.Exp, bias=st[:, u, 0:1], accum_out=st[:, u, 1:2]))
                m["e", u] = e

            def normalise(u):
                h, t = units[u]
                w = META + P * (t + 1)
                x = xs[u % 4][:, 0:w]
                wait(dve, m["e", u])
                wait(dve, self.V(dve.reciprocal(st[:, u, 2:3], st[:, u, 1:2])))
                n_ = self.V(dve.tensor_scalar(x, x, st[:, u, 2:3], None, ALU.mult))
                ps = self.bank(4 + u % 2)
                wait(pe, n_, m.get(("pT", u - 2)))
                for j in range(t + 2):
                    c, n = TILES[j]
                    tr = pe.transpose(ps[0:n, j * P:(j + 1) * P], x[:, c:c + n], C["ident"][:, :])
                m["tr", u] = self.T(tr)
                p = pT[u % 2]
                wait(act, m["tr", u], m.get(("o", u - 2)))
                self.A(act.activation(p[0:META, 0, :], ps[0:META, 0:P], ACT.Copy))
                m["pT", u] = self.A(act.activation(p[:, 1:t + 2, :], ps[:, P:(t + 2) * P].rearrange("p (a b) -> p a b", b=P), ACT.Copy))
                po = self.bank(6 + u % 2, P)
                wait(pe, m["pT", u], m.get(("ob", u - 2)))
                for j in range(t + 2):
                    n = TILES[j][1]
                    mm = pe.matmul(po, vb[0:n, j, h * P:(h + 1) * P], p[0:n, j, :], start=(j == 0), stop=(j == t + 1))
                m["o", u] = self.T(mm)
                wait(dve, m["o", u])
                m["ob", u] = self.V(dve.tensor_copy(self.obT[:, h, t * P:(t + 1) * P], po))

            for u in range(len(units) + 1):
                if u < len(units):
                    scores(u)
                if u:
                    normalise(u - 1)
            self.meet()

    def merge_branches(self, xs):
        nc, dve, act = self.nc, self.dve, self.act
        with nc.sbuf_tensor("gates", [P, 2 * KD, S], F32) as gates, nc.sbuf_tensor("branch_y", [P, 2 * KD, S], F32) as y:
            def put(dst):
                def f(eng, i, q, ps):
                    d = dst[:, bass.ds(i * 8 + q, 1), :].rearrange("p o n -> p (o n)")
                    return eng.tensor_copy(d, ps) if eng is dve else act.activation(d, ps, ACT.Copy)
                return f
            self.dense_cols(8, xs, S, put(gates))
            self.meet()
            sig = self.A(act.activation(gates[:, :, :], gates[:, :, :], ACT.Sigmoid))
            for b, o in enumerate((self.oaT, self.obT)):
                self.dense_cols(4, o, S, put(y[:, b * KD:(b + 1) * KD, :]))
                wait(dve, sig, self.c_act.now(), self.c_dve.now())
                self.V(dve.tensor_tensor(y[:, b * KD:(b + 1) * KD, :], y[:, b * KD:(b + 1) * KD, :],
                                         gates[:, b * KD:(b + 1) * KD, :], ALU.mult))
            wait(dve, self.c_dve.now())
            self.V(dve.tensor_tensor(y[:, 0:KD, :], y[:, 0:KD, :], y[:, KD:, :], ALU.add))
            self.meet()
            self.dense_rows(KD, 2, y, lambda i, u, t, ps: self.add_to_h(i, u, t, ps, 2))
            self.meet()

    def experts(self):
        nc, pe, dve, act, pool, C = self.nc, self.pe, self.dve, self.act, self.pool, self.C
        NU = 8
        late = Counter(nc.alloc_semaphore("expert_constants_landed"), 16)
        g_peer, keys = self.sb("g_peer", [P, D]), self.sb("keys", [P, 2 * PEER_H * KEYS])
        self.meet()
        late.mark(act.dma_start(g_peer[:, :], self.ins["c_g_peer"]))
        late.mark(act.dma_start(keys[:, :], self.ins["c_keys"]))
        xb = self.hn[:, 0:NT, :]
        wait(dve, self.rms_scale([(ap, n) for ap, n, _ in self.h_tiles()], D, self.rstd, self.junk), late.now())
        for t in range(NT):
            x = self.V(dve.scalar_tensor_tensor(xb[:, t, :], self.h[:, t, :], self.rstd[:, t:t + 1], g_peer[:, :], ALU.mult, ALU.mult))
        wait(pe, x)
        self.turn_cols(self.h_tiles(), [xb[:, t, :] for t in range(NT)], KD, self.xT)
        sc = self.sb("key_scores", [P, NT, 2 * PEER_H * KEYS])
        with nc.sbuf_tensor("queries", [P, 2 * PEER_H, S], F32) as qh:
            def put(eng, i, q, ps):
                d = qh[:, bass.ds(i * 8 + q, 1), :].rearrange("p o n -> p (o n)")
                return eng.tensor_copy(d, ps) if eng is dve else act.activation(d, ps, ACT.Copy)
            self.dense_cols(8, self.xT, S, put)
            self.meet()
            wait(pe, late.now())
            for t in range(NT):
                for b in range(4):
                    ps = self.bank(4 * t + b)
                    for j in range(4):
                        c = 4 * b + j
                        mm = pe.matmul(ps[:, j * KEYS:(j + 1) * KEYS], qh[:, c, t * P:(t + 1) * P],
                                       keys[:, c * KEYS:(c + 1) * KEYS], start=True, stop=True)
                    mm = self.T(mm)
                    wait(dve, mm)
                    self.V(dve.tensor_copy(sc[:, t, b * BANK:(b + 1) * BANK], ps))
            self.meet()
        for t in range(NT):
            for half in range(2):
                mm = pe.matmul(self.bank(2 * t + half), C["ident"][:, :], self.h[:, t, half * BANK:(half + 1) * BANK],
                               start=True, stop=False, skip_group_check=True)
        self.T(mm)

        u_rows = [self.sb(f"u_rows{j}", [P, D]) for j in range(NU)]
        v_rows = [self.sb(f"v_rows{j}", [P, D]) for j in range(NU)]
        u_in = [nc.alloc_semaphore(f"u_landed{j}") for j in range(NU)]
        v_in = [nc.alloc_semaphore(f"v_landed{j}") for j in range(NU)]
        dots, added = Counter(nc.alloc_semaphore("dots_done")), Counter(nc.alloc_semaphore("rows_added"))
        w = self.sb("pick_from", [P, 2 * KEYS])
        w2 = self.sb("pick_rest", [P, 2 * KEYS])
        best = self.sb("best", [P, 2, TOPK])
        where = self.sb("where", [P, 2, TOPK], U32)
        wheref = self.sb("wheref", [P, 2, TOPK])
        top = [self.sb(f"top{t}", [P, TOPK]) for t in range(NT)]
        ci = self.sb("ci", [P, TOPK], U32)
        part = self.sb("part", [P, 2, TOPK], U32)
        partf = self.sb("partf", [P, 2, TOPK])
        hot = self.sb("hot", [P, 2, TOPK, TOPK])
        half_index = self.sb("half_index", [P, 2, TOPK])
        index = [self.sb(f"index{t}", [P, TOPK], I32) for t in range(NT)]
        gate = [self.sb(f"gate{t}", [P, TOPK]) for t in range(NT)]
        soft = self.sb("soft", [P, NT, 4])
        act_in = [self.sb(f"act_in{t}", [P, TOPK]) for t in range(NT)]
        coef = [self.sb(f"coef{t}", [P, TOPK]) for t in range(NT)]
        diag = self.sb("diag", [P, TOPK, P])
        for j in range(NU):
            dots.mark(dve.memset(w[:, j:j + 1], 0.0))
        for j in range(TOPK):
            added.mark(dve.memset(w[:, NU + j:NU + j + 1], 0.0))
        wait(dve, dots.now(), added.now())

        def v(ins):
            m = self.V(ins)
            wait(dve, m)
            return m

        def apart(engine):
            engine.nop(nofuse=True)

        def top16(values, rest, val, idx):
            apart(dve)
            v(dve.max(val[:, 0:8], values))
            apart(dve)
            self.V(dve.max_index(idx[:, 0:8], val[:, 0:8], values))
            v(dve.match_replace(rest, val[:, 0:8], values, NEG))
            apart(dve)
            v(dve.max(val[:, 8:16], rest))
            apart(dve)
            v(dve.max_index(idx[:, 8:16], val[:, 8:16], rest))

        def choose(i, t, free):
            v(dve.tensor_copy(w[:, :], sc[:, t, bass.ds(i * (2 * KEYS), 2 * KEYS)]))
            for j in range(2):
                f = slice(j * KEYS, (j + 1) * KEYS)
                top16(w[:, f], w2[:, f], best[:, j, :], where[:, j, :])
            v(dve.tensor_copy(wheref[:, :, :], where[:, :, :]))
            v(dve.tensor_tensor(w[:, :].rearrange("p (a b) -> p a b", a=TOPK), best[:, 0, :, None].to_broadcast([P, TOPK, TOPK]),
                                best[:, 1, None, :].to_broadcast([P, TOPK, TOPK]), ALU.add))
            top16(w[:, :], w2[:, :], top[t], ci)
            self.V(dve.tensor_scalar(part[:, 0, :], ci[:, :], 4, None, ALU.logical_shift_right))
            v(dve.tensor_scalar(part[:, 1, :], ci[:, :], TOPK - 1, None, ALU.bitwise_and))
            v(dve.tensor_copy(partf[:, :, :], part[:, :, :]))
            for j in range(2):
                v(dve.tensor_tensor(hot[:, j], C["iota"][:, None, :].to_broadcast([P, TOPK, TOPK]),
                                    partf[:, j, :, None].to_broadcast([P, TOPK, TOPK]), ALU.is_equal))
                v(dve.tensor_tensor(hot[:, j], hot[:, j], wheref[:, j, None, :].to_broadcast([P, TOPK, TOPK]), ALU.mult))
            v(dve.tensor_reduce(half_index[:, :, :], hot[:, :, :, :], AX, ALU.add))
            for sem, value in free:
                dve.wait_ge(sem, value)
            v(dve.scalar_tensor_tensor(index[t][:, :], half_index[:, 0, :], float(KEYS), half_index[:, 1, :], ALU.mult, ALU.add))
            m = v(dve.tensor_scalar(soft[:, t, 0:1], top[t][:, 0:1], -1.0, None, ALU.mult))
            wait(act, m)
            m = self.A(act.activation(gate[t][:, :], top[t][:, :], ACT.Exp, bias=soft[:, t, 0:1], accum_out=soft[:, t, 1:2]))
            wait(dve, m)
            v(dve.reciprocal(soft[:, t, 2:3], soft[:, t, 1:2]))
            return v(dve.tensor_scalar(gate[t][:, :], gate[t][:, :], soft[:, t, 2:3], None, ALU.mult))

        def row_landed(i, t, k):
            return i * (NT * TOPK // NU * 16) + (t * (TOPK // NU) + k // NU + 1) * 16

        def read_before(c, base, i, t, k, back):
            return i * (NT * TOPK) + (base + t * TOPK + k + 1 - back)

        def unit(i, t, ready, following):
            wait(pool, ready)
            for rows, sems, counter, base, table in (
                    (u_rows, u_in, dots, NU, self.ins["expert_u"]), (v_rows, v_in, added, TOPK, self.ins["expert_v"])):
                for k in range(TOPK):
                    pool.wait_ge(counter.sem, read_before(counter, base, i, t, k, NU))
                    apart(pool)
                    pool.indirect_dma_start(rows[k % NU][:, :], None, table,
                                            bass.IndirectOffsetOnAxis(ap=index[t][:, k:k + 1], axis=0)).then_inc(sems[k % NU], 16)
            for k in range(TOPK):
                dve.wait_ge(u_in[k % NU], row_landed(i, t, k))
                dots.mark(dve.tensor_tensor_reduce(u_rows[k % NU][:, :], u_rows[k % NU][:, :], xb[:, t, :], 1.0, 0.0,
                                                   ALU.mult, ALU.add, act_in[t][:, k:k + 1]))
            wait(act, dots.now())
            m = self.A(act.activation(coef[t][:, :], act_in[t][:, :], ACT.Gelu))
            wait(dve, m)
            m = self.V(dve.tensor_tensor(coef[t][:, :], coef[t][:, :], gate[t][:, :], ALU.mult))
            wait(act, m)
            wait(dve, m)
            for k in range(TOPK):
                act.wait_ge(added.sem, read_before(added, TOPK, i, t, k, TOPK))
                d = self.A(act.activation(diag[:, k, :], C["ident"][:, :], ACT.Copy, scale=coef[t][:, k:k + 1]))
                wait(pe, d)
                pe.wait_ge(v_in[k % NU], row_landed(i, t, k))
                for half in range(2):
                    mm = pe.matmul(self.bank(2 * t + half), diag[:, k, :], v_rows[k % NU][:, half * BANK:(half + 1) * BANK],
                                   start=False, stop=False, skip_group_check=True)
                added.mark(mm)
            if following:
                free = [(v_in[j], row_landed(i, t, TOPK - NU + j)) for j in range(NU)]
                return choose(i + 1, t, free)

        ready = [choose(0, t, []) for t in range(NT)]
        wait(pool, *ready)
        per = self.unit_counts(dots, added)
        with loop(nc, PEER_H - 1, [ENG.PE, ENG.DVE, ENG.Activation, ENG.Pool], per) as i:
            for t in range(NT):
                unit(i, t, Mark(self.c_dve, self.c_dve.value, self.c_dve.loop) if t == 0 else None, True)
        wait(pool, self.c_dve.now())
        for t in range(NT):
            unit(PEER_H - 1, t, None, False)
        wait(dve, added.now())
        for t in range(NT):
            for half in range(2):
                self.V(dve.tensor_copy(self.h[:, t, half * BANK:(half + 1) * BANK], self.bank(2 * t + half)))

    def unit_counts(self, dots, added):
        return {dots: NT * TOPK, added: NT * TOPK, self.c_dve: 31 * NT, self.c_act: 18 * NT}

    def debug_out(self):
        self.meet()
        wait(self.sp, *[c.now() for c in (self.c_pe, self.c_dve, self.c_act, self.c_pool, self.blocks)])
        self.store()

    def store(self):
        done = Counter(self.nc.alloc_semaphore("stored"), 16)
        for t in range(NT):
            last = done.mark(self.sp.dma_start(self.out.rearrange("o (t p) d -> t p (o d)", p=P)[t], self.h[:, t, :]))
        wait(self.sp, last)

    def build(self):
        self.setup()
        steps = [self.stick_breaking, lambda: self.mlp(self.C["g_mlp0"], "0"), self.retention,
                 lambda: self.mlp(self.C["g_mlp1"], "1"), self.final_norm, self.mixer, self.experts]
        for n, s in enumerate(steps):
            s()
            if self.stop == n + 1:
                break
        self.debug_out()


def program(nc, ins, out, stop=None):
    with nc.allow_non_contiguous_dma(reason="layouts"):
        Program(nc, ins, out, stop).build()


def host_arrays(a):
    weights, small = weight_stream(a)
    arrays = {"x": a["x"], "meta": a["meta_tokens_2"], "expert_u": a["expert_u_2"][0],
              "expert_v": a["expert_v_2"][0], "weights": weights, "c_small": small}
    for name, v in (*shape_constants().items(), *vectors(a).items()):
        arrays["c_" + name] = v
    return {name: np.ascontiguousarray(v) for name, v in arrays.items()}


def kernel(**inputs):
    import concourse.bacc as bacc
    from concourse.bass_utils import run_bass_kernel_spmd

    arrays = host_arrays({k: np.asarray(v) for k, v in inputs.items()})
    nc = bacc.Bacc("TRN2", target_bir_lowering=False, num_devices=1)
    ins = {name: nc.dram_tensor(name, v.shape, mybir.dt.from_np(v.dtype), kind="ExternalInput").ap()
           for name, v in arrays.items()}
    out = nc.dram_tensor("out", (1, S, D), F32, kind="ExternalOutput").ap()
    program(nc, ins, out)
    r = run_bass_kernel_spmd(nc, [arrays], core_ids=[0])
    return r.results[0]["out"]
```

```python
from contextlib import ExitStack, contextmanager

import numpy as np

import concourse.bass as bass
from concourse import mybir

F32 = mybir.dt.float32
F32R = mybir.dt.float32r
I32 = mybir.dt.int32
U32 = mybir.dt.uint32
ALU = mybir.AluOpType
ACT = mybir.ActivationFunctionType
AX = mybir.AxisListType.X
ENG = mybir.EngineType

P = 128
D = 1024
KD = D // P
S = 256
NT = S // P
META = 16
SM = META + S
HID = 4096
SB_H, SB_D = 16, 64
RET_H, RET_QK, RET_V = 4, 256, 512
H2, DH = 8, 128
CONV_K = 4
CONV_CH = 3 * H2 * DH
KEYS, TOPK, PEER_H = 128, 16, 8
EPS = 1e-6
BANK = 512
BLK = 2048
TURN = 4
SLOTS = 2
PARTS = 2
NEG = -1.0e30
COLS_W = BLK // KD
ROWS_K = BLK // BANK
TILES = [(0, META), (META, P), (META + P, P)]


FIRST_BLOCK = ("sb_keep", "sb_cap", "cos", "sin", "decay", "g_final")
PEER_ONLY = ("g_peer", "keys")


def cols_blocks(w):
    k, n = w.shape
    return w.reshape(KD, P, n // COLS_W, COLS_W).transpose(2, 1, 0, 3).reshape(-1, P, BLK)


def rows_blocks(w):
    k, n = w.shape
    w = w.reshape(k // (ROWS_K * P), ROWS_K, P, n // BANK, BANK)
    return w.transpose(3, 0, 2, 1, 4).reshape(-1, P, BLK)


def per_partition(v):
    return v.reshape(-1, P).T


def weight_stream(a):
    w_in = a["w_in_2"][0]
    at = np.cumsum([0, CONV_CH, D, H2, H2, CONV_CH, H2, 2 * D])
    sb, ret = a["w_sb_in"][0], a["w_ret_in"][0]
    parts = [
        cols_blocks(sb[:, :2 * D]), rows_blocks(sb[:, 2 * D:]), rows_blocks(a["w_sb_out"][0]),
        cols_blocks(a["w_mlp_up"][0]), rows_blocks(a["w_mlp_down"][0]),
        cols_blocks(ret[:, :2 * D]), rows_blocks(ret[:, 2 * D:]), rows_blocks(a["w_ret_out"][0]),
        cols_blocks(a["w_mlp_up"][1]), rows_blocks(a["w_mlp_down"][1]),
        cols_blocks(w_in[:, at[0]:at[1]]), cols_blocks(w_in[:, at[1]:at[2]]),
        cols_blocks(w_in[:, at[4]:at[5]]), cols_blocks(w_in[:, at[6]:at[7]]),
        cols_blocks(a["w_branch_2"][0, 0]), cols_blocks(a["w_branch_2"][0, 1]),
        rows_blocks(a["w_out_2"][0]), cols_blocks(a["peer_wq_2"][0]),
    ]
    small = np.concatenate([w_in[:, at[2]:at[4]], w_in[:, at[5]:at[6]]], axis=1)
    small = small.reshape(KD, P, 3 * H2).transpose(1, 0, 2).reshape(P, -1)
    return np.concatenate(parts), small


def pack(arrays):
    where, at = {}, 0
    for name, v in arrays.items():
        where[name] = (v.shape[0], at, v.shape[1])
        at += v.shape[1]
    return np.concatenate([np.pad(v, ((0, P - v.shape[0]), (0, 0))) for v in arrays.values()], 1), where


def shape_constants():
    p, f = np.arange(P)[:, None], np.arange(P)[None, :]
    c = {}
    c["ident"] = (p == f)
    c["ones"] = np.ones((P, P))
    c["from_here"] = (p >= f)
    before = (p < f)
    c["sb_keep"] = np.concatenate([before, np.ones((P, P)), before], 1)
    c["sb_cap"] = np.where(c["sb_keep"] > 0, 0.0, NEG)
    inv = (1.0 / (np.float32(10000.0) ** np.linspace(0, 1, P, dtype=np.float32))).astype(np.float32)
    ang = (np.arange(S, dtype=np.float32)[None, :] * inv[:, None]).astype(np.float32)
    c["cos"], c["sin"] = np.cos(ang), np.sin(ang)
    lg = np.log1p(-np.exp2(-5.0 - np.arange(RET_H)))
    rel = np.concatenate([f - p, f + P - p, f - p], 1).astype(np.float64)
    c["decay"] = np.concatenate([np.where(rel >= 0, np.exp(g * np.maximum(rel, 0)), 0) for g in lg], 1)
    c["earlier"] = (p < f)
    c["not_later"] = (p <= f)
    c["merge"] = np.concatenate([((p >> l) == (f >> l) + 1) & ((p >> l) % 2 == 1)
                                 for l in range(7)], 1)
    c["causal"] = np.concatenate([np.zeros((P, SM - P)), np.where(f <= p, 0.0, NEG)], 1)
    head = np.zeros((P, H2 * P))
    for h in range(H2):
        head[h, h * P:(h + 1) * P] = 1.0
    c["to_row"] = np.broadcast_to(np.eye(H2).reshape(1, -1), (P, H2 * H2))
    c["pick"] = head[:H2]
    c["iota"] = np.broadcast_to(np.arange(TOPK), (P, TOPK))
    return {k: np.ascontiguousarray(v, dtype=np.float32) for k, v in c.items()}


def vectors(a):
    conv = a["conv_w_2"][0].reshape(CONV_K, CONV_CH // P, P).transpose(2, 1, 0).reshape(P, -1)
    v = {
        "g_mix0": per_partition(a["g_mix"][0]), "g_mix1": per_partition(a["g_mix"][1]),
        "g_mlp0": per_partition(a["g_mlp"][0]), "g_mlp1": per_partition(a["g_mlp"][1]),
        "g_mixer": per_partition(a["norm_mix_2"][0]), "conv": conv,
        "o_norm": a["o_norm_a_2"][0][:, None], "q_norm": a["q_norm_b_2"][0][:, None],
        "k_norm": a["k_norm_b_2"][0][:, None],
    }
    for n in ("a_log", "dt_bias", "f_bias"):
        v[n] = a[n + "_2"][0][:, None]
    rows = {"g_final": a["g_final"], "g_peer": a["norm_ffn_2"][0]}
    v.update({k: np.broadcast_to(x, (P, D)) for k, x in rows.items()})
    v["keys"] = a["peer_sub_keys_2"][0].transpose(3, 1, 0, 2).reshape(P, -1)
    return {k: np.ascontiguousarray(x) for k, x in v.items()}


class Mark:

    def __init__(self, counter, value, loop=None):
        self.counter, self.value, self.loop = counter, value, loop

    def at(self):
        if self.loop is None:
            return self.value
        i, per = self.loop
        return i * per[self.counter] + self.value

    def back(self, turns=1):
        value = self.value - turns * self.loop[1][self.counter]
        assert value >= 1, "a wait needs a positive value"
        return Mark(self.counter, value, self.loop)


class Counter:

    def __init__(self, sem, step=1):
        self.sem, self.step, self.value, self.loop = sem, step, 0, None

    def mark(self, ins):
        ins.then_inc(self.sem, self.step)
        self.value += self.step
        return Mark(self, self.value, self.loop)

    def now(self):
        return Mark(self, self.value, self.loop)


@contextmanager
def loop(nc, turns, engines, per):
    entry = {c: c.value for c in per}
    with nc.Fori(0, turns, engines=engines) as i:
        for c in per:
            c.loop = (i, per)
        yield i
        for c in per:
            assert c.value - entry[c] == per[c], (c.sem, c.value - entry[c], per[c])
    for c in per:
        c.value, c.loop = entry[c] + turns * per[c], None


def wait(engine, *marks):
    best = {}
    for m in marks:
        if m is None:
            continue
        o = best.get(m.counter)
        if o is None or o.loop is not m.loop and m.loop is not None or o.loop is m.loop and m.value > o.value:
            best[m.counter] = m
    for m in best.values():
        if m.loop is not None or m.value > 0:
            engine.wait_ge(m.counter.sem, m.at())


class Program:
    def __init__(self, nc, ins, out, where, stop=None):
        self.where = where
        self.nc, self.ins, self.out, self.stop = nc, ins, out, stop
        self.pe, self.dve, self.act, self.pool, self.sp = nc.tensor, nc.vector, nc.scalar, nc.gpsimd, nc.sync
        self.c_pe = Counter(nc.alloc_semaphore("tensor_done"))
        self.c_dve = Counter(nc.alloc_semaphore("vector_done"))
        self.c_act = Counter(nc.alloc_semaphore("scalar_done"))
        self.c_pool = Counter(nc.alloc_semaphore("gpsimd_done"))
        self.out_v = Counter(nc.alloc_semaphore("vector_moved"))
        self.out_a = Counter(nc.alloc_semaphore("scalar_moved"))
        self.blocks = Counter(nc.alloc_semaphore("blocks_read"))
        self.hi_made = Counter(nc.alloc_semaphore("block_hi_made"))
        self.lo_made = Counter(nc.alloc_semaphore("block_lo_made"))
        self.block_full = [nc.alloc_semaphore(f"block_full{s}") for s in range(SLOTS)]
        self.n_block = 0
        self.first_block = ExitStack()

    def sb(self, name, shape, dt=F32):
        return self.nc.alloc_sbuf_tensor(name, shape, dt)

    def V(self, ins): return self.c_dve.mark(ins)
    def A(self, ins): return self.c_act.mark(ins)
    def G(self, ins): return self.c_pool.mark(ins)
    def T(self, ins): return self.c_pe.mark(ins)

    def everything(self):
        return [c.now() for c in (self.c_pe, self.c_dve, self.c_act, self.c_pool, self.blocks, self.out_v, self.out_a)]

    def vector(self):
        return self.c_dve.now(), self.out_v.now()

    def scalar(self):
        return self.c_act.now(), self.out_a.now()

    def meet(self):
        all_marks = self.everything()
        for e in (self.pe, self.dve, self.act, self.pool):
            wait(e, *all_marks)

    def bank(self, b, width=BANK, count=1):
        return self.psum[:, b * BANK:b * BANK + width]

    def split_block(self, i, per_turn, b):
        s, n = b % SLOTS, BLK // PARTS
        raw, hi, lo = self.raw[s], self.w_hi[s], self.w_lo[s]
        self.act.wait_ge(self.block_full[s], i * (16 * per_turn // SLOTS) + 16 * (b // SLOTS + 1))
        for p in range(PARTS):
            f = slice(p * n, (p + 1) * n)
            made = self.hi_made.mark(self.act.activation(hi[:, f], raw[:, f], ACT.Copy))
            wait(self.dve, made)
            self.lo_made.mark(self.dve.tensor_tensor(lo[:, f], raw[:, f], hi[:, f], ALU.subtract))

    def block_split(self, i, per_turn, b, k_pieces):
        self.pe.wait_ge(self.lo_made.sem, i * (PARTS * per_turn) + PARTS * (b + 1))
        return [w[b % SLOTS][:, :].rearrange("p (k n) -> p k n", k=k_pieces) for w in (self.w_hi, self.w_lo)]

    def split(self, x, pair):
        hi, lo = pair
        wait(self.dve, self.A(self.act.activation(hi, x, ACT.Copy)))
        return self.V(self.dve.tensor_tensor(lo, x, hi, ALU.subtract))

    def product(self, out, w, x, first, last):
        (wh, wl), (xh, xl) = w, x
        self.pe.matmul(out, wh, xh, start=first, stop=False)
        self.pe.matmul(out, wh, xl, start=False, stop=False)
        return self.pe.matmul(out, wl, xh, start=False, stop=last)

    def dense_cols(self, n_blocks, x, width, evac, counts=None, final=False):
        nc, pe = self.nc, self.pe
        assert self.n_block % TURN == 0 and n_blocks % TURN == 0
        first, turns = self.n_block, n_blocks // TURN
        xh, xl = x

        def turn(i, ahead):
            v0, a0 = self.out_v.value, self.out_a.value
            for s in range(TURN):
                w = self.block_split(i, TURN, first + s, KD)
                wait(pe, Mark(self.out_v, v0 + s + 1 - TURN, self.out_v.loop),
                     Mark(self.out_a, a0 + s + 1 - TURN, self.out_a.loop))
                for sub in range(2):
                    f = slice(sub * P, (sub + 1) * P)
                    for k in range(KD):
                        mm = self.product(self.bank(2 * s + sub, width), [y[:, k, f] for y in w],
                                          (xh[:, k, 0:width], xl[:, k, 0:width]), k == 0, k == KD - 1)
                read = self.blocks.mark(mm)
                wait(self.dve, read)
                wait(self.act, read)
                if s < ahead:
                    self.split_block(i, TURN, first + s + SLOTS)
                ps = self.psum[:, 2 * s * BANK:(2 * s + 2) * BANK].rearrange("p (b n) -> p b n", b=2)[:, :, 0:width]
                v, a = evac(i, s, ps)
                for counter, ins in ((self.out_v, v), (self.out_a, a)):
                    if ins is not None:
                        counter.mark(ins)

        per = {self.blocks: TURN, self.out_v: TURN, self.out_a: TURN,
               self.hi_made: PARTS * TURN, self.lo_made: PARTS * TURN, **(counts or {})}
        with loop(nc, turns - final, [ENG.PE, ENG.DVE, ENG.Activation], per) as i:
            turn(i, TURN)
        if final:
            turn(turns - 1, TURN - SLOTS)
        self.n_block += n_blocks

    def dense_rows(self, n_k, halves, x, evac):
        nc, pe = self.nc, self.pe
        wait(pe, self.out_a.now(), self.out_v.now())
        per_half = n_k // ROWS_K
        unroll = max(1, TURN // per_half)
        per_turn = per_half * unroll
        assert self.n_block % SLOTS == 0 and per_turn % SLOTS == 0 and halves % unroll == 0
        first, n_out = self.n_block, unroll * NT
        per = {self.blocks: per_turn, self.out_v: n_out, self.hi_made: PARTS * per_turn, self.lo_made: PARTS * per_turn}
        with loop(nc, halves // unroll, [ENG.PE, ENG.DVE, ENG.Activation], per) as i:
            base = self.out_v.value
            for u in range(unroll):
                for kb in range(per_half):
                    b = u * per_half + kb
                    w = self.block_split(i, per_turn, first + b, ROWS_K)
                    for t in range(NT):
                        if kb == 0:
                            wait(pe, Mark(self.out_v, base if n_out < 4 else base + u * NT + t + 1 - n_out, self.out_v.loop))
                        for k in range(ROWS_K):
                            kk = kb * ROWS_K + k
                            mm = self.product(self.bank(u * NT + t), [y[:, kk, t * P:(t + 1) * P] for y in x],
                                              [y[:, k, :] for y in w], kk == 0, kk == n_k - 1)
                    read = self.blocks.mark(mm)
                    wait(self.dve, read)
                    wait(self.act, read)
                    if kb == per_half - 1:
                        for t in range(NT):
                            self.out_v.mark(evac(i, u, t, self.bank(u * NT + t)))
                    self.split_block(i, per_turn, first + b + SLOTS)
        self.n_block += per_half * halves

    def inverse_root(self, out, x):
        power = self.power[0:x.shape[0], :].to_broadcast(list(x.shape))
        return self.G(self.pool.tensor_tensor(out, x, power, ALU.pow))

    def rms_scale(self, tiles):
        r, width, rstd, junk = self.stat, D, self.rstd, self.junk
        for j, (ap, n) in enumerate(tiles):
            sq = self.A(self.act.activation(junk[0:n, 0:width], ap, ACT.Square, accum_out=r[0:n, j:j + 1]))
            wait(self.act, sq)
        for j, (ap, n) in enumerate(tiles):
            wait(self.pool, sq)
            wait(self.pool, self.G(self.pool.tensor_scalar(r[0:n, 4 + j:5 + j], r[0:n, j:j + 1], 1.0 / width, EPS, ALU.mult, ALU.add)))
            m = self.inverse_root(rstd[0:n, j:j + 1], r[0:n, 4 + j:5 + j])
        return m

    def norm_cols(self, tiles, gain):
        self.meet()
        with self.nc.sbuf_tensor(f"scales{self.n_block}", [P, len(tiles), P], F32) as scales:
            wait(self.dve, self.rms_scale([(ap, n) for ap, n, _ in tiles]))
            for j, (ap, n, _) in enumerate(tiles):
                ready = self.V(self.dve.tensor_scalar(scales[0:n, j, 0:n], self.C["ident"][0:n, 0:n],
                                                      self.rstd[0:n, j:j + 1], None, ALU.mult))
            wait(self.pe, ready)
            self.turn_cols(tiles, [ap for ap, _, _ in tiles], KD, self.x, lambda k: gain[:, k:k + 1],
                           [scales[0:n, j, 0:n] for j, (_, n, _) in enumerate(tiles)])

    def turn_cols(self, tiles, rows, pieces, out, gain=None, scales=None):
        width = max(c + n for _, n, c in tiles)
        moved = {}
        for k in range(pieces):
            wait(self.pe, moved.get(k - 8))
            for j, ((_, n, c), r) in enumerate(zip(tiles, rows)):
                dst, src = self.bank(k % 8)[:, c:c + n], r[:, k * P:(k + 1) * P]
                tr = self.pe.matmul(dst, src, scales[j], start=True, stop=True) if scales \
                    else self.pe.transpose(dst, src, self.C["ident"][0:n, 0:n])
            src, (hi, lo) = self.bank(k % 8, width), (y[:, k, 0:width] for y in out)
            wait(self.act, self.T(tr))
            if gain:
                wait(self.dve, self.A(self.act.activation(hi, src, ACT.Copy, scale=gain(k))))
                moved[k] = self.V(self.dve.scalar_tensor_tensor(lo, src, gain(k), hi, ALU.mult, ALU.subtract))
            else:
                moved[k] = self.split(src, (hi, lo))
        wait(self.pe, moved[pieces - 1])

    def setup(self):
        nc = self.nc
        self.raw = [self.sb(f"weights{s}", [P, BLK]) for s in range(SLOTS)]
        self.w_hi = [self.sb(f"weights_hi{s}", [P, BLK], F32R) for s in range(SLOTS)]
        self.w_lo = [self.sb(f"weights_lo{s}", [P, BLK], F32R) for s in range(SLOTS)]
        self.psum = nc.alloc_psum_tensor("banks", [P, 8 * BANK], F32)
        self.h = self.sb("h", [P, NT, D])
        self.x = [self.sb(n, [P, KD, SM], F32R) for n in ("x_hi", "x_lo")]
        self.junk = self.sb("junk", [P, D])
        self.stat = self.sb("stat", [P, 16])
        self.rstd = self.sb("rstd", [P, 4])
        self.power = self.sb("power", [P, 1])
        self.meta = self.sb("meta_rows", [META, D])
        self.ret_stat = self.sb("ret_stat", [P, NT * RET_H, 12])
        self.C = {}
        self.c_load = Counter(nc.alloc_semaphore("constants_landed"), 16)
        self.x_in = Counter(nc.alloc_semaphore("x_landed"), 16)
        self.x_in.mark(self.act.dma_start(self.h[:, :, :], self.ins["x"].rearrange("o (t p) d -> p (o t) d", p=P)))
        self.x_in.mark(self.act.dma_start(self.meta[:, :], self.ins["meta"]))
        self.load_constants("always", self.act, self.c_load)
        self.load_constants("first", self.act, self.c_load, self.first_block)
        w = self.ins["weights"]
        n = {1: 20, 2: 52, 3: 84, 4: 116, 5: 116, 6: 164}.get(self.stop, w.shape[0])
        for s in range(SLOTS):
            self.sp.dma_start(self.raw[s][:, :], w[s]).then_inc(self.block_full[s], 16)
        with nc.Fori(1, n // SLOTS, engines=[ENG.SP]) as i:
            for s in range(SLOTS):
                self.sp.wait_ge(self.lo_made.sem, i * (PARTS * SLOTS) + PARTS * (s + 1 - SLOTS))
                self.sp.dma_start(self.raw[s][:, :], w[bass.ds(i * SLOTS + s, 1), :, :].rearrange("o p n -> p (o n)"))\
                    .then_inc(self.block_full[s], 16)
        for b in range(SLOTS):
            self.split_block(0, SLOTS, b)
        for k in range(4):
            self.out_v.mark(self.dve.memset(self.stat[:, k:k + 1], 0.0))
            self.V(self.dve.memset(self.stat[:, 4 + k:5 + k], 0.0))
        for e in (self.pe, self.dve, self.act, self.pool):
            wait(e, self.c_load.now(), self.x_in.now())
        for k in range(4):
            self.out_a.mark(self.act.activation(self.stat[:, 8 + k:9 + k], self.C["ident"][:, 0:1], ACT.Copy))
            self.A(self.act.activation(self.stat[:, 12 + k:13 + k], self.C["ident"][:, 0:1], ACT.Copy))
        wait(self.pool, self.G(self.pool.memset(self.power[:, :], -0.5)))

    def load_constants(self, group, engine, counter, stack=None):
        ap = self.ins["constants_" + group]
        t = stack.enter_context(self.nc.sbuf_tensor("sb_" + group, list(ap.shape), F32)) if stack \
            else self.sb("sb_" + group, list(ap.shape))
        for name, (rows, at, n) in self.where[group].items():
            self.C[name] = t[0:rows, at:at + n]
        return counter.mark(engine.dma_start(t[:, :], ap))

    def h_tiles(self):
        return [(self.h[:, t, :], P, t * P) for t in range(NT)]

    def put(self, dst):
        def piece(i, j):
            return dst[:, bass.ds(i * (2 * TURN) + j, 1), :].rearrange("p o n -> p (o n)")

        return lambda i, s, ps: (self.dve.tensor_copy(piece(i, 2 * s), ps[:, 0, :]),
                                 self.act.activation(piece(i, 2 * s + 1), ps[:, 1, :], ACT.Copy))

    def add_to_h(self, i, u, t, ps, turn_halves):
        at = bass.ds((i * turn_halves + u) * BANK, BANK)
        return self.dve.tensor_tensor(self.h[:, t, at], self.h[:, t, at], ps, ALU.add)

    def stick_breaking(self):
        nc, pe, dve, act, pool = self.nc, self.pe, self.dve, self.act, self.pool
        self.norm_cols(self.h_tiles(), self.C["g_mix0"])
        with nc.sbuf_tensor("sb_qk", [P, 16, S], F32) as qk, nc.sbuf_tensor("sb_v", [P, NT, D], F32) as v, \
                nc.sbuf_tensor("sb_o_hi", [P, KD, S], F32R) as o_hi, nc.sbuf_tensor("sb_o_lo", [P, KD, S], F32R) as o_lo, \
                nc.sbuf_tensor("sb_e", [P, 2, 2, 384], F32) as e, nc.sbuf_tensor("sb_sp", [P, 2, 2, 384], F32) as sp, \
                nc.sbuf_tensor("sb_a", [P, 2, 2, 384], F32) as a, \
                nc.sbuf_tensor("sb_z", [P, 3, 2, 384], F32) as zs:
            self.dense_cols(8, self.x, S, self.put(qk))
            self.dense_rows(KD, 2, self.x, lambda i, u, t, ps: dve.tensor_copy(v[:, t, u * BANK:(u + 1) * BANK], ps))
            act.preload_act_table_set("natural_log_exp_and_others")
            self.meet()
            self.V(dve.tensor_scalar(qk[:, 0:8, :], qk[:, 0:8, :], SB_D ** -0.5, None, ALU.mult))
            wait(pe, self.c_dve.now())

            def banks(first, n=384):
                return self.psum[:, first * BANK:(first + 2) * BANK].rearrange("p (b n) -> p b n", b=2)[:, :, 0:n]

            pairs, m = SB_H // 2, {}

            def logits(c):
                wait(pe, m.get(("z copied", c - 2)))
                for j in range(2):
                    r = slice(64 * j, 64 * j + 64)
                    z = self.bank(2 * (c % 2) + j)
                    pe.matmul(z[:, 0:S], qk[r, 8 + c, 0:P], qk[r, c, 0:S], start=True, stop=True)
                    mm = pe.matmul(z[:, S:384], qk[r, 8 + c, P:S], qk[r, c, P:S], start=True, stop=True)
                m["z", c] = self.T(mm)

            def log1p(c):
                b = c % 2
                wait(act, m["exp", c])
                m["ln", c] = self.A(act.activation(e[:, b], e[:, b], ACT.Ln, bias=1.0))
                wait(dve, m["ln", c], m.get(("sums", c - 2)))
                m["sp", c] = self.V(dve.scalar_tensor_tensor(sp[:, b], zs[:, c % 3], 0.0, e[:, b], ALU.max, ALU.add))
                wait(pool, m["sp", c])
                keep = self.C["sb_keep"][:, None, :].to_broadcast([P, 2, 384])
                m["keep", c] = self.G(pool.tensor_tensor(sp[:, b], sp[:, b], keep, ALU.mult))

            def cumulate(c):
                b = c % 2
                wait(pe, m["keep", c], m.get(("o moved", c - 2)))
                for j in range(2):
                    L = self.bank(4 + 2 * b + j)
                    pe.matmul(L[:, 0:S], self.C["from_here"][:, :], sp[:, b, j, 0:S], start=True, stop=False)
                    pe.matmul(L[:, P:S], self.C["ones"][:, :], sp[:, b, j, S:384], start=False, stop=True)
                    mm = pe.matmul(L[:, S:384], self.C["from_here"][:, :], sp[:, b, j, S:384], start=True, stop=True)
                m["sums", c] = self.T(mm)
                wait(dve, m["sums", c], m.get(("o", c - 2)))
                m["d", c] = self.V(dve.tensor_tensor(a[:, b], zs[:, c % 3], banks(4 + 2 * b), ALU.subtract))
                wait(pool, m["d", c])
                cap = self.C["sb_cap"][:, None, :].to_broadcast([P, 2, 384])
                m["masked", c] = self.G(pool.tensor_tensor(a[:, b], a[:, b], cap, ALU.add))

            def exp_abs(c):
                b, z = c % 2, zs[:, c % 3]
                wait(act, m["z", c], m.get(("d", c - 3)))
                m["z copied", c] = self.A(act.activation(z, banks(2 * b), ACT.Copy))
                wait(dve, m["z copied", c], m.get(("sp", c - 2)))
                x = self.V(dve.scalar_tensor_tensor(e[:, b], z, -1.0, z, ALU.mult, ALU.min))
                wait(act, x)
                m["exp", c] = self.A(act.activation(e[:, b], e[:, b], ACT.Exp))

            def weights(c):
                wait(act, m["masked", c])
                m["a", c] = self.A(act.activation(a[:, c % 2], a[:, c % 2], ACT.Exp))

            def values(c):
                b = c % 2
                wait(pe, m["a", c])
                for j in range(2):
                    o = self.psum[64 * j:64 * j + 64, (4 + 2 * b) * BANK:(4 + 2 * b) * BANK + S]
                    f = slice((2 * c + j) * SB_D, (2 * c + j + 1) * SB_D)
                    pe.matmul(o[:, 0:S], v[:, 0, f], a[:, b, j, 0:S], start=True, stop=False)
                    mm = pe.matmul(o[:, P:S], v[:, 1, f], a[:, b, j, S:384], start=False, stop=True)
                m["o", c] = self.T(mm)
                wait(act, m["o", c])
                wait(dve, m["o", c])
                m["o moved", c] = self.split(self.bank(4 + 2 * b, S), (o_hi[:, c, :], o_lo[:, c, :]))

            for c in range(pairs + 3):
                for stage, p in ((weights, c - 3), (logits, c), (log1p, c - 1), (cumulate, c - 2), (exp_abs, c), (values, c - 3)):
                    if 0 <= p < pairs:
                        stage(p)
            self.meet()
            self.dense_rows(KD, 2, (o_hi, o_lo), lambda i, u, t, ps: self.add_to_h(i, u, t, ps, 2))

    def mlp(self, gain, name):
        nc, dve, act = self.nc, self.dve, self.act
        self.norm_cols(self.h_tiles(), gain)
        with ExitStack() as stack:
            hi, lo = (stack.enter_context(nc.sbuf_tensor(f"mlp_{n}{name}", [P, HID // P, S], F32R)) for n in ("hi", "lo"))
            relu, sq = (stack.enter_context(nc.sbuf_tensor(f"mlp_{n}{name}", [P, TURN, 2, S], F32)) for n in ("relu", "sq"))

            def square(i, s, ps):
                at = bass.ds(i * (2 * TURN) + 2 * s, 2)
                r = self.A(act.activation(relu[:, s], ps, ACT.Relu))
                wait(dve, r)
                wait(act, r)
                h = self.out_a.mark(act.activation(hi[:, at, :], relu[:, s], ACT.Square))
                wait(dve, self.V(dve.tensor_tensor(sq[:, s], relu[:, s], relu[:, s], ALU.mult)), h)
                return dve.tensor_tensor(lo[:, at, :], sq[:, s], hi[:, at, :], ALU.subtract), None

            self.dense_cols(16, self.x, S, square, {self.c_act: TURN, self.c_dve: TURN})
            self.meet()
            self.dense_rows(HID // P, 2, (hi, lo), lambda i, u, t, ps: self.add_to_h(i, u, t, ps, 1))

    def retention(self):
        nc, pe, dve, act, pool = self.nc, self.pe, self.dve, self.act, self.pool
        self.norm_cols(self.h_tiles(), self.C["g_mix1"])
        with nc.sbuf_tensor("ret_v", [P, NT, 2 * D], F32) as v, nc.sbuf_tensor("ret_g", [P, NT, 2 * D], F32) as g:
            self.retention_heads(v, g)
            self.meet()
            with nc.sbuf_tensor("ret_hi", [P, 2 * KD, S], F32R) as hi, nc.sbuf_tensor("ret_lo", [P, 2 * KD, S], F32R) as lo:
                self.turn_cols(self.h_tiles(), [g[:, t, :] for t in range(NT)], 2 * KD, (hi, lo))
                self.dense_rows(2 * KD, 2, (hi, lo), lambda i, u, t, ps: self.add_to_h(i, u, t, ps, 1))

    def retention_heads(self, v, g):
        nc, pe, dve, act, pool = self.nc, self.pe, self.dve, self.act, self.pool
        with nc.sbuf_tensor("ret_qk", [P, 16, S], F32) as qk, nc.sbuf_tensor("ret_rot", [P, 16, S], F32) as rot, \
                nc.sbuf_tensor("ret_tmp", [P, 8, S], F32) as tmp, nc.sbuf_tensor("ret_norm", [P, 2, RET_V], F32) as norm:
            self.dense_cols(8, self.x, S, self.put(qk))
            wait(dve, *self.scalar(), *self.vector())
            wait(pool, *self.scalar(), *self.vector())
            ready = []
            for e, mark, o in ((dve, self.V, 0), (pool, self.G, 8)):
                x = qk[:, o:o + 8, :].rearrange("p (h two) s -> p two h s", two=2)
                r = rot[:, o:o + 8, :].rearrange("p (h two) s -> p two h s", two=2)
                w = tmp[:, o // 2:o // 2 + 4, :]
                cos, sin = (self.C[n][:, None, :].to_broadcast([P, 4, S]) for n in ("cos", "sin"))
                for half, op in ((0, ALU.subtract), (1, ALU.add)):
                    a = mark(e.tensor_tensor(r[:, half], x[:, half], cos, ALU.mult))
                    b = mark(e.tensor_tensor(w, x[:, 1 - half], sin, ALU.mult))
                    wait(e, b)
                    a = mark(e.tensor_tensor(r[:, half], r[:, half], w, op))
                    wait(e, a)
                if o:
                    a = mark(e.tensor_scalar(rot[:, 8:16, :], rot[:, 8:16, :], RET_QK ** -0.5, None, ALU.mult))
                ready.append(a)
            self.dense_rows(KD, 4, self.x, lambda i, u, t, ps: dve.tensor_copy(v[:, t, bass.ds((i * 2 + u) * BANK, BANK)], ps))
            self.dense_rows(KD, 4, self.x, lambda i, u, t, ps: dve.tensor_copy(g[:, t, bass.ds((i * 2 + u) * BANK, BANK)], ps))
            wait(act, *self.vector())
            for t in range(NT):
                silu = self.A(act.activation(g[:, t, :], g[:, t, :], ACT.Silu))
            wait(pe, *ready, *self.vector())
            wait(dve, silu, *self.vector(), *ready)
            sc = qk[:, :, :].rearrange("p a b -> p (a b)")
            decay = self.C["decay"][:, :].rearrange("p (h n) -> p h n", h=RET_H)
            m = {}
            for hd in range(RET_H):
                b = self.bank(hd % 2)
                wait(pe, m.get(("sc", hd - 2)))
                for key, (q0, o) in enumerate(((0, 0), (P, S))):
                    for k in range(2):
                        mm = pe.matmul(b[:, o:o + S - q0], rot[:, 8 + 2 * hd + k, key * P:key * P + P],
                                       rot[:, 2 * hd + k, q0:S], start=(k == 0), stop=(k == 1))
                m["s", hd] = self.T(mm)
                wait(dve, m["s", hd])
                s_h = sc[:, hd * 384:hd * 384 + 384]
                m["sc", hd] = self.V(dve.tensor_tensor(s_h, b[:, 0:384], decay[:, hd], ALU.mult))
                wait(pe, m["sc", hd])
                for t in range(NT):
                    n = NT * hd + t
                    o = self.bank(2 + n % 6)
                    wait(pe, m.get(("o", n - 6)))
                    vh = slice(hd * RET_V, (hd + 1) * RET_V)
                    mm = pe.matmul(o, s_h[:, t * P:t * P + P], v[:, 0, vh], start=True, stop=(t == 0))
                    if t:
                        mm = pe.matmul(o, s_h[:, S:384], v[:, 1, vh], start=False, stop=True)
                    m["m", n] = self.T(mm)
                    wait(dve, m["m", n])
                    st = self.ret_stat[:, n, :]
                    wait(dve, self.V(dve.bn_stats(st[:, 0:6], o)))
                    wait(dve, self.V(dve.bn_aggr(st[:, 6:8], st[:, 0:6])))
                    wait(pool, self.c_dve.now())
                    wait(pool, self.G(pool.tensor_scalar(st[:, 8:9], st[:, 7:8], EPS, None, ALU.add)))
                    wait(dve, self.inverse_root(st[:, 10:11], st[:, 8:9]))
                    nrm = norm[:, n % 2, :]
                    wait(dve, self.V(dve.tensor_scalar(nrm, o, st[:, 6:7], st[:, 10:11], ALU.subtract, ALU.mult)))
                    m["o", n] = self.V(dve.tensor_tensor(g[:, t, vh], nrm, g[:, t, vh], ALU.mult))

    def final_norm(self):
        dve = self.dve
        self.meet()
        wait(dve, self.rms_scale([(ap, n) for ap, n, _ in self.h_tiles()]))
        for t in range(NT):
            self.V(dve.scalar_tensor_tensor(self.h[:, t, :], self.h[:, t, :], self.rstd[:, t:t + 1],
                                            self.C["g_final"][:, :], ALU.mult, ALU.mult))
        self.meet()
        self.first_block.close()

    def small_rows(self):
        self.act.preload_act_table_set("natural_log_exp_and_others")
        nc, pe, dve, act = self.nc, self.pe, self.dve, self.act
        with nc.sbuf_tensor("small_hi", [P, KD, 3 * H2], F32R) as hi, nc.sbuf_tensor("small_lo", [P, KD, 3 * H2], F32R) as lo:
            wait(pe, self.split(self.C["small"].rearrange("p (k n) -> p k n", k=KD), (hi[:, :, :], lo[:, :, :])))
            for g in range(3):
                for k in range(KD):
                    mm = self.product(self.bank(g, SM)[0:H2, :], [y[:, k, g * H2:(g + 1) * H2] for y in (hi, lo)],
                                      [y[:, k, :] for y in self.x], k == 0, k == KD - 1)
        done = self.T(mm)
        b, a, f = (self.bank(g, SM)[0:H2, :] for g in range(3))
        R = {n: self.lam[:, j, :] for j, n in enumerate(
            ("beta", "G", "nbe", "tail", "eG", "ncum", "y", "t", "u", "g"))}
        C = self.C

        def v(ins):
            wait(dve, self.V(ins))

        def soft(x):
            v(dve.scalar_tensor_tensor(R["t"], x, -1.0, x, ALU.mult, ALU.min))
            wait(act, self.c_dve.now())
            wait(act, self.A(act.activation(R["t"], R["t"], ACT.Exp)))
            wait(dve, self.A(act.activation(R["t"], R["t"], ACT.Ln, bias=1.0)))

        wait(act, done)
        wait(dve, done)
        wait(dve, self.A(act.activation(R["u"], b, ACT.Exp, scale=-1.0)))
        v(dve.tensor_scalar(R["u"], R["u"], 1.0, None, ALU.add))
        v(dve.reciprocal(R["beta"], R["u"]))
        ea = self.stat[0:H2, 0:1]
        self.A(act.activation(ea, C["a_log"][:, :], ACT.Exp))
        v(dve.tensor_scalar(R["y"], a, C["dt_bias"][:, 0:1], None, ALU.add))
        soft(R["y"])
        v(dve.scalar_tensor_tensor(R["t"], R["y"], 0.0, R["t"], ALU.max, ALU.add))
        v(dve.tensor_scalar(R["g"], R["t"], ea, -1.0, ALU.mult, ALU.mult))
        ones = C["ones"][0:H2, :]
        for c, n in TILES:
            v(dve.tensor_tensor_scan(R["G"][:, c:c + n], ones[:, 0:n], R["g"][:, c:c + n], 0.0, ALU.mult, ALU.add))
        wait(act, self.c_dve.now())
        self.A(act.activation(R["eG"], R["G"], ACT.Exp))
        for c, n in TILES:
            self.A(act.activation(R["tail"][:, c:c + n], R["G"][:, c:c + n], ACT.Exp, scale=-1.0,
                                  bias=R["G"][:, c + n - 1:c + n]))
        wait(dve, self.c_act.now())
        v(dve.scalar_tensor_tensor(R["nbe"], R["beta"], -1.0, R["eG"], ALU.mult, ALU.mult))
        v(dve.tensor_scalar(R["y"], f, C["f_bias"][:, 0:1], None, ALU.add))
        soft(R["y"])
        v(dve.tensor_scalar(R["y"], R["y"], -1.0, 0.0, ALU.mult, ALU.max))
        v(dve.tensor_tensor(R["t"], R["t"], R["y"], ALU.add))
        v(dve.memset(R["u"], 1.0))
        v(dve.tensor_tensor_scan(R["ncum"], R["u"], R["t"], 0.0, ALU.mult, ALU.add))
        ps = self.bank(3)
        wait(pe, self.c_dve.now(), self.c_act.now())
        for t, (c, n) in enumerate(TILES):
            for j in range(4):
                o = (4 * t + j) * H2
                tr = pe.transpose(ps[0:n, o:o + H2], self.lam[:, j, c:c + n], C["ident"][0:H2, 0:H2])
        wait(dve, self.T(tr))
        w = 4 * H2
        self.V(dve.tensor_copy(self.tok[0:META, 0:w], ps[0:META, 0:w]))
        v(dve.tensor_copy(self.tok[:, w:3 * w], ps[:, w:3 * w]))
        return R

    def token_scalar(self, t, j, h):
        o = (4 * t + j) * H2 + h
        return self.tok[0:TILES[t][1], o:o + 1]

    def feature_rms(self, x, width, total, eps, sq):
        pe, dve, act = self.pe, self.dve, self.act
        wait(act, *self.vector())
        wait(pe, self.A(act.activation(sq, x, ACT.Square)), *self.vector())
        rows, sums = self.lam[:, 9, 0:width], self.bank(7, width)[0:H2, :]
        for k in range(H2):
            mm = pe.matmul(sums, self.C["to_row"][:, k * H2:(k + 1) * H2], sq[:, k, :], start=(k == 0), stop=(k == H2 - 1))
        wait(dve, self.T(mm))
        wait(act, self.V(dve.tensor_scalar(rows, sums, 1.0 / total, eps, ALU.mult, ALU.add)))
        wait(act, self.A(act.activation(rows, rows, ACT.Ln)))
        wait(pe, self.A(act.activation(rows, rows, ACT.Exp, scale=-0.5)))
        for k in range(H2):
            mm = pe.matmul(self.bank(k, width), self.C["pick"][:, k * P:(k + 1) * P], rows, start=True, stop=True)
        wait(dve, self.T(mm))
        return self.psum[:, :].rearrange("p (b n) -> p b n", b=8)[:, :, 0:width]

    def mixer(self):
        with self.nc.sbuf_tensor("obT", [P, H2, S], F32) as self.obT, \
                self.nc.sbuf_tensor("oaT", [P, H2, S], F32) as self.oaT, \
                self.nc.sbuf_tensor("lam", [H2, 10, SM], F32) as self.lam:
            self.mixer_stages()

    def mixer_stages(self):
        nc, pe, dve, act, pool, C = self.nc, self.pe, self.dve, self.act, self.pool, self.C
        tiles = [(self.meta[:, :], META, 0)] + [(self.h[:, t, :], P, META + t * P) for t in range(NT)]
        self.norm_cols(tiles, C["g_mixer"])
        xs = [y[:, :, META:SM] for y in self.x]
        with nc.sbuf_tensor("tok", [P, 12 * H2], F32) as tok:
            self.tok = tok
            R = self.small_rows()
            with nc.sbuf_tensor("conv_out", [P, CONV_CH // P, SM], F32) as y:
                self.convolved(y)
                for group in range(2):
                    self.meet()
                    self.delta_group(group, y, R)
            self.meet()
            self.delta_gate(xs)
            self.meet()
            self.forgetting(R)
        self.meet()
        self.merge_branches(xs)

    def convolved(self, y):
        stack = ExitStack()
        nc, pe, dve, act, C = self.nc, self.pe, self.dve, self.act, self.C
        pad = CONV_K - 1
        w = C["conv"].rearrange("p (c k) -> p c k", k=CONV_K)
        with nc.sbuf_tensor("conv_in", [P, 2 * TURN, pad + SM], F32) as cin:
            self.V(dve.memset(cin[:, :, 0:pad], 0.0))

            def convolve(i, s, ps):
                moved = self.out_a.mark(act.activation(cin[:, 2 * s:2 * s + 2, pad:], ps, ACT.Copy))
                wait(dve, moved)
                done = {}
                for tap in range(CONV_K):
                    for j in (2 * s, 2 * s + 1):
                        x = cin[:, j, tap:tap + SM]
                        out = y[:, bass.ds(i * (2 * TURN) + j, 1), :].rearrange("p o n -> p (o n)")
                        wt = w[:, bass.ds(i * (2 * TURN) + j, 1), tap:tap + 1].rearrange("p o n -> p (o n)")
                        if tap == 0:
                            ins = dve.tensor_scalar(out, x, wt, None, ALU.mult)
                        else:
                            wait(dve, done[j])
                            ins = dve.scalar_tensor_tensor(out, x, wt, out, ALU.mult, ALU.add)
                        if tap < CONV_K - 1 or j % 2 == 0:
                            done[j] = self.V(ins)
                return ins, None

            wait(dve, self.c_dve.now())
            wait(pe, *self.vector(), *self.scalar())
            self.dense_cols(CONV_CH // COLS_W, self.x, SM, convolve, {self.c_dve: TURN * (2 * CONV_K - 1)})
        self.meet()
        for j in range(3):
            f = slice(j * H2, (j + 1) * H2)
            self.A(act.activation(y[:, f, :], y[:, f, :], ACT.Silu))
        wait(act, self.c_act.now())
        sq = stack.enter_context(nc.sbuf_tensor("conv_sq", [P, H2, SM], F32))
        for j, scale in ((0, DH ** -0.5), (1, 1.0)):
            x = y[:, j * H2:(j + 1) * H2, :]
            r = self.feature_rms(x, SM, 1.0, EPS, sq[:, :, :])
            wait(pe, self.V(dve.scalar_tensor_tensor(x, x, scale, r, ALU.mult, ALU.mult)))
        stack.close()

    def delta_group(self, group, conv, R):
        nc, pe, dve, act, pool, C = self.nc, self.pe, self.dve, self.act, self.pool, self.C
        HG = 4
        stack = ExitStack()

        def sb(name, shape):
            return stack.enter_context(nc.sbuf_tensor(f"{name}{group}", shape, F32))

        def four(ap, n=P):
            return ap.rearrange("p (h n) -> p h n", h=HG)[:, :, 0:n]

        kb = sb("dkb", [P, HG, SM])
        qe = sb("dqe", [P, HG, S])
        last_decay = sb("dlast", [P, HG, 3])
        q, k, v = (conv[:, j * H2 + group * HG:j * H2 + (group + 1) * HG, :] for j in range(3))
        gam = sb("dgam", [P, HG, SM])
        for name, out in (("beta", kb), ("eG", qe), ("G", gam)):
            wait(pe, self.c_dve.now())
            for hh in range(HG):
                h = group * HG + hh
                mm = pe.matmul(self.bank(hh, SM), C["pick"][0:H2, h * P:(h + 1) * P], R[name], start=True, stop=True)
            wait(dve, self.T(mm))
            rows = self.psum[:, 0:HG * BANK].rearrange("p (b n) -> p b n", b=HG)
            if name == "beta":
                self.V(dve.tensor_tensor(kb[:, :, :], k, rows[:, :, 0:SM], ALU.mult))
            elif name == "eG":
                self.V(dve.tensor_tensor(qe[:, :, :], q[:, :, META:SM], rows[:, :, META:SM], ALU.mult))
                for t, (c, n) in enumerate(TILES):
                    self.V(dve.tensor_copy(last_decay[:, :, t:t + 1], rows[:, :, c + n - 1:c + n]))
            else:
                for t, (c, n) in enumerate(TILES):
                    for hh in range(HG):
                        g = self.V(dve.tensor_scalar(gam[0:n, hh, c:c + n], self.bank(hh)[0:n, c:c + n],
                                                     self.token_scalar(t, 1, group * HG + hh), 0.0, ALU.subtract, ALU.min))
                wait(act, g)
                for c, n in TILES:
                    self.A(act.activation(gam[0:n, :, c:c + n], gam[0:n, :, c:c + n], ACT.Exp))
        self.meet()
        A, AT, B, T, TT, M1 = (sb(n, [P, 2, HG * P]) for n in ("dA", "dAT", "dB", "dT", "dTT", "dM"))
        small = {n: sb(n + "m", [META, HG * META]) for n in ("dA", "dAT", "dB", "dT", "dTT", "dM")}
        attn = sb("dattn", [P, 2, HG * P])
        ktail, bv = sb("dkt", [P, 3, HG * P]), sb("dbv", [P, 3, HG * P])

        def of(x, name, t):
            n = TILES[t][1]
            return (small[name][:, :] if t == 0 else x[:, t - 1, :]).rearrange("p (h n) -> p h n", h=HG)

        for t, (c, n) in enumerate(TILES):
            tile = slice(c, c + n)
            kk, qk, kt, vt = (self.bank(b)[0:n, :] for b in range(4))
            wait(pe, self.c_dve.now(), self.c_act.now())
            for hh in range(HG):
                pe.matmul(kk[:, hh * n:(hh + 1) * n], k[:, hh, tile], kb[:, hh, tile], start=True, stop=True)
                if t:
                    pe.matmul(qk[:, hh * n:(hh + 1) * n], k[:, hh, tile], q[:, hh, tile], start=True, stop=True)
                pe.transpose(kt[:, hh * P:(hh + 1) * P], k[:, hh, tile], C["ident"][:, :])
                mm = pe.transpose(vt[:, hh * P:(hh + 1) * P], v[:, hh, tile], C["ident"][:, :])
            done = self.T(mm)
            wait(act, done)
            for hh in range(HG):
                h, f = group * HG + hh, slice(hh * P, (hh + 1) * P)
                self.A(act.activation(ktail[0:n, t, f], kt[:, f], ACT.Copy, scale=self.token_scalar(t, 3, h)))
                self.A(act.activation(bv[0:n, t, f], vt[:, f], ACT.Copy, scale=self.token_scalar(t, 0, h)))
            wait(dve, done)
            at = of(AT, "dAT", t)
            earlier = C["earlier"][0:n, None, 0:n].to_broadcast([n, HG, n])
            wait(dve, self.V(dve.tensor_tensor(at, kk[:, 0:HG * n].rearrange("p (h n) -> p h n", h=HG), gam[0:n, :, tile], ALU.mult)))
            wait(pe, self.V(dve.tensor_tensor(at, at, earlier, ALU.mult)))
            if t:
                x = attn[:, t - 1, :].rearrange("p (h n) -> p h n", h=HG)
                wait(dve, self.V(dve.tensor_tensor(x, qk[:, :].rearrange("p (h n) -> p h n", h=HG), gam[0:n, :, tile], ALU.mult)))
                self.V(dve.tensor_tensor(x, x, C["not_later"][:, None, :].to_broadcast([P, HG, P]), ALU.mult))
            back = self.bank(4 + t)[0:n, :]
            for hh in range(HG):
                mm = pe.transpose(back[:, hh * n:(hh + 1) * n], at[:, hh, :], C["ident"][0:n, 0:n])
            wait(act, self.T(mm))
            self.A(act.activation(of(A, "dA", t), back[:, 0:HG * n].rearrange("p (h n) -> p h n", h=HG), ACT.Copy))
            eye = C["ident"][0:n, None, 0:n].to_broadcast([n, HG, n])
            self.V(dve.tensor_copy(of(T, "dT", t), eye))
            self.V(dve.tensor_copy(of(TT, "dTT", t), eye))
        self.meet()
        levels = {0: 4, 1: 7, 2: 7}
        upd = {}
        for lvl in range(7):
            act_t = [t for t in range(3) if lvl < levels[t]]
            for t in act_t:
                n = TILES[t][1]
                m = C["merge"][0:n, None, lvl * P:lvl * P + n].to_broadcast([n, HG, n])
                wait(pool, upd.get(("M", t)))
                upd["B", t] = self.G(pool.tensor_tensor(of(B, "dB", t), of(A, "dA", t), m, ALU.mult))
            for t in act_t:
                n = TILES[t][1]
                b, tt = of(B, "dB", t), of(TT, "dTT", t)
                ps = self.bank([6, 0, 3][t])[0:n, :]
                wait(pe, upd["B", t], upd.get(("T", t)))
                for hh in range(HG):
                    mm = pe.matmul(ps[:, hh * n:(hh + 1) * n], b[:, hh, :], tt[:, hh, :], start=True, stop=True)
                upd["M", t] = self.T(mm)
                wait(act, upd["M", t])
                upd["M1", t] = self.A(act.activation(of(M1, "dM", t), ps[:, 0:HG * n].rearrange("p (h n) -> p h n", h=HG), ACT.Copy))
            for t in act_t:
                n = TILES[t][1]
                last = lvl == levels[t] - 1
                m1, tm, tt = of(M1, "dM", t), of(T, "dT", t), of(TT, "dTT", t)
                pz, pzt = self.bank([7, 1, 4][t])[0:n, :], self.bank([7, 2, 5][t])[0:n, :]
                if t == 0:
                    pzt = pzt[:, HG * META:]
                wait(pe, upd["M1", t])
                for hh in range(HG):
                    if not last:
                        pe.matmul(pz[:, hh * n:(hh + 1) * n], m1[:, hh, :], tm[:, hh, :], start=True, stop=True)
                    mm = pe.matmul(pzt[:, hh * n:(hh + 1) * n], tm[:, hh, :], m1[:, hh, :], start=True, stop=True)
                wait(dve, self.T(mm))
                if not last:
                    self.V(dve.tensor_tensor(tm, tm, pz[:, 0:HG * n].rearrange("p (h n) -> p h n", h=HG), ALU.subtract))
                upd["T", t] = self.V(dve.tensor_tensor(tt, tt, pzt[:, 0:HG * n].rearrange("p (h n) -> p h n", h=HG), ALU.subtract))
        self.meet()
        St, rhs, vn = sb("dS", [P, HG * P]), sb("drhs", [P, HG * P]), sb("dvn", [P, HG * P])
        H = [slice(hh * P, (hh + 1) * P) for hh in range(HG)]
        for t, (c, n) in enumerate(TILES):
            tile, tt = slice(c, c + n), of(TT, "dTT", t)
            right = bv[0:n, t, :]
            if t:
                ks = self.bank(0)
                for hh in range(HG):
                    mm = pe.matmul(ks[:, H[hh]], k[:, hh, tile], St[:, H[hh]], start=True, stop=True)
                wait(dve, self.T(mm))
                for hh in range(HG):
                    x = self.V(dve.scalar_tensor_tensor(rhs[:, H[hh]], ks[:, H[hh]], self.token_scalar(t, 2, group * HG + hh),
                                                        bv[:, t, H[hh]], ALU.mult, ALU.add))
                wait(pe, x)
                right = rhs[:, :]
            pv = self.bank(1)[0:n, :]
            for hh in range(HG):
                mm = pe.matmul(pv[:, H[hh]], tt[:, hh, :], right[:, H[hh]], start=True, stop=True)
            wait(act, self.T(mm))
            wait(pe, self.A(act.activation(vn[0:n, :], pv, ACT.Copy)))
            ps = self.bank(2)
            for hh in range(HG):
                mm = pe.matmul(ps[:, H[hh]], ktail[0:n, t, H[hh]], vn[0:n, H[hh]], start=True, stop=True)
            s_done = self.T(mm)
            if t:
                po, xc = self.bank(3), slice(c - META, c - META + n)
                for hh in range(HG):
                    pe.matmul(po[:, H[hh]], St[:, H[hh]], qe[:, hh, xc], start=True, stop=False)
                    mm = pe.matmul(po[:, H[hh]], vn[:, H[hh]], attn[:, t - 1, H[hh]], start=False, stop=True)
                o_done = self.T(mm)
                wait(dve, o_done)
                self.V(dve.tensor_copy(self.oaT[:, group * HG:(group + 1) * HG, xc], po[:, :].rearrange("p (h n) -> p h n", h=HG)))
                for hh in range(HG):
                    x = self.V(dve.scalar_tensor_tensor(St[:, H[hh]], St[:, H[hh]], last_decay[:, hh, t:t + 1],
                                                        ps[:, H[hh]], ALU.mult, ALU.add))
            else:
                wait(dve, s_done)
                x = self.V(dve.tensor_copy(St[:, :], ps))
            wait(pe, x)
        stack.close()

    def delta_gate(self, xs):
        nc, dve, act = self.nc, self.dve, self.act
        with nc.sbuf_tensor("zT", [P, H2, S], F32) as z, nc.sbuf_tensor("zs", [P, H2, S], F32) as sq:
            self.dense_cols(4, xs, S, self.put(z))
            self.meet()
            silu = self.A(act.activation(z[:, :, :], z[:, :, :], ACT.Silu))
            oa, o_norm = self.oaT[:, :, :], self.C["o_norm"]
            r = self.feature_rms(oa, S, DH, EPS, sq[:, :, :])
            wait(dve, self.V(dve.scalar_tensor_tensor(oa, oa, o_norm, r, ALU.mult, ALU.mult)), silu)
            self.V(dve.tensor_tensor(oa, oa, z[:, :, :], ALU.mult))
            self.meet()

    def forgetting(self, R):
        nc, pe, dve, act, pool, C = self.nc, self.pe, self.dve, self.act, self.pool, self.C
        with ExitStack() as stack:
            def sb(name, shape):
                return stack.enter_context(nc.sbuf_tensor(name, shape, F32))
            qkv = sb("fa_qkv", [P, 3 * H2, SM])
            vb = sb("fa_v", [P, 3, H2 * P])
            sq = sb("fa_sq", [P, H2, SM])

            self.dense_cols(3 * H2 * P // COLS_W, self.x, SM, self.put(qkv))
            self.meet()
            ws = self.stat[:, 0:1]
            self.V(dve.tensor_scalar(ws, C["q_norm"][:, 0:1], DH ** -0.5, None, ALU.mult))
            for j, gain in ((0, ws), (1, C["k_norm"][:, 0:1])):
                x = qkv[:, j * H2:(j + 1) * H2, :]
                r = self.feature_rms(x, SM, DH, EPS, sq[:, :, :])
                wait(pe, self.V(dve.scalar_tensor_tensor(x, x, gain, r, ALU.mult, ALU.mult)))
            q, k, v = (qkv[:, j * H2:(j + 1) * H2, :] for j in range(3))
            self.meet()
            moved = {}
            j = 0
            for t, (c, n) in enumerate(TILES):
                for half in range(2):
                    ps = self.bank(j)[0:n, :]
                    for hh in range(4):
                        tr = pe.transpose(ps[:, hh * P:(hh + 1) * P], v[:, 4 * half + hh, c:c + n], C["ident"][:, :])
                    tr = self.T(tr)
                    wait(act, tr)
                    self.A(act.activation(vb[0:n, t, half * 512:half * 512 + 512], ps, ACT.Copy))
                    j += 1
            wait(pe, self.c_act.now())
            m = {}
            xs = [sb(f"fa_x{b}", [P, SM]) for b in range(4)]
            pT = [sb(f"fa_p{b}", [P, 3, P]) for b in range(2)]
            st = sb("fa_stat", [P, 16, 4])
            units = [(h, t) for h in range(H2) for t in range(NT)]

            def scores(u):
                h, t = units[u]
                w = META + P * (t + 1)
                ps = self.bank(u % 4, w)
                wait(pe, m.get(("x", u - 4)))
                pe.matmul(ps, q[:, h, META + t * P:META + (t + 1) * P], k[:, h, 0:w], start=True, stop=False)
                m["z", u] = self.T(pe.matmul(ps, C["pick"][0:H2, h * P:(h + 1) * P], R["ncum"][:, 0:w], start=False, stop=True))

            def exponent(u):
                w = META + P * (units[u][1] + 1)
                ps = self.bank(u % 4, w)
                x = xs[u % 4][:, 0:w]
                wait(dve, m["z", u], m.get(("tr", u - 4)))
                m["x", u] = self.V(dve.tensor_tensor(x, ps, C["causal"][:, SM - w:SM], ALU.add))
                wait(dve, m["x", u])
                mx = self.V(dve.tensor_reduce(st[:, u, 0:1], x, AX, ALU.max, negate=True))
                wait(act, mx)
                m["e", u] = self.A(act.activation(x, x, ACT.Exp, bias=st[:, u, 0:1], accum_out=st[:, u, 1:2]))

            def normalise(u):
                h, t = units[u]
                w = META + P * (t + 1)
                x = xs[u % 4][:, 0:w]
                wait(dve, m["e", u])
                wait(dve, self.V(dve.reciprocal(st[:, u, 2:3], st[:, u, 1:2])))
                n_ = self.V(dve.tensor_scalar(x, x, st[:, u, 2:3], None, ALU.mult))
                ps = self.bank(4 + u % 2)
                wait(pe, n_, m.get(("pT", u - 2)))
                for j in range(t + 2):
                    c, n = TILES[j]
                    tr = pe.transpose(ps[0:n, j * P:(j + 1) * P], x[:, c:c + n], C["ident"][:, :])
                m["tr", u] = self.T(tr)

            def values(u):
                h, t = units[u]
                ps = self.bank(4 + u % 2)
                p = pT[u % 2]
                wait(act, m["tr", u], m.get(("o", u - 2)))
                self.A(act.activation(p[0:META, 0, :], ps[0:META, 0:P], ACT.Copy))
                m["pT", u] = self.A(act.activation(p[:, 1:t + 2, :], ps[:, P:(t + 2) * P].rearrange("p (a b) -> p a b", b=P), ACT.Copy))
                po = self.bank(6 + u % 2, P)
                wait(pe, m["pT", u], m.get(("ob", u - 2)))
                for j in range(t + 2):
                    n = TILES[j][1]
                    mm = pe.matmul(po, vb[0:n, j, h * P:(h + 1) * P], p[0:n, j, :], start=(j == 0), stop=(j == t + 1))
                m["o", u] = self.T(mm)
                wait(dve, m["o", u])
                m["ob", u] = self.V(dve.tensor_copy(self.obT[:, h, t * P:(t + 1) * P], po))

            for u in range(len(units) + 3):
                for stage, x in ((scores, u), (normalise, u - 2), (values, u - 3), (exponent, u - 1)):
                    if 0 <= x < len(units):
                        stage(x)
            self.meet()

    def merge_branches(self, xs):
        nc, dve, act = self.nc, self.dve, self.act
        with ExitStack() as stack:
            gates, y = (stack.enter_context(nc.sbuf_tensor(n, [P, 2 * KD, S], F32)) for n in ("gates", "branch_y"))
            pairs = [[stack.enter_context(nc.sbuf_tensor(f"branch_{n}{b}", [P, KD, S], F32R)) for n in ("hi", "lo")]
                     for b in range(2)]
            for o, pair in zip((self.oaT, self.obT), pairs):
                self.split(o[:, :, :], [x[:, :, :] for x in pair])
            self.dense_cols(8, xs, S, self.put(gates))
            self.meet()
            sig = self.A(act.activation(gates[:, :, :], gates[:, :, :], ACT.Sigmoid))
            for b, pair in enumerate(pairs):
                self.dense_cols(4, pair, S, self.put(y[:, b * KD:(b + 1) * KD, :]))
                wait(dve, sig, *self.scalar(), *self.vector())
                self.V(dve.tensor_tensor(y[:, b * KD:(b + 1) * KD, :], y[:, b * KD:(b + 1) * KD, :],
                                         gates[:, b * KD:(b + 1) * KD, :], ALU.mult))
            wait(dve, self.c_dve.now())
            wait(act, self.V(dve.tensor_tensor(y[:, 0:KD, :], y[:, 0:KD, :], y[:, KD:, :], ALU.add)))
            wait(dve, self.c_dve.now())
            self.split(y[:, 0:KD, :], [x[:, :, :] for x in pairs[0]])
            self.meet()
            self.dense_rows(KD, 2, pairs[0], lambda i, u, t, ps: self.add_to_h(i, u, t, ps, 2))
            self.meet()

    def experts(self):
        nc, pe, dve, act, pool, C = self.nc, self.pe, self.dve, self.act, self.pool, self.C
        NU = 8
        late = Counter(nc.alloc_semaphore("expert_constants_landed"), 16)
        self.meet()
        self.load_constants("peer", act, late)
        g_peer, keys = C["g_peer"], C["keys"]
        xb = self.sb("tokens", [P, NT, D])
        wait(dve, self.rms_scale([(ap, n) for ap, n, _ in self.h_tiles()]), late.now())
        for t in range(NT):
            x = self.V(dve.scalar_tensor_tensor(xb[:, t, :], self.h[:, t, :], self.rstd[:, t:t + 1], g_peer, ALU.mult, ALU.mult))
        wait(pe, x)
        self.turn_cols(self.h_tiles(), [xb[:, t, :] for t in range(NT)], KD, self.x)
        sc = self.sb("key_scores", [P, NT, 2 * PEER_H * KEYS])
        with nc.sbuf_tensor("queries", [P, 2 * PEER_H, S], F32) as qh:
            self.dense_cols(8, self.x, S, self.put(qh), final=True)
            self.meet()
            wait(pe, late.now())
            for t in range(NT):
                for b in range(4):
                    ps = self.bank(4 * t + b)
                    for j in range(4):
                        c = 4 * b + j
                        mm = pe.matmul(ps[:, j * KEYS:(j + 1) * KEYS], qh[:, c, t * P:(t + 1) * P],
                                       keys[:, c * KEYS:(c + 1) * KEYS], start=True, stop=True)
                    mm = self.T(mm)
                    wait(dve, mm)
                    self.V(dve.tensor_copy(sc[:, t, b * BANK:(b + 1) * BANK], ps))
            self.meet()
        for t in range(NT):
            for half in range(2):
                mm = pe.matmul(self.bank(2 * t + half), C["ident"][:, :], self.h[:, t, half * BANK:(half + 1) * BANK],
                               start=True, stop=False, skip_group_check=True)
        self.T(mm)

        u_rows = [self.sb(f"u_rows{j}", [P, D]) for j in range(NU)]
        v_rows = [self.sb(f"v_rows{j}", [P, D]) for j in range(NU)]
        u_in = [nc.alloc_semaphore(f"u_landed{j}") for j in range(NU)]
        v_in = [nc.alloc_semaphore(f"v_landed{j}") for j in range(NU)]
        dots, added = Counter(nc.alloc_semaphore("dots_done")), Counter(nc.alloc_semaphore("rows_added"))
        w = self.sb("pick_from", [P, 2 * KEYS])
        w2 = self.sb("pick_rest", [P, 2 * KEYS])
        best = self.sb("best", [P, 2, TOPK])
        where = self.sb("where", [P, 2, TOPK], U32)
        wheref = self.sb("wheref", [P, 2, TOPK])
        top = [self.sb(f"top{t}", [P, TOPK]) for t in range(NT)]
        ci = self.sb("ci", [P, TOPK], U32)
        part = self.sb("part", [P, 2, TOPK], U32)
        partf = self.sb("partf", [P, 2, TOPK])
        hot = self.sb("hot", [P, 2, TOPK, TOPK])
        half_index = self.sb("half_index", [P, 2, TOPK])
        index = [self.sb(f"index{t}", [P, TOPK], I32) for t in range(NT)]
        gate = [self.sb(f"gate{t}", [P, TOPK]) for t in range(NT)]
        soft = self.sb("soft", [P, NT, 4])
        act_in = [self.sb(f"act_in{t}", [P, TOPK]) for t in range(NT)]
        coef = [self.sb(f"coef{t}", [P, TOPK]) for t in range(NT)]
        diag = self.sb("diag", [P, TOPK, P])
        for j in range(NU):
            dots.mark(dve.memset(w[:, j:j + 1], 0.0))
        for j in range(TOPK):
            added.mark(dve.memset(w[:, NU + j:NU + j + 1], 0.0))
        wait(dve, dots.now(), added.now())

        def v(ins):
            m = self.V(ins)
            wait(dve, m)
            return m

        def apart(engine):
            engine.nop(nofuse=True)

        after_index = [0] * NT

        def top16(values, rest, val, idx):
            apart(dve)
            v(dve.max(val[:, 0:8], values))
            apart(dve)
            self.V(dve.max_index(idx[:, 0:8], val[:, 0:8], values))
            v(dve.match_replace(rest, val[:, 0:8], values, NEG))
            apart(dve)
            v(dve.max(val[:, 8:16], rest))
            apart(dve)
            v(dve.max_index(idx[:, 8:16], val[:, 8:16], rest))

        def choose(i, t, free):
            v(dve.tensor_copy(w[:, :], sc[:, t, bass.ds(i * (2 * KEYS), 2 * KEYS)]))
            for j in range(2):
                f = slice(j * KEYS, (j + 1) * KEYS)
                top16(w[:, f], w2[:, f], best[:, j, :], where[:, j, :])
            v(dve.tensor_copy(wheref[:, :, :], where[:, :, :]))
            v(dve.tensor_tensor(w[:, :].rearrange("p (a b) -> p a b", a=TOPK), best[:, 0, :, None].to_broadcast([P, TOPK, TOPK]),
                                best[:, 1, None, :].to_broadcast([P, TOPK, TOPK]), ALU.add))
            top16(w[:, :], w2[:, :], top[t], ci)
            self.V(dve.tensor_scalar(part[:, 0, :], ci[:, :], 4, None, ALU.logical_shift_right))
            v(dve.tensor_scalar(part[:, 1, :], ci[:, :], TOPK - 1, None, ALU.bitwise_and))
            v(dve.tensor_copy(partf[:, :, :], part[:, :, :]))
            for j in range(2):
                v(dve.tensor_tensor(hot[:, j], C["iota"][:, None, :].to_broadcast([P, TOPK, TOPK]),
                                    partf[:, j, :, None].to_broadcast([P, TOPK, TOPK]), ALU.is_equal))
                v(dve.tensor_tensor(hot[:, j], hot[:, j], wheref[:, j, None, :].to_broadcast([P, TOPK, TOPK]), ALU.mult))
            v(dve.tensor_reduce(half_index[:, :, :], hot[:, :, :, :], AX, ALU.add))
            for sem, value in free:
                dve.wait_ge(sem, value)
            v(dve.scalar_tensor_tensor(index[t][:, :], half_index[:, 0, :], float(KEYS), half_index[:, 1, :], ALU.mult, ALU.add))
            after_index[t] = self.c_dve.value
            m = v(dve.tensor_scalar(soft[:, t, 0:1], top[t][:, 0:1], -1.0, None, ALU.mult))
            wait(act, m)
            m = self.A(act.activation(gate[t][:, :], top[t][:, :], ACT.Exp, bias=soft[:, t, 0:1], accum_out=soft[:, t, 1:2]))
            wait(dve, m)
            v(dve.reciprocal(soft[:, t, 2:3], soft[:, t, 1:2]))
            return v(dve.tensor_scalar(gate[t][:, :], gate[t][:, :], soft[:, t, 2:3], None, ALU.mult))

        def row_landed(i, t, k):
            return i * (NT * TOPK // NU * 16) + (t * (TOPK // NU) + k // NU + 1) * 16

        def read_before(c, base, i, t, k, back):
            return i * (NT * TOPK) + (base + t * TOPK + k + 1 - back)

        def unit(i, t, ready, following):
            wait(pool, ready)
            for rows, sems, counter, base, table in (
                    (u_rows, u_in, dots, NU, self.ins["expert_u"]), (v_rows, v_in, added, TOPK, self.ins["expert_v"])):
                for k in range(TOPK):
                    pool.wait_ge(counter.sem, read_before(counter, base, i, t, k, NU))
                    apart(pool)
                    pool.indirect_dma_start(rows[k % NU][:, :], None, table,
                                            bass.IndirectOffsetOnAxis(ap=index[t][:, k:k + 1], axis=0)).then_inc(sems[k % NU], 16)
            for k in range(TOPK):
                dve.wait_ge(u_in[k % NU], row_landed(i, t, k))
                dots.mark(dve.tensor_tensor_reduce(u_rows[k % NU][:, :], u_rows[k % NU][:, :], xb[:, t, :], 1.0, 0.0,
                                                   ALU.mult, ALU.add, act_in[t][:, k:k + 1]))
            wait(act, dots.now())
            m = self.A(act.activation(coef[t][:, :], act_in[t][:, :], ACT.Gelu))
            wait(dve, m)
            m = self.V(dve.tensor_tensor(coef[t][:, :], coef[t][:, :], gate[t][:, :], ALU.mult))
            wait(act, m)
            wait(dve, m)
            for k in range(TOPK):
                act.wait_ge(added.sem, read_before(added, TOPK, i, t, k, TOPK))
                d = self.A(act.activation(diag[:, k, :], C["ident"][:, :], ACT.Copy, scale=coef[t][:, k:k + 1]))
                wait(pe, d)
                pe.wait_ge(v_in[k % NU], row_landed(i, t, k))
                for half in range(2):
                    mm = pe.matmul(self.bank(2 * t + half), diag[:, k, :], v_rows[k % NU][:, half * BANK:(half + 1) * BANK],
                                   start=False, stop=False, skip_group_check=True)
                added.mark(mm)
            if following:
                free = [(v_in[j], row_landed(i, t, TOPK - NU + j)) for j in range(NU)]
                return choose(i + 1, t, free)

        for t in range(NT):
            choose(0, t, [])
        back = [self.c_dve.value - x for t, x in enumerate(after_index)]
        per = self.unit_counts(dots, added)

        def units(i, following):
            start, turn = self.c_dve.value, self.c_dve.loop
            for t in range(NT):
                unit(i, t, Mark(self.c_dve, start - back[t], turn), following)

        with loop(nc, PEER_H - 1, [ENG.PE, ENG.DVE, ENG.Activation, ENG.Pool], per) as i:
            units(i, True)
        units(PEER_H - 1, False)
        wait(dve, added.now())
        for t in range(NT):
            for half in range(2):
                self.V(dve.tensor_copy(self.h[:, t, half * BANK:(half + 1) * BANK], self.bank(2 * t + half)))

    def unit_counts(self, dots, added):
        return {dots: NT * TOPK, added: NT * TOPK, self.c_dve: 31 * NT, self.c_act: 18 * NT}

    def debug_out(self):
        self.meet()
        wait(self.sp, *self.everything())
        self.store()

    def store(self):
        done = Counter(self.nc.alloc_semaphore("stored"), 16)
        for t in range(NT):
            last = done.mark(self.sp.dma_start(self.out.rearrange("o (t p) d -> t p (o d)", p=P)[t], self.h[:, t, :]))
        wait(self.sp, last)

    def build(self):
        self.setup()
        steps = [self.stick_breaking, lambda: self.mlp(self.C["g_mlp0"], "0"), self.retention,
                 lambda: self.mlp(self.C["g_mlp1"], "1"), self.final_norm, self.mixer, self.experts]
        for n, s in enumerate(steps):
            s()
            if self.stop == n + 1:
                break
        self.debug_out()


def program(nc, ins, out, where, stop=None):
    with nc.allow_non_contiguous_dma(reason="layouts"):
        Program(nc, ins, out, where, stop).build()


def host_arrays(a):
    weights, small = weight_stream(a)
    arrays = {"x": a["x"], "meta": a["meta_tokens_2"], "expert_u": a["expert_u_2"][0],
              "expert_v": a["expert_v_2"][0], "weights": weights}
    every = {**shape_constants(), **vectors(a), "small": small}
    groups = {"first": FIRST_BLOCK, "peer": PEER_ONLY}
    groups["always"] = [n for n in every if n not in FIRST_BLOCK and n not in PEER_ONLY]
    where = {}
    for group, names in groups.items():
        arrays["constants_" + group], where[group] = pack({n: every[n] for n in names})
    return {name: np.ascontiguousarray(v) for name, v in arrays.items()}, where


def kernel(**inputs):
    import concourse.bacc as bacc
    from concourse.bass_utils import run_bass_kernel_spmd

    arrays, where = host_arrays({k: np.asarray(v) for k, v in inputs.items()})
    nc = bacc.Bacc("TRN2", target_bir_lowering=False, num_devices=1)
    ins = {name: nc.dram_tensor(name, v.shape, mybir.dt.from_np(v.dtype), kind="ExternalInput").ap()
           for name, v in arrays.items()}
    out = nc.dram_tensor("out", (1, S, D), F32, kind="ExternalOutput").ap()
    program(nc, ins, out, where)
    r = run_bass_kernel_spmd(nc, [arrays], core_ids=[0])
    return r.results[0]["out"]
```

```python
from contextlib import ExitStack, contextmanager

import numpy as np

import concourse.bass as bass
from concourse import mybir

F32 = mybir.dt.float32
F32R = mybir.dt.float32r
I32 = mybir.dt.int32
U32 = mybir.dt.uint32
ALU = mybir.AluOpType
ACT = mybir.ActivationFunctionType
AX = mybir.AxisListType.X
ENG = mybir.EngineType

P = 128
D = 1024
KD = D // P
S = 256
NT = S // P
META = 16
SM = META + S
HID = 4096
SB_H, SB_D = 16, 64
RET_H, RET_QK, RET_V = 4, 256, 512
H2, DH = 8, 128
CONV_K = 4
CONV_CH = 3 * H2 * DH
KEYS, TOPK, PEER_H = 128, 16, 8
EPS = 1e-6
BANK = 512
BLK = 2048
TURN = 4
SLOTS = 2
PARTS = 2
NEG = -1.0e30
COLS_W = BLK // KD
ROWS_K = BLK // BANK
TILES = [(0, META), (META, P), (META + P, P)]


FIRST_BLOCK = ("sb_keep", "sb_cap", "cos", "sin", "decay", "g_final")
PEER_ONLY = ("g_peer", "keys")


def cols_blocks(w):
    k, n = w.shape
    return w.reshape(KD, P, n // COLS_W, COLS_W).transpose(2, 1, 0, 3).reshape(-1, P, BLK)


def rows_blocks(w):
    k, n = w.shape
    w = w.reshape(k // (ROWS_K * P), ROWS_K, P, n // BANK, BANK)
    return w.transpose(3, 0, 2, 1, 4).reshape(-1, P, BLK)


def per_partition(v):
    return v.reshape(-1, P).T


def weight_stream(a):
    w_in = a["w_in_2"][0]
    at = np.cumsum([0, CONV_CH, D, H2, H2, CONV_CH, H2, 2 * D])
    sb, ret = a["w_sb_in"][0], a["w_ret_in"][0]
    parts = [
        cols_blocks(sb[:, :2 * D]), rows_blocks(sb[:, 2 * D:]), rows_blocks(a["w_sb_out"][0]),
        cols_blocks(a["w_mlp_up"][0]), rows_blocks(a["w_mlp_down"][0]),
        cols_blocks(ret[:, :2 * D]), rows_blocks(ret[:, 2 * D:]), rows_blocks(a["w_ret_out"][0]),
        cols_blocks(a["w_mlp_up"][1]), rows_blocks(a["w_mlp_down"][1]),
        cols_blocks(w_in[:, at[0]:at[1]]), cols_blocks(w_in[:, at[1]:at[2]]),
        cols_blocks(w_in[:, at[4]:at[5]]), cols_blocks(w_in[:, at[6]:at[7]]),
        cols_blocks(a["w_branch_2"][0, 0]), cols_blocks(a["w_branch_2"][0, 1]),
        rows_blocks(a["w_out_2"][0]), cols_blocks(a["peer_wq_2"][0]),
    ]
    small = np.concatenate([w_in[:, at[2]:at[4]], w_in[:, at[5]:at[6]]], axis=1)
    small = small.reshape(KD, P, 3 * H2).transpose(1, 0, 2).reshape(P, -1)
    return np.concatenate(parts), small


def pack(arrays):
    where, at = {}, 0
    for name, v in arrays.items():
        where[name] = (v.shape[0], at, v.shape[1])
        at += v.shape[1]
    return np.concatenate([np.pad(v, ((0, P - v.shape[0]), (0, 0))) for v in arrays.values()], 1), where


def shape_constants():
    p, f = np.arange(P)[:, None], np.arange(P)[None, :]
    c = {}
    c["ident"] = (p == f)
    c["ones"] = np.ones((P, P))
    c["from_here"] = (p >= f)
    before = (p < f)
    c["sb_keep"] = np.concatenate([before, np.ones((P, P)), before], 1)
    c["sb_cap"] = np.where(c["sb_keep"] > 0, 0.0, NEG)
    inv = (1.0 / (np.float32(10000.0) ** np.linspace(0, 1, P, dtype=np.float32))).astype(np.float32)
    ang = (np.arange(S, dtype=np.float32)[None, :] * inv[:, None]).astype(np.float32)
    c["cos"], c["sin"] = np.cos(ang), np.sin(ang)
    lg = np.log1p(-np.exp2(-5.0 - np.arange(RET_H)))
    rel = np.concatenate([f - p, f + P - p, f - p], 1).astype(np.float64)
    c["decay"] = np.concatenate([np.where(rel >= 0, np.exp(g * np.maximum(rel, 0)), 0) for g in lg], 1)
    c["earlier"] = (p < f)
    c["not_later"] = (p <= f)
    c["merge"] = np.concatenate([((p >> l) == (f >> l) + 1) & ((p >> l) % 2 == 1)
                                 for l in range(7)], 1)
    c["next"] = (p % 2 == 0) & (f == p + 1)
    c["causal"] = np.concatenate([np.zeros((P, SM - P)), np.where(f <= p, 0.0, NEG)], 1)
    head = np.zeros((P, H2 * P))
    for h in range(H2):
        head[h, h * P:(h + 1) * P] = 1.0
    c["to_row"] = np.broadcast_to(np.eye(H2).reshape(1, -1), (P, H2 * H2))
    c["pick"] = head[:H2]
    c["iota"] = np.broadcast_to(np.arange(TOPK), (P, TOPK))
    return {k: np.ascontiguousarray(v, dtype=np.float32) for k, v in c.items()}


def vectors(a):
    conv = a["conv_w_2"][0].reshape(CONV_K, CONV_CH // P, P).transpose(2, 1, 0).reshape(P, -1)
    v = {
        "g_mix0": per_partition(a["g_mix"][0]), "g_mix1": per_partition(a["g_mix"][1]),
        "g_mlp0": per_partition(a["g_mlp"][0]), "g_mlp1": per_partition(a["g_mlp"][1]),
        "g_mixer": per_partition(a["norm_mix_2"][0]), "conv": conv,
        "o_norm": a["o_norm_a_2"][0][:, None], "q_norm": a["q_norm_b_2"][0][:, None],
        "k_norm": a["k_norm_b_2"][0][:, None],
    }
    for n in ("a_log", "dt_bias", "f_bias"):
        v[n] = a[n + "_2"][0][:, None]
    rows = {"g_final": a["g_final"], "g_peer": a["norm_ffn_2"][0]}
    v.update({k: np.broadcast_to(x, (P, D)) for k, x in rows.items()})
    v["keys"] = a["peer_sub_keys_2"][0].transpose(3, 1, 0, 2).reshape(P, -1)
    return {k: np.ascontiguousarray(x) for k, x in v.items()}


class Mark:

    def __init__(self, counter, value, loop=None):
        self.counter, self.value, self.loop = counter, value, loop

    def at(self):
        if self.loop is None:
            return self.value
        i, per = self.loop
        return i * per[self.counter] + self.value

    def back(self, turns=1):
        value = self.value - turns * self.loop[1][self.counter]
        assert value >= 1, "a wait needs a positive value"
        return Mark(self.counter, value, self.loop)


class Counter:

    def __init__(self, sem, step=1):
        self.sem, self.step, self.value, self.loop = sem, step, 0, None

    def mark(self, ins):
        ins.then_inc(self.sem, self.step)
        self.value += self.step
        return Mark(self, self.value, self.loop)

    def now(self):
        return Mark(self, self.value, self.loop)


@contextmanager
def loop(nc, turns, engines, per):
    entry = {c: c.value for c in per}
    with nc.Fori(0, turns, engines=engines) as i:
        for c in per:
            c.loop = (i, per)
        yield i
        for c in per:
            assert c.value - entry[c] == per[c], (c.sem, c.value - entry[c], per[c])
    for c in per:
        c.value, c.loop = entry[c] + turns * per[c], None


def wait(engine, *marks):
    best = {}
    for m in marks:
        if m is None:
            continue
        o = best.get(m.counter)
        if o is None or o.loop is not m.loop and m.loop is not None or o.loop is m.loop and m.value > o.value:
            best[m.counter] = m
    for m in best.values():
        if m.loop is not None or m.value > 0:
            engine.wait_ge(m.counter.sem, m.at())


class Program:
    def __init__(self, nc, ins, out, where):
        self.nc, self.ins, self.out, self.where = nc, ins, out, where
        self.pe, self.dve, self.act, self.pool, self.sp = nc.tensor, nc.vector, nc.scalar, nc.gpsimd, nc.sync
        self.c_pe = Counter(nc.alloc_semaphore("tensor_done"))
        self.c_dve = Counter(nc.alloc_semaphore("vector_done"))
        self.c_act = Counter(nc.alloc_semaphore("scalar_done"))
        self.c_pool = Counter(nc.alloc_semaphore("gpsimd_done"))
        self.out_v = Counter(nc.alloc_semaphore("vector_moved"))
        self.out_a = Counter(nc.alloc_semaphore("scalar_moved"))
        self.blocks = Counter(nc.alloc_semaphore("blocks_read"))
        self.hi_made = Counter(nc.alloc_semaphore("block_hi_made"))
        self.lo_made = Counter(nc.alloc_semaphore("block_lo_made"))
        self.block_full = [nc.alloc_semaphore(f"block_full{s}") for s in range(SLOTS)]
        self.n_block = 0
        self.first_block = ExitStack()

    def sb(self, name, shape, dt=F32):
        return self.nc.alloc_sbuf_tensor(name, shape, dt)

    def V(self, ins): return self.c_dve.mark(ins)
    def A(self, ins): return self.c_act.mark(ins)
    def G(self, ins): return self.c_pool.mark(ins)
    def T(self, ins): return self.c_pe.mark(ins)

    def everything(self):
        return [c.now() for c in (self.c_pe, self.c_dve, self.c_act, self.c_pool, self.blocks, self.out_v, self.out_a)]

    def vector(self):
        return self.c_dve.now(), self.out_v.now()

    def scalar(self):
        return self.c_act.now(), self.out_a.now()

    def meet(self):
        all_marks = self.everything()
        for e in (self.pe, self.dve, self.act, self.pool):
            wait(e, *all_marks)

    def bank(self, b, width=BANK):
        return self.psum[:, b * BANK:b * BANK + width]

    def split_block(self, i, per_turn, b):
        s, n = b % SLOTS, BLK // PARTS
        raw, hi, lo = self.raw[s], self.w_hi[s], self.w_lo[s]
        self.act.wait_ge(self.block_full[s], i * (16 * per_turn // SLOTS) + 16 * (b // SLOTS + 1))
        for p in range(PARTS):
            f = slice(p * n, (p + 1) * n)
            made = self.hi_made.mark(self.act.activation(hi[:, f], raw[:, f], ACT.Copy))
            wait(self.dve, made)
            self.lo_made.mark(self.dve.tensor_tensor(lo[:, f], raw[:, f], hi[:, f], ALU.subtract))

    def block_split(self, i, per_turn, b, k_pieces):
        self.pe.wait_ge(self.lo_made.sem, i * (PARTS * per_turn) + PARTS * (b + 1))
        return [w[b % SLOTS][:, :].rearrange("p (k n) -> p k n", k=k_pieces) for w in (self.w_hi, self.w_lo)]

    def split(self, x, pair):
        hi, lo = pair
        wait(self.dve, self.A(self.act.activation(hi, x, ACT.Copy)))
        return self.V(self.dve.tensor_tensor(lo, x, hi, ALU.subtract))

    def product(self, out, w, x, first, last):
        (wh, wl), (xh, xl) = w, x
        self.pe.matmul(out, wh, xh, start=first, stop=False)
        self.pe.matmul(out, wh, xl, start=False, stop=False)
        return self.pe.matmul(out, wl, xh, start=False, stop=last)

    def dense_cols(self, n_blocks, x, width, evac, counts=None, final=False, upper_banks=()):
        nc, pe = self.nc, self.pe
        assert self.n_block % TURN == 0 and n_blocks % TURN == 0
        first, turns = self.n_block, n_blocks // TURN
        xh, xl = x

        def turn(i, ahead):
            v0, a0 = self.out_v.value, self.out_a.value
            for s in range(TURN):
                w = self.block_split(i, TURN, first + s, KD)
                if s == TURN // 2:
                    wait(pe, *upper_banks)
                wait(pe, Mark(self.out_v, v0 + s + 1 - TURN, self.out_v.loop),
                     Mark(self.out_a, a0 + s + 1 - TURN, self.out_a.loop))
                for sub in range(2):
                    f = slice(sub * P, (sub + 1) * P)
                    for k in range(KD):
                        mm = self.product(self.bank(2 * s + sub, width), [y[:, k, f] for y in w],
                                          (xh[:, k, 0:width], xl[:, k, 0:width]), k == 0, k == KD - 1)
                read = self.blocks.mark(mm)
                wait(self.dve, read)
                wait(self.act, read)
                if s < ahead:
                    self.split_block(i, TURN, first + s + SLOTS)
                ps = self.psum[:, 2 * s * BANK:(2 * s + 2) * BANK].rearrange("p (b n) -> p b n", b=2)[:, :, 0:width]
                v, a = evac(i, s, ps)
                for counter, ins in ((self.out_v, v), (self.out_a, a)):
                    if ins is not None:
                        counter.mark(ins)

        per = {self.blocks: TURN, self.out_v: TURN, self.out_a: TURN,
               self.hi_made: PARTS * TURN, self.lo_made: PARTS * TURN, **(counts or {})}
        with loop(nc, turns - final, [ENG.PE, ENG.DVE, ENG.Activation], per) as i:
            turn(i, TURN)
        if final:
            turn(turns - 1, TURN - SLOTS)
        self.n_block += n_blocks

    def dense_rows(self, n_k, halves, x, evac, x_after=None):
        nc, pe = self.nc, self.pe
        if x_after is None:
            wait(pe, self.out_a.now(), self.out_v.now())
        per_half = n_k // ROWS_K
        unroll = max(1, TURN // per_half)
        per_turn = per_half * unroll
        assert self.n_block % SLOTS == 0 and per_turn % SLOTS == 0 and halves % unroll == 0
        first, n_out = self.n_block, unroll * NT
        per = {self.blocks: per_turn, self.out_v: n_out, self.c_pe: unroll, self.hi_made: PARTS * per_turn, self.lo_made: PARTS * per_turn}
        with loop(nc, halves // unroll, [ENG.PE, ENG.DVE, ENG.Activation], per) as i:
            base = self.out_v.value
            for u in range(unroll):
                for kb in range(per_half):
                    b = u * per_half + kb
                    w = self.block_split(i, per_turn, first + b, ROWS_K)
                    if kb == per_half - 1 and x_after:
                        wait(pe, *x_after)
                    for t in range(NT):
                        if kb == 0:
                            wait(pe, Mark(self.out_v, base + u * NT + t + 1 - n_out, self.out_v.loop))
                        for k in range(ROWS_K):
                            kk = kb * ROWS_K + k
                            mm = self.product(self.bank(u * NT + t), [y[:, kk, t * P:(t + 1) * P] for y in x],
                                              [y[:, k, :] for y in w], kk == 0, kk == n_k - 1)
                        if kb == per_half - 1 and t == 0:
                            tile0 = self.T(mm)
                    read = self.blocks.mark(mm)
                    if kb == per_half - 1:
                        for t in range(NT):
                            wait(self.dve, read if t else tile0)
                            self.out_v.mark(evac(i, u, t, self.bank(u * NT + t)))
                    wait(self.dve, read)
                    wait(self.act, read)
                    self.split_block(i, per_turn, first + b + SLOTS)
        self.n_block += per_half * halves

    def inverse_root(self, out, x):
        power = self.power[0:x.shape[0], :].to_broadcast(list(x.shape))
        return self.G(self.pool.tensor_tensor(out, x, power, ALU.pow))

    def rms_scale(self, tiles):
        r, marks = self.stat, []
        for j, (ap, n) in enumerate(tiles):
            squares = self.psum[0:n, j * D:(j + 1) * D]
            if j % 2 == 0:
                sq = self.V(self.dve.tensor_tensor_reduce(squares, ap, ap, 1.0, 0.0, ALU.mult, ALU.add, r[0:n, j:j + 1]))
            else:
                sq = self.A(self.act.activation(squares, ap, ACT.Square, accum_out=r[0:n, j:j + 1]))
            wait(self.pool, sq)
            wait(self.pool, self.G(self.pool.tensor_scalar(r[0:n, 4 + j:5 + j], r[0:n, j:j + 1], 1.0 / D, EPS, ALU.mult, ALU.add)))
            marks.append(self.inverse_root(self.rstd[0:n, j:j + 1], r[0:n, 4 + j:5 + j]))
        return marks

    def norm_cols(self, tiles, gain):
        self.meet()
        with self.nc.sbuf_tensor(f"normed{self.n_block}", [P, len(tiles), D], F32) as hn:
            scale = self.rms_scale([(ap, n) for ap, n, _ in tiles])
            for j, (ap, n, _) in enumerate(tiles):
                if j % 2 == 0:
                    wait(self.dve, scale[j])
                    done = self.V(self.dve.tensor_scalar(hn[0:n, j, :], ap, self.rstd[0:n, j:j + 1], None, ALU.mult))
                else:
                    wait(self.act, scale[j])
                    done = self.A(self.act.activation(hn[0:n, j, :], ap, ACT.Copy, scale=self.rstd[0:n, j:j + 1]))
                wait(self.pe, done)
            self.turn_cols(tiles, [hn[0:n, j, :] for j, (_, n, _) in enumerate(tiles)], KD, self.x,
                           lambda k: gain[:, k:k + 1])

    def turn_cols(self, tiles, rows, pieces, out, gain=None):
        width = max(c + n for _, n, c in tiles)
        moved = {}
        for k in range(pieces):
            wait(self.pe, moved.get(k - 8))
            for (_, n, c), r in zip(tiles, rows):
                tr = self.pe.transpose(self.bank(k % 8)[:, c:c + n], r[:, k * P:(k + 1) * P], self.C["ident"][0:n, 0:n])
            src, (hi, lo) = self.bank(k % 8, width), (y[:, k, 0:width] for y in out)
            wait(self.act, self.T(tr))
            if gain:
                wait(self.dve, self.A(self.act.activation(hi, src, ACT.Copy, scale=gain(k))))
                moved[k] = self.V(self.dve.scalar_tensor_tensor(lo, src, gain(k), hi, ALU.mult, ALU.subtract))
            else:
                moved[k] = self.split(src, (hi, lo))
        wait(self.pe, moved[pieces - 1])

    def setup(self):
        nc = self.nc
        self.raw = [self.sb(f"weights{s}", [P, BLK]) for s in range(SLOTS)]
        self.w_hi = [self.sb(f"weights_hi{s}", [P, BLK], F32R) for s in range(SLOTS)]
        self.w_lo = [self.sb(f"weights_lo{s}", [P, BLK], F32R) for s in range(SLOTS)]
        self.psum = nc.alloc_psum_tensor("banks", [P, 8 * BANK], F32)
        self.h = self.sb("h", [P, NT, D])
        self.x = [self.sb(n, [P, KD, SM], F32R) for n in ("x_hi", "x_lo")]
        self.stat = self.sb("stat", [P, 16])
        self.rstd = self.sb("rstd", [P, 4])
        self.power = self.sb("power", [P, 1])
        self.meta = self.sb("meta_rows", [META, D])
        self.ret_stat = self.sb("ret_stat", [P, NT * RET_H, 12])
        self.C = {}
        self.c_load = Counter(nc.alloc_semaphore("constants_landed"), 16)
        self.x_in = Counter(nc.alloc_semaphore("x_landed"), 16)
        self.x_in.mark(self.act.dma_start(self.h[:, :, :], self.ins["x"].rearrange("o (t p) d -> p (o t) d", p=P)))
        self.load_constants("always", self.act, self.c_load)
        self.later_in = Counter(nc.alloc_semaphore("later_constants_landed"), 16)
        self.load_constants("first", self.act, self.later_in, self.first_block)
        self.later_in.mark(self.act.dma_start(self.meta[:, :], self.ins["meta"]))
        w = self.ins["weights"]
        n = w.shape[0]
        for s in range(SLOTS):
            self.sp.dma_start(self.raw[s][:, :], w[s]).then_inc(self.block_full[s], 16)
        with nc.Fori(1, n // SLOTS, engines=[ENG.SP]) as i:
            for s in range(SLOTS):
                self.sp.wait_ge(self.lo_made.sem, i * (PARTS * SLOTS) + PARTS * (s + 1 - SLOTS))
                self.sp.dma_start(self.raw[s][:, :], w[bass.ds(i * SLOTS + s, 1), :, :].rearrange("o p n -> p (o n)"))\
                    .then_inc(self.block_full[s], 16)
        for b in range(SLOTS):
            self.split_block(0, SLOTS, b)
        for k in range(4):
            self.out_v.mark(self.dve.memset(self.stat[:, k:k + 1], 0.0))
            self.V(self.dve.memset(self.stat[:, 4 + k:5 + k], 0.0))
        for e in (self.pe, self.dve, self.act, self.pool):
            wait(e, self.c_load.now(), self.x_in.now())
        for k in range(4):
            self.out_a.mark(self.act.activation(self.stat[:, 8 + k:9 + k], self.C["ident"][:, 0:1], ACT.Copy))
            self.A(self.act.activation(self.stat[:, 12 + k:13 + k], self.C["ident"][:, 0:1], ACT.Copy))
        wait(self.pool, self.G(self.pool.memset(self.power[:, :], -0.5)))

    def load_constants(self, group, engine, counter, stack=None):
        ap = self.ins["constants_" + group]
        t = stack.enter_context(self.nc.sbuf_tensor("sb_" + group, list(ap.shape), F32)) if stack \
            else self.sb("sb_" + group, list(ap.shape))
        for name, (rows, at, n) in self.where[group].items():
            self.C[name] = t[0:rows, at:at + n]
        return counter.mark(engine.dma_start(t[:, :], ap))

    def h_tiles(self):
        return [(self.h[:, t, :], P, t * P) for t in range(NT)]

    def put(self, dst):
        def piece(i, j):
            return dst[:, bass.ds(i * (2 * TURN) + j, 1), :].rearrange("p o n -> p (o n)")

        return lambda i, s, ps: (self.dve.tensor_copy(piece(i, 2 * s), ps[:, 0, :]),
                                 self.act.activation(piece(i, 2 * s + 1), ps[:, 1, :], ACT.Copy))

    def add_to_h(self, i, u, t, ps, turn_halves):
        at = bass.ds((i * turn_halves + u) * BANK, BANK)
        return self.dve.tensor_tensor(self.h[:, t, at], self.h[:, t, at], ps, ALU.add)

    def stick_breaking(self):
        nc, pe, dve, act, pool = self.nc, self.pe, self.dve, self.act, self.pool
        self.norm_cols(self.h_tiles(), self.C["g_mix0"])
        with nc.sbuf_tensor("sb_qk", [P, 16, S], F32) as qk, nc.sbuf_tensor("sb_v", [P, NT, D], F32) as v, \
                nc.sbuf_tensor("sb_o_hi", [P, KD, S], F32R) as o_hi, nc.sbuf_tensor("sb_o_lo", [P, KD, S], F32R) as o_lo, \
                nc.sbuf_tensor("sb_e", [P, 2, 2, 384], F32) as e, nc.sbuf_tensor("sb_sp", [P, 2, 2, 384], F32) as sp, \
                nc.sbuf_tensor("sb_a", [P, 2, 2, 384], F32) as a, \
                nc.sbuf_tensor("sb_z", [P, 3, 2, 384], F32) as zs:
            self.dense_cols(8, self.x, S, self.put(qk))
            self.dense_rows(KD, 2, self.x, lambda i, u, t, ps: dve.tensor_copy(v[:, t, u * BANK:(u + 1) * BANK], ps))
            act.preload_act_table_set("natural_log_exp_and_others")
            self.meet()
            for engine in (pe, dve, act, pool):
                wait(engine, self.later_in.now())
            self.V(dve.tensor_scalar(qk[:, 0:8, :], qk[:, 0:8, :], SB_D ** -0.5, None, ALU.mult))
            wait(pe, self.c_dve.now())

            def banks(first, n=384):
                return self.psum[:, first * BANK:(first + 2) * BANK].rearrange("p (b n) -> p b n", b=2)[:, :, 0:n]

            pairs, m = SB_H // 2, {}

            def logits(c):
                wait(pe, m.get(("z copied", c - 2)))
                for j in range(2):
                    r = slice(64 * j, 64 * j + 64)
                    z = self.bank(2 * (c % 2) + j)
                    pe.matmul(z[:, 0:S], qk[r, 8 + c, 0:P], qk[r, c, 0:S], start=True, stop=True)
                    mm = pe.matmul(z[:, S:384], qk[r, 8 + c, P:S], qk[r, c, P:S], start=True, stop=True)
                m["z", c] = self.T(mm)

            def log1p(c):
                b = c % 2
                wait(act, m["exp", c])
                m["ln", c] = self.A(act.activation(e[:, b], e[:, b], ACT.Ln, bias=1.0))
                wait(dve, m["ln", c], m.get(("sums", c - 2)))
                m["sp", c] = self.V(dve.scalar_tensor_tensor(sp[:, b], zs[:, c % 3], 0.0, e[:, b], ALU.max, ALU.add))
                wait(pool, m["sp", c])
                keep = self.C["sb_keep"][:, None, :].to_broadcast([P, 2, 384])
                m["keep", c] = self.G(pool.tensor_tensor(sp[:, b], sp[:, b], keep, ALU.mult))

            def cumulate(c):
                b = c % 2
                wait(pe, m["keep", c], m.get(("o moved", c - 2)))
                for j in range(2):
                    L = self.bank(4 + 2 * b + j)
                    pe.matmul(L[:, 0:S], self.C["from_here"][:, :], sp[:, b, j, 0:S], start=True, stop=False)
                    pe.matmul(L[:, P:S], self.C["ones"][:, :], sp[:, b, j, S:384], start=False, stop=True)
                    mm = pe.matmul(L[:, S:384], self.C["from_here"][:, :], sp[:, b, j, S:384], start=True, stop=True)
                m["sums", c] = self.T(mm)
                wait(dve, m["sums", c], m.get(("o", c - 2)))
                m["d", c] = self.V(dve.tensor_tensor(a[:, b], zs[:, c % 3], banks(4 + 2 * b), ALU.subtract))
                wait(pool, m["d", c])
                cap = self.C["sb_cap"][:, None, :].to_broadcast([P, 2, 384])
                m["masked", c] = self.G(pool.tensor_tensor(a[:, b], a[:, b], cap, ALU.add))

            def exp_abs(c):
                b, z = c % 2, zs[:, c % 3]
                wait(act, m["z", c], m.get(("d", c - 3)))
                m["z copied", c] = self.A(act.activation(z, banks(2 * b), ACT.Copy))
                wait(dve, m["z copied", c], m.get(("sp", c - 2)))
                x = self.V(dve.scalar_tensor_tensor(e[:, b], z, -1.0, z, ALU.mult, ALU.min))
                wait(act, x)
                m["exp", c] = self.A(act.activation(e[:, b], e[:, b], ACT.Exp))

            def weights(c):
                wait(act, m["masked", c])
                m["a", c] = self.A(act.activation(a[:, c % 2], a[:, c % 2], ACT.Exp))

            def values(c):
                b = c % 2
                wait(pe, m["a", c])
                for j in range(2):
                    o = self.psum[64 * j:64 * j + 64, (4 + 2 * b) * BANK:(4 + 2 * b) * BANK + S]
                    f = slice((2 * c + j) * SB_D, (2 * c + j + 1) * SB_D)
                    pe.matmul(o[:, 0:S], v[:, 0, f], a[:, b, j, 0:S], start=True, stop=False)
                    mm = pe.matmul(o[:, P:S], v[:, 1, f], a[:, b, j, S:384], start=False, stop=True)
                m["o", c] = self.T(mm)
                wait(act, m["o", c])
                wait(dve, m["o", c])
                m["o moved", c] = self.split(self.bank(4 + 2 * b, S), (o_hi[:, c, :], o_lo[:, c, :]))

            for c in range(pairs + 3):
                for stage, p in ((weights, c - 3), (logits, c), (log1p, c - 1), (cumulate, c - 2), (exp_abs, c), (values, c - 3)):
                    if 0 <= p < pairs:
                        stage(p)
            self.meet()
            self.dense_rows(KD, 2, (o_hi, o_lo), lambda i, u, t, ps: self.add_to_h(i, u, t, ps, 2))

    def mlp(self, gain, name):
        nc, dve, act = self.nc, self.dve, self.act
        self.norm_cols(self.h_tiles(), gain)
        with ExitStack() as stack:
            hi, lo = (stack.enter_context(nc.sbuf_tensor(f"mlp_{n}{name}", [P, HID // P, S], F32R)) for n in ("hi", "lo"))
            relu, sq = (stack.enter_context(nc.sbuf_tensor(f"mlp_{n}{name}", [P, TURN, 2, S], F32)) for n in ("relu", "sq"))

            def square(i, s, ps):
                at = bass.ds(i * (2 * TURN) + 2 * s, 2)
                r = self.A(act.activation(relu[:, s], ps, ACT.Relu))
                wait(dve, r)
                wait(act, r)
                h = self.out_a.mark(act.activation(hi[:, at, :], relu[:, s], ACT.Square))
                wait(dve, self.V(dve.tensor_tensor(sq[:, s], relu[:, s], relu[:, s], ALU.mult)), h)
                return dve.tensor_tensor(lo[:, at, :], sq[:, s], hi[:, at, :], ALU.subtract), None

            self.dense_cols(16, self.x, S, square, {self.c_act: TURN, self.c_dve: TURN})
            done = self.out_v.now(), self.out_a.now()
            wait(self.pe, *(Mark(m.counter, m.value - 2) for m in done))
            self.dense_rows(HID // P, 2, (hi, lo), lambda i, u, t, ps: self.add_to_h(i, u, t, ps, 1), done)

    def retention(self):
        nc, pe, dve, act, pool = self.nc, self.pe, self.dve, self.act, self.pool
        self.norm_cols(self.h_tiles(), self.C["g_mix1"])
        with nc.sbuf_tensor("ret_v", [P, NT, 2 * D], F32) as v, nc.sbuf_tensor("ret_g", [P, NT, 2 * D], F32) as g:
            self.retention_heads(v, g)
            self.meet()
            with nc.sbuf_tensor("ret_hi", [P, 2 * KD, S], F32R) as hi, nc.sbuf_tensor("ret_lo", [P, 2 * KD, S], F32R) as lo:
                self.turn_cols(self.h_tiles(), [g[:, t, :] for t in range(NT)], 2 * KD, (hi, lo))
                self.dense_rows(2 * KD, 2, (hi, lo), lambda i, u, t, ps: self.add_to_h(i, u, t, ps, 1))

    def retention_heads(self, v, g):
        nc, pe, dve, act, pool = self.nc, self.pe, self.dve, self.act, self.pool
        with nc.sbuf_tensor("ret_qk", [P, 16, S], F32) as qk, nc.sbuf_tensor("ret_rot", [P, 16, S], F32) as rot, \
                nc.sbuf_tensor("ret_tmp", [P, 8, S], F32) as tmp, nc.sbuf_tensor("ret_norm", [P, 2, RET_V], F32) as norm:
            self.dense_cols(8, self.x, S, self.put(qk))
            wait(dve, *self.scalar(), *self.vector())
            wait(pool, *self.scalar(), *self.vector())
            ready = []
            for e, mark, o in ((dve, self.V, 0), (pool, self.G, 8)):
                x = qk[:, o:o + 8, :].rearrange("p (h two) s -> p two h s", two=2)
                r = rot[:, o:o + 8, :].rearrange("p (h two) s -> p two h s", two=2)
                w = tmp[:, o // 2:o // 2 + 4, :]
                cos, sin = (self.C[n][:, None, :].to_broadcast([P, 4, S]) for n in ("cos", "sin"))
                for half, op in ((0, ALU.subtract), (1, ALU.add)):
                    a = mark(e.tensor_tensor(r[:, half], x[:, half], cos, ALU.mult))
                    b = mark(e.tensor_tensor(w, x[:, 1 - half], sin, ALU.mult))
                    wait(e, b)
                    a = mark(e.tensor_tensor(r[:, half], r[:, half], w, op))
                    wait(e, a)
                if o:
                    a = mark(e.tensor_scalar(rot[:, 8:16, :], rot[:, 8:16, :], RET_QK ** -0.5, None, ALU.mult))
                ready.append(a)
            self.dense_rows(KD, 4, self.x, lambda i, u, t, ps: dve.tensor_copy(v[:, t, bass.ds((i * 2 + u) * BANK, BANK)], ps))
            self.dense_rows(KD, 4, self.x, lambda i, u, t, ps: dve.tensor_copy(g[:, t, bass.ds((i * 2 + u) * BANK, BANK)], ps))
            wait(act, *self.vector())
            for t in range(NT):
                silu = self.A(act.activation(g[:, t, :], g[:, t, :], ACT.Silu))
            wait(pe, *ready, *self.vector())
            wait(dve, silu, *self.vector(), *ready)
            sc = qk[:, :, :].rearrange("p a b -> p (a b)")
            decay = self.C["decay"][:, :].rearrange("p (h n) -> p h n", h=RET_H)
            m = {}

            def scores(hd):
                b = self.bank(hd % 2)
                wait(pe, m.get(("sc", hd - 2)))
                for key, (q0, o) in enumerate(((0, 0), (P, S))):
                    for k in range(2):
                        mm = pe.matmul(b[:, o:o + S - q0], rot[:, 8 + 2 * hd + k, key * P:key * P + P],
                                       rot[:, 2 * hd + k, q0:S], start=(k == 0), stop=(k == 1))
                m["s", hd] = self.T(mm)
                wait(dve, m["s", hd])
                m["sc", hd] = self.V(dve.tensor_tensor(sc[:, hd * 384:hd * 384 + 384], b[:, 0:384], decay[:, hd], ALU.mult))

            def values(n):
                hd, t = n // NT, n % NT
                s_h, vh = sc[:, hd * 384:hd * 384 + 384], slice(hd * RET_V, (hd + 1) * RET_V)
                o = self.bank(2 + n % 6)
                wait(pe, m["sc", hd], m.get(("o", n - 6)))
                mm = pe.matmul(o, s_h[:, t * P:t * P + P], v[:, 0, vh], start=True, stop=(t == 0))
                if t:
                    mm = pe.matmul(o, s_h[:, S:384], v[:, 1, vh], start=False, stop=True)
                m["m", n] = self.T(mm)
                wait(dve, m["m", n])
                st = self.ret_stat[:, n, :]
                wait(dve, self.V(dve.bn_stats(st[:, 0:6], o)))
                wait(pool, self.V(dve.bn_aggr(st[:, 6:8], st[:, 0:6])))
                wait(pool, self.G(pool.tensor_scalar(st[:, 8:9], st[:, 7:8], EPS, None, ALU.add)))
                m["scale", n] = self.inverse_root(st[:, 10:11], st[:, 8:9])

            def gated(n):
                hd, t = n // NT, n % NT
                o, st, nrm, vh = self.bank(2 + n % 6), self.ret_stat[:, n, :], norm[:, n % 2, :], slice(hd * RET_V, (hd + 1) * RET_V)
                wait(dve, m["scale", n], m.get(("o", n - 2)))
                wait(dve, self.V(dve.tensor_scalar(nrm, o, st[:, 6:7], st[:, 10:11], ALU.subtract, ALU.mult)))
                m["o", n] = self.V(dve.tensor_tensor(g[:, t, vh], nrm, g[:, t, vh], ALU.mult))

            scores(0)
            for n in range(RET_H * NT + 1):
                if n % NT == 0 and n // NT + 1 < RET_H:
                    scores(n // NT + 1)
                if n < RET_H * NT:
                    values(n)
                if n:
                    gated(n - 1)

    def final_norm(self):
        dve = self.dve
        self.meet()
        wait(dve, *self.rms_scale([(ap, n) for ap, n, _ in self.h_tiles()]))
        for t in range(NT):
            self.V(dve.scalar_tensor_tensor(self.h[:, t, :], self.h[:, t, :], self.rstd[:, t:t + 1],
                                            self.C["g_final"][:, :], ALU.mult, ALU.mult))
        self.meet()
        self.first_block.close()

    def small_rows(self):
        self.act.preload_act_table_set("natural_log_exp_and_others")
        nc, pe, dve, act = self.nc, self.pe, self.dve, self.act
        with nc.sbuf_tensor("small_hi", [P, KD, 3 * H2], F32R) as hi, nc.sbuf_tensor("small_lo", [P, KD, 3 * H2], F32R) as lo:
            wait(pe, self.split(self.C["small"].rearrange("p (k n) -> p k n", k=KD), (hi[:, :, :], lo[:, :, :])))
            for g in range(3):
                for k in range(KD):
                    mm = self.product(self.bank(4 + g, SM)[0:H2, :], [y[:, k, g * H2:(g + 1) * H2] for y in (hi, lo)],
                                      [y[:, k, :] for y in self.x], k == 0, k == KD - 1)
        done = self.T(mm)
        b, a, f = (self.bank(4 + g, SM)[0:H2, :] for g in range(3))
        R = {n: self.lam[:, j, :] for j, n in enumerate(
            ("beta", "G", "nbe", "tail", "eG", "ncum", "y", "t", "u", "g"))}
        C = self.C

        def v(ins):
            wait(dve, self.V(ins))

        def soft(x):
            v(dve.scalar_tensor_tensor(R["t"], x, -1.0, x, ALU.mult, ALU.min))
            wait(act, self.c_dve.now())
            wait(act, self.A(act.activation(R["t"], R["t"], ACT.Exp)))
            wait(dve, self.A(act.activation(R["t"], R["t"], ACT.Ln, bias=1.0)))

        wait(act, done)
        wait(dve, done)
        wait(dve, self.A(act.activation(R["u"], b, ACT.Exp, scale=-1.0)))
        v(dve.tensor_scalar(R["u"], R["u"], 1.0, None, ALU.add))
        v(dve.reciprocal(R["beta"], R["u"]))
        ea = self.stat[0:H2, 0:1]
        self.A(act.activation(ea, C["a_log"][:, :], ACT.Exp))
        v(dve.tensor_scalar(R["y"], a, C["dt_bias"][:, 0:1], None, ALU.add))
        soft(R["y"])
        v(dve.scalar_tensor_tensor(R["t"], R["y"], 0.0, R["t"], ALU.max, ALU.add))
        v(dve.tensor_scalar(R["g"], R["t"], ea, -1.0, ALU.mult, ALU.mult))
        ones = C["ones"][0:H2, :]
        for c, n in TILES:
            v(dve.tensor_tensor_scan(R["G"][:, c:c + n], ones[:, 0:n], R["g"][:, c:c + n], 0.0, ALU.mult, ALU.add))
        wait(act, self.c_dve.now())
        self.A(act.activation(R["eG"], R["G"], ACT.Exp))
        for c, n in TILES:
            self.A(act.activation(R["tail"][:, c:c + n], R["G"][:, c:c + n], ACT.Exp, scale=-1.0,
                                  bias=R["G"][:, c + n - 1:c + n]))
        wait(dve, self.c_act.now())
        v(dve.scalar_tensor_tensor(R["nbe"], R["beta"], -1.0, R["eG"], ALU.mult, ALU.mult))
        v(dve.tensor_scalar(R["y"], f, C["f_bias"][:, 0:1], None, ALU.add))
        soft(R["y"])
        v(dve.tensor_scalar(R["y"], R["y"], -1.0, 0.0, ALU.mult, ALU.max))
        v(dve.tensor_tensor(R["t"], R["t"], R["y"], ALU.add))
        v(dve.memset(R["u"], 1.0))
        v(dve.tensor_tensor_scan(R["ncum"], R["u"], R["t"], 0.0, ALU.mult, ALU.add))
        return R

    def token_columns(self):
        pe, dve, C = self.pe, self.dve, self.C
        ps = self.bank(3)
        for t, (c, n) in enumerate(TILES):
            for j in range(4):
                o = (4 * t + j) * H2
                tr = pe.transpose(ps[0:n, o:o + H2], self.lam[:, j, c:c + n], C["ident"][0:H2, 0:H2])
        wait(dve, self.T(tr))
        w = 4 * H2
        self.V(dve.tensor_copy(self.tok[0:META, 0:w], ps[0:META, 0:w]))
        self.V(dve.tensor_copy(self.tok[:, w:3 * w], ps[:, w:3 * w]))

    def token_scalar(self, t, j, h):
        o = (4 * t + j) * H2 + h
        return self.tok[0:TILES[t][1], o:o + 1]

    def rms_rows(self, xs, width, total, eps, squares, meanwhile=None):
        pe, dve, act = self.pe, self.dve, self.act
        made = []
        wait(act, *self.vector())
        for x, sq in zip(xs, squares):
            made.append(self.A(act.activation(sq, x, ACT.Square)))
        if meanwhile:
            meanwhile()
        read, ready = [], []
        for j, mark in enumerate(made):
            rows, sums = self.lam[:, 9 - j, 0:width], self.bank(7 - j, width)[0:H2, :]
            wait(pe, mark, *self.vector())
            for k in range(H2):
                mm = pe.matmul(sums, self.C["to_row"][:, k * H2:(k + 1) * H2], squares[j][:, k, :], start=(k == 0), stop=(k == H2 - 1))
            wait(dve, self.T(mm))
            read.append(self.V(dve.tensor_scalar(rows, sums, 1.0 / total, eps, ALU.mult, ALU.add)))
        for j, mark in enumerate(read):
            rows = self.lam[:, 9 - j, 0:width]
            wait(act, mark)
            wait(act, self.A(act.activation(rows, rows, ACT.Ln)))
            ready.append(self.A(act.activation(rows, rows, ACT.Exp, scale=-0.5)))
        return read, ready

    def scale_by_rows(self, xs, width, gains, marks):
        pe, dve = self.pe, self.dve
        read, ready = marks
        used = {}
        wait(pe, *read)
        for j, (x, gain) in enumerate(zip(xs, gains)):
            rows = self.lam[:, 9 - j, 0:width]
            for half in range(2):
                wait(pe, ready[j], used.get(half))
                for k in range(4 * half, 4 * half + 4):
                    mm = pe.matmul(self.bank(k, width), self.C["pick"][:, k * P:(k + 1) * P], rows, start=True, stop=True)
                wait(dve, self.T(mm))
                r = self.psum[:, :].rearrange("p (b n) -> p b n", b=8)[:, 4 * half:4 * half + 4, 0:width]
                part = x[:, 4 * half:4 * half + 4, :]
                used[half] = self.V(dve.scalar_tensor_tensor(part, part, gain, r, ALU.mult, ALU.mult))

    def mixer(self):
        with self.nc.sbuf_tensor("obT", [P, H2, S], F32) as self.obT, \
                self.nc.sbuf_tensor("oaT", [P, H2, S], F32) as self.oaT, \
                self.nc.sbuf_tensor("lam", [H2, 10, SM], F32) as self.lam:
            self.mixer_stages()

    def mixer_stages(self):
        nc, pe, dve, act, pool, C = self.nc, self.pe, self.dve, self.act, self.pool, self.C
        tiles = [(self.meta[:, :], META, 0)] + [(self.h[:, t, :], P, META + t * P) for t in range(NT)]
        self.norm_cols(tiles, C["g_mixer"])
        xs = [y[:, :, META:SM] for y in self.x]
        with nc.sbuf_tensor("tok", [P, 12 * H2], F32) as tok:
            self.tok = tok
            R = self.small_rows()
            with nc.sbuf_tensor("conv_out", [P, CONV_CH // P, SM], F32) as y:
                self.convolved(y)
                for group in range(2):
                    self.meet()
                    self.delta_group(group, y, R)
            self.meet()
            self.delta_gate(xs)
            self.meet()
            self.forgetting(R)
        self.meet()
        self.merge_branches(xs)

    def convolved(self, y):
        stack = ExitStack()
        nc, pe, dve, act, C = self.nc, self.pe, self.dve, self.act, self.C
        pad = CONV_K - 1
        w = C["conv"].rearrange("p (c k) -> p c k", k=CONV_K)
        with nc.sbuf_tensor("conv_in", [P, 2 * TURN, pad + SM], F32) as cin:
            self.V(dve.memset(cin[:, :, 0:pad], 0.0))

            def convolve(i, s, ps):
                moved = self.out_a.mark(act.activation(cin[:, 2 * s:2 * s + 2, pad:], ps, ACT.Copy))
                wait(dve, moved)
                done = {}
                for tap in range(CONV_K):
                    for j in (2 * s, 2 * s + 1):
                        x = cin[:, j, tap:tap + SM]
                        out = y[:, bass.ds(i * (2 * TURN) + j, 1), :].rearrange("p o n -> p (o n)")
                        wt = w[:, bass.ds(i * (2 * TURN) + j, 1), tap:tap + 1].rearrange("p o n -> p (o n)")
                        if tap == 0:
                            ins = dve.tensor_scalar(out, x, wt, None, ALU.mult)
                        else:
                            wait(dve, done[j])
                            ins = dve.scalar_tensor_tensor(out, x, wt, out, ALU.mult, ALU.add)
                        if tap < CONV_K - 1 or j % 2 == 0:
                            done[j] = self.V(ins)
                return ins, None

            wait(dve, self.c_dve.now())
            self.dense_cols(CONV_CH // COLS_W, self.x, SM, convolve, {self.c_dve: TURN * (2 * CONV_K - 1)},
                            upper_banks=(*self.vector(), *self.scalar()))
        self.meet()
        self.token_columns()
        wait(pe, self.c_dve.now())
        parts = [y[:, j * H2:(j + 1) * H2, :] for j in range(3)]
        for x in parts[0:2]:
            silu = self.A(act.activation(x, x, ACT.Silu))
        wait(act, silu)

        def value_silu():
            self.A(act.activation(parts[2], parts[2], ACT.Silu))
            act.preload_act_table_set("natural_log_exp_and_others")

        squares = [stack.enter_context(nc.sbuf_tensor(f"conv_sq{j}", [P, H2, SM], F32))[:, :, :] for j in range(2)]
        marks = self.rms_rows(parts[0:2], SM, 1.0, EPS, squares, value_silu)
        self.scale_by_rows(parts[0:2], SM, (DH ** -0.5, 1.0), marks)
        stack.close()

    def delta_group(self, group, conv, R):
        nc, pe, dve, act, pool, C = self.nc, self.pe, self.dve, self.act, self.pool, self.C
        HG = 4
        stack = ExitStack()

        def sb(name, shape):
            return stack.enter_context(nc.sbuf_tensor(f"{name}{group}", shape, F32))

        def four(ap, n=P):
            return ap.rearrange("p (h n) -> p h n", h=HG)[:, :, 0:n]

        kb = sb("dkb", [P, HG, SM])
        qe = sb("dqe", [P, HG, S])
        last_decay = sb("dlast", [P, HG, 3])
        q, k, v = (conv[:, j * H2 + group * HG:j * H2 + (group + 1) * HG, :] for j in range(3))
        gam = sb("dgam", [P, HG, SM])
        used = {}
        for j, name in enumerate(("beta", "eG", "G")):
            first = HG * (j % 2)
            wait(pe, used.get(j - 2))
            for hh in range(HG):
                h = group * HG + hh
                mm = pe.matmul(self.bank(first + hh, SM), C["pick"][0:H2, h * P:(h + 1) * P], R[name], start=True, stop=True)
            wait(dve, self.T(mm))
            rows = self.psum[:, first * BANK:(first + HG) * BANK].rearrange("p (b n) -> p b n", b=HG)
            if name == "beta":
                self.V(dve.tensor_tensor(kb[:, :, :], k, rows[:, :, 0:SM], ALU.mult))
            elif name == "eG":
                self.V(dve.tensor_tensor(qe[:, :, :], q[:, :, META:SM], rows[:, :, META:SM], ALU.mult))
                for t, (c, n) in enumerate(TILES):
                    self.V(dve.tensor_copy(last_decay[:, :, t:t + 1], rows[:, :, c + n - 1:c + n]))
            else:
                for t, (c, n) in enumerate(TILES):
                    for hh in range(HG):
                        g = self.V(dve.tensor_scalar(gam[0:n, hh, c:c + n], self.bank(hh)[0:n, c:c + n],
                                                     self.token_scalar(t, 1, group * HG + hh), 0.0, ALU.subtract, ALU.min))
                wait(act, g)
                for c, n in TILES:
                    self.A(act.activation(gam[0:n, :, c:c + n], gam[0:n, :, c:c + n], ACT.Exp))
            used[j] = self.c_dve.now()
        self.meet()
        A, AT, B, T, TT, M1 = (sb(n, [P, 2, HG * P]) for n in ("dA", "dAT", "dB", "dT", "dTT", "dM"))
        small = {n: sb(n + "m", [META, HG * META]) for n in ("dA", "dAT", "dB", "dT", "dTT", "dM")}
        attn = sb("dattn", [P, 2, HG * P])
        ktail, bv = sb("dkt", [P, 3, HG * P]), sb("dbv", [P, 3, HG * P])

        def of(x, name, t):
            n = TILES[t][1]
            return (small[name][:, :] if t == 0 else x[:, t - 1, :]).rearrange("p (h n) -> p h n", h=HG)

        products_read = rows_read = None
        for t, (c, n) in enumerate(TILES):
            tile = slice(c, c + n)
            kk, qk, kt, vt = (self.bank(b)[0:n, :] for b in range(4))
            wait(pe, products_read)
            for hh in range(HG):
                mm = pe.matmul(kk[:, hh * n:(hh + 1) * n], k[:, hh, tile], kb[:, hh, tile], start=True, stop=True)
                if t:
                    mm = pe.matmul(qk[:, hh * n:(hh + 1) * n], k[:, hh, tile], q[:, hh, tile], start=True, stop=True)
            done = self.T(mm)
            wait(pe, rows_read)
            for hh in range(HG):
                pe.transpose(kt[:, hh * P:(hh + 1) * P], k[:, hh, tile], C["ident"][:, :])
                mm = pe.transpose(vt[:, hh * P:(hh + 1) * P], v[:, hh, tile], C["ident"][:, :])
            wait(act, self.T(mm))
            for hh in range(HG):
                h, f = group * HG + hh, slice(hh * P, (hh + 1) * P)
                self.A(act.activation(ktail[0:n, t, f], kt[:, f], ACT.Copy, scale=self.token_scalar(t, 3, h)))
                rows_read = self.A(act.activation(bv[0:n, t, f], vt[:, f], ACT.Copy, scale=self.token_scalar(t, 0, h)))
            wait(dve, done)
            at = of(AT, "dAT", t)
            earlier = C["earlier"][0:n, None, 0:n].to_broadcast([n, HG, n])
            products_read = self.V(dve.tensor_tensor(at, kk[:, 0:HG * n].rearrange("p (h n) -> p h n", h=HG), gam[0:n, :, tile], ALU.mult))
            wait(dve, products_read)
            masked = self.V(dve.tensor_tensor(at, at, earlier, ALU.mult))
            if t:
                x = attn[:, t - 1, :].rearrange("p (h n) -> p h n", h=HG)
                products_read = self.V(dve.tensor_tensor(x, qk[:, :].rearrange("p (h n) -> p h n", h=HG), gam[0:n, :, tile], ALU.mult))
                wait(dve, products_read)
                self.V(dve.tensor_tensor(x, x, C["not_later"][:, None, :].to_broadcast([P, HG, P]), ALU.mult))
            wait(pe, masked)
            back = self.bank(4 + t)[0:n, :]
            for hh in range(HG):
                mm = pe.transpose(back[:, hh * n:(hh + 1) * n], at[:, hh, :], C["ident"][0:n, 0:n])
            wait(act, self.T(mm))
            self.A(act.activation(of(A, "dA", t), back[:, 0:HG * n].rearrange("p (h n) -> p h n", h=HG), ACT.Copy))
            eye = C["ident"][0:n, None, 0:n].to_broadcast([n, HG, n])
            self.V(dve.tensor_copy(of(T, "dT", t), eye))
            self.V(dve.tensor_copy(of(TT, "dTT", t), eye))
        self.meet()
        levels = {0: 4, 1: 7, 2: 7}
        upd = {}
        for t in range(3):
            n = TILES[t][1]
            for name, x, mask, made, out in (("dB", A, "merge", B, T), ("dM", AT, "next", M1, TT)):
                m = C[mask][0:n, None, 0:n].to_broadcast([n, HG, n])
                src, b, o = of(x, {"dB": "dA", "dM": "dAT"}[name], t), of(made, name, t), of(out, {"dB": "dT", "dM": "dTT"}[name], t)
                e, mark = (pool, self.G) if t == 2 else (dve, self.V)
                wait(e, mark(e.tensor_tensor(b, src, m, ALU.mult)))
                upd["T", t] = mark(e.tensor_tensor(o, o, b, ALU.subtract))
            wait(act, upd["T", t])
        for lvl in range(1, 7):
            act_t = [t for t in range(3) if lvl < levels[t]]
            for t in act_t:
                n = TILES[t][1]
                m = C["merge"][0:n, None, lvl * P:lvl * P + n].to_broadcast([n, HG, n])
                wait(pool, upd.get(("M", t)), upd["T", t] if lvl == 1 else None)
                upd["B", t] = self.G(pool.tensor_tensor(of(B, "dB", t), of(A, "dA", t), m, ALU.mult))
            for t in act_t:
                n = TILES[t][1]
                b, tt = of(B, "dB", t), of(TT, "dTT", t)
                ps = self.bank([6, 0, 3][t])[0:n, :]
                wait(pe, upd["B", t], upd.get(("T", t)))
                for hh in range(HG):
                    mm = pe.matmul(ps[:, hh * n:(hh + 1) * n], b[:, hh, :], tt[:, hh, :], start=True, stop=True)
                upd["M", t] = self.T(mm)
                wait(act, upd["M", t])
                upd["M1", t] = self.A(act.activation(of(M1, "dM", t), ps[:, 0:HG * n].rearrange("p (h n) -> p h n", h=HG), ACT.Copy))
            for t in act_t:
                n = TILES[t][1]
                last = lvl == levels[t] - 1
                m1, tm, tt = of(M1, "dM", t), of(T, "dT", t), of(TT, "dTT", t)
                pz, pzt = self.bank([7, 1, 4][t])[0:n, :], self.bank([7, 2, 5][t])[0:n, :]
                if t == 0:
                    pzt = pzt[:, HG * META:]
                wait(pe, upd["M1", t])
                for hh in range(HG):
                    if not last:
                        pe.matmul(pz[:, hh * n:(hh + 1) * n], m1[:, hh, :], tm[:, hh, :], start=True, stop=True)
                    mm = pe.matmul(pzt[:, hh * n:(hh + 1) * n], tm[:, hh, :], m1[:, hh, :], start=True, stop=True)
                wait(dve, self.T(mm))
                if not last:
                    self.V(dve.tensor_tensor(tm, tm, pz[:, 0:HG * n].rearrange("p (h n) -> p h n", h=HG), ALU.subtract))
                upd["T", t] = self.V(dve.tensor_tensor(tt, tt, pzt[:, 0:HG * n].rearrange("p (h n) -> p h n", h=HG), ALU.subtract))
        self.meet()
        states, rhs, vn = sb("dS", [P, 2, HG * P]), sb("drhs", [P, HG * P]), sb("dvn", [P, HG * P])
        H = [slice(hh * P, (hh + 1) * P) for hh in range(HG)]
        for t, (c, n) in enumerate(TILES):
            tile, tt = slice(c, c + n), of(TT, "dTT", t)
            St, new = states[:, 1 - t % 2, :], states[:, t % 2, :]
            right = bv[0:n, t, :]
            if t:
                ks = self.bank(0)
                for hh in range(HG):
                    mm = pe.matmul(ks[:, H[hh]], k[:, hh, tile], St[:, H[hh]], start=True, stop=True)
                wait(dve, self.T(mm))
                for hh in range(HG):
                    x = self.V(dve.scalar_tensor_tensor(rhs[:, H[hh]], ks[:, H[hh]], self.token_scalar(t, 2, group * HG + hh),
                                                        bv[:, t, H[hh]], ALU.mult, ALU.add))
                wait(pe, x)
                right = rhs[:, :]
            pv = self.bank(1)[0:n, :]
            for hh in range(HG):
                mm = pe.matmul(pv[:, H[hh]], tt[:, hh, :], right[:, H[hh]], start=True, stop=True)
            wait(act, self.T(mm))
            wait(pe, self.A(act.activation(vn[0:n, :], pv, ACT.Copy)))
            ps = self.bank(2)
            for hh in range(HG):
                mm = pe.matmul(ps[:, H[hh]], ktail[0:n, t, H[hh]], vn[0:n, H[hh]], start=True, stop=True)
            s_done = self.T(mm)
            wait(dve, s_done)
            if t:
                for hh in range(HG):
                    x = self.V(dve.scalar_tensor_tensor(new[:, H[hh]], St[:, H[hh]], last_decay[:, hh, t:t + 1],
                                                        ps[:, H[hh]], ALU.mult, ALU.add))
                po, xc = self.bank(3 + t), slice(c - META, c - META + n)
                for hh in range(HG):
                    pe.matmul(po[:, H[hh]], St[:, H[hh]], qe[:, hh, xc], start=True, stop=False)
                    mm = pe.matmul(po[:, H[hh]], vn[:, H[hh]], attn[:, t - 1, H[hh]], start=False, stop=True)
                wait(dve, self.T(mm))
                self.V(dve.tensor_copy(self.oaT[:, group * HG:(group + 1) * HG, xc], po[:, :].rearrange("p (h n) -> p h n", h=HG)))
            else:
                x = self.V(dve.tensor_copy(new, ps))
            wait(pe, x)
        stack.close()

    def delta_gate(self, xs):
        nc, pe, dve, act = self.nc, self.pe, self.dve, self.act
        with nc.sbuf_tensor("zT", [P, H2, S], F32) as z, nc.sbuf_tensor("zs", [P, H2, S], F32) as sq:
            oa = self.oaT[:, :, :]
            rows = self.rms_rows([oa], S, DH, EPS, [sq[:, :, :]])
            wait(pe, *rows[0])

            def silu(i, s, ps):
                at = bass.ds(i * (2 * TURN) + 2 * s, 2)
                wait(dve, self.out_a.mark(act.activation(z[:, at, :], ps, ACT.Silu)))
                x = self.oaT[:, at, :]
                return dve.tensor_tensor(x, x, z[:, at, :], ALU.mult), None

            self.dense_cols(4, xs, S, silu)
            wait(dve, *self.scalar(), *self.vector())
            wait(pe, *self.scalar(), *self.vector())
            self.scale_by_rows([oa], S, [self.C["o_norm"]], rows)
            self.meet()

    def forgetting(self, R):
        nc, pe, dve, act, pool, C = self.nc, self.pe, self.dve, self.act, self.pool, self.C
        with ExitStack() as stack:
            def sb(name, shape):
                return stack.enter_context(nc.sbuf_tensor(name, shape, F32))
            qkv = sb("fa_qkv", [P, 3 * H2, SM])
            vb = sb("fa_v", [P, 3, H2 * P])
            sq = sb("fa_sq", [P, 2, H2, SM])

            self.dense_cols(3 * H2 * P // COLS_W, self.x, SM, self.put(qkv))
            self.meet()
            ws = self.stat[:, 0:1]
            self.V(dve.tensor_scalar(ws, C["q_norm"][:, 0:1], DH ** -0.5, None, ALU.mult))
            act.preload_act_table_set("natural_log_exp_and_others")
            qk = [qkv[:, j * H2:(j + 1) * H2, :] for j in range(2)]
            marks = self.rms_rows(qk, SM, DH, EPS, [sq[:, j] for j in range(2)])
            self.scale_by_rows(qk, SM, (ws, C["k_norm"][:, 0:1]), marks)
            q, k, v = (qkv[:, j * H2:(j + 1) * H2, :] for j in range(3))
            self.meet()
            moved = {}
            j = 0
            for t, (c, n) in enumerate(TILES):
                for half in range(2):
                    ps = self.bank(j)[0:n, :]
                    for hh in range(4):
                        tr = pe.transpose(ps[:, hh * P:(hh + 1) * P], v[:, 4 * half + hh, c:c + n], C["ident"][:, :])
                    tr = self.T(tr)
                    wait(act, tr)
                    self.A(act.activation(vb[0:n, t, half * 512:half * 512 + 512], ps, ACT.Copy))
                    j += 1
            wait(pe, self.c_act.now())
            m = {}
            xs = [sb(f"fa_x{b}", [P, SM]) for b in range(4)]
            pT = [sb(f"fa_p{b}", [P, 3, P]) for b in range(2)]
            st = sb("fa_stat", [P, 16, 4])
            units = [(h, t) for h in range(H2) for t in range(NT)]

            def scores(u):
                h, t = units[u]
                w = META + P * (t + 1)
                ps = self.bank(u % 4, w)
                wait(pe, m.get(("x", u - 4)))
                pe.matmul(ps, q[:, h, META + t * P:META + (t + 1) * P], k[:, h, 0:w], start=True, stop=False)
                m["z", u] = self.T(pe.matmul(ps, C["pick"][0:H2, h * P:(h + 1) * P], R["ncum"][:, 0:w], start=False, stop=True))

            def exponent(u):
                w = META + P * (units[u][1] + 1)
                ps = self.bank(u % 4, w)
                x = xs[u % 4][:, 0:w]
                wait(dve, m["z", u], m.get(("tr", u - 4)))
                m["x", u] = self.V(dve.tensor_tensor(x, ps, C["causal"][:, SM - w:SM], ALU.add))
                wait(dve, m["x", u])
                mx = self.V(dve.tensor_reduce(st[:, u, 0:1], x, AX, ALU.max, negate=True))
                wait(act, mx)
                m["e", u] = self.A(act.activation(x, x, ACT.Exp, bias=st[:, u, 0:1], accum_out=st[:, u, 1:2]))

            def normalise(u):
                h, t = units[u]
                w = META + P * (t + 1)
                x = xs[u % 4][:, 0:w]
                wait(dve, m["e", u])
                wait(dve, self.V(dve.reciprocal(st[:, u, 2:3], st[:, u, 1:2])))
                n_ = self.V(dve.tensor_scalar(x, x, st[:, u, 2:3], None, ALU.mult))
                ps = self.bank(4 + u % 2)
                wait(pe, n_, m.get(("pT", u - 2)))
                for j in range(t + 2):
                    c, n = TILES[j]
                    tr = pe.transpose(ps[0:n, j * P:(j + 1) * P], x[:, c:c + n], C["ident"][:, :])
                m["tr", u] = self.T(tr)

            def values(u):
                h, t = units[u]
                ps = self.bank(4 + u % 2)
                p = pT[u % 2]
                wait(act, m["tr", u], m.get(("o", u - 2)))
                self.A(act.activation(p[0:META, 0, :], ps[0:META, 0:P], ACT.Copy))
                m["pT", u] = self.A(act.activation(p[:, 1:t + 2, :], ps[:, P:(t + 2) * P].rearrange("p (a b) -> p a b", b=P), ACT.Copy))
                po = self.bank(6 + u % 2, P)
                wait(pe, m["pT", u], m.get(("ob", u - 2)))
                for j in range(t + 2):
                    n = TILES[j][1]
                    mm = pe.matmul(po, vb[0:n, j, h * P:(h + 1) * P], p[0:n, j, :], start=(j == 0), stop=(j == t + 1))
                m["o", u] = self.T(mm)
                wait(dve, m["o", u])
                m["ob", u] = self.V(dve.tensor_copy(self.obT[:, h, t * P:(t + 1) * P], po))

            for u in range(len(units) + 3):
                for stage, x in ((scores, u), (normalise, u - 2), (values, u - 3), (exponent, u - 1)):
                    if 0 <= x < len(units):
                        stage(x)
            self.meet()

    def merge_branches(self, xs):
        nc, dve, act = self.nc, self.dve, self.act
        with ExitStack() as stack:
            gates, y = (stack.enter_context(nc.sbuf_tensor(n, [P, 2 * KD, S], F32)) for n in ("gates", "branch_y"))
            pairs = [[stack.enter_context(nc.sbuf_tensor(f"branch_{n}{b}", [P, KD, S], F32R)) for n in ("hi", "lo")]
                     for b in range(2)]
            for o, pair in zip((self.oaT, self.obT), pairs):
                self.split(o[:, :, :], [x[:, :, :] for x in pair])

            def sigmoid(i, s, ps):
                g = [gates[:, bass.ds(i * (2 * TURN) + 2 * s + j, 1), :].rearrange("p o n -> p (o n)") for j in range(2)]
                moved = self.out_v.mark(dve.tensor_copy(g[0], ps[:, 0, :]))
                self.A(act.activation(g[1], ps[:, 1, :], ACT.Sigmoid))
                wait(act, moved)
                return None, act.activation(g[0], g[0], ACT.Sigmoid)

            def first(i, s, ps):
                at = slice(2 * s, 2 * s + 2)
                wait(dve, self.out_a.mark(act.activation(y[:, at, :], ps, ACT.Copy)))
                return dve.tensor_tensor(y[:, at, :], y[:, at, :], gates[:, at, :], ALU.mult), None

            def second(i, s, ps):
                at, at_b = slice(2 * s, 2 * s + 2), slice(KD + 2 * s, KD + 2 * s + 2)
                hi, lo = (x[:, at, :] for x in pairs[0])
                wait(dve, self.A(act.activation(y[:, at_b, :], ps, ACT.Copy)))
                wait(dve, self.V(dve.tensor_tensor(y[:, at_b, :], y[:, at_b, :], gates[:, at_b, :], ALU.mult)))
                total = self.V(dve.tensor_tensor(y[:, at, :], y[:, at, :], y[:, at_b, :], ALU.add))
                wait(act, total)
                wait(dve, total)
                wait(dve, self.out_a.mark(act.activation(hi, y[:, at, :], ACT.Copy)))
                return dve.tensor_tensor(lo, y[:, at, :], hi, ALU.subtract), None

            self.dense_cols(8, xs, S, sigmoid, {self.c_act: TURN})
            self.dense_cols(4, pairs[0], S, first)
            self.dense_cols(4, pairs[1], S, second, {self.c_act: TURN, self.c_dve: 2 * TURN})
            self.dense_rows(KD, 2, pairs[0], lambda i, u, t, ps: self.add_to_h(i, u, t, ps, 2))
            self.meet()

    def experts(self):
        nc, pe, dve, act, pool, C = self.nc, self.pe, self.dve, self.act, self.pool, self.C
        NU = 8
        late = Counter(nc.alloc_semaphore("expert_constants_landed"), 16)
        self.meet()
        self.load_constants("peer", act, late)
        g_peer, keys = C["g_peer"], C["keys"]
        xb = self.sb("tokens", [P, NT, D])
        wait(dve, *self.rms_scale([(ap, n) for ap, n, _ in self.h_tiles()]), late.now())
        for t in range(NT):
            x = self.V(dve.scalar_tensor_tensor(xb[:, t, :], self.h[:, t, :], self.rstd[:, t:t + 1], g_peer, ALU.mult, ALU.mult))
        wait(pe, x)
        self.turn_cols(self.h_tiles(), [xb[:, t, :] for t in range(NT)], KD, self.x)
        sc = self.sb("key_scores", [P, NT, 2 * PEER_H * KEYS])
        with nc.sbuf_tensor("queries", [P, 2 * PEER_H, S], F32) as qh:
            self.dense_cols(8, self.x, S, self.put(qh), final=True)
            self.meet()
            wait(pe, late.now())
            for t in range(NT):
                for b in range(4):
                    ps = self.bank(4 * t + b)
                    for j in range(4):
                        c = 4 * b + j
                        mm = pe.matmul(ps[:, j * KEYS:(j + 1) * KEYS], qh[:, c, t * P:(t + 1) * P],
                                       keys[:, c * KEYS:(c + 1) * KEYS], start=True, stop=True)
                    mm = self.T(mm)
                    wait(dve, mm)
                    self.V(dve.tensor_copy(sc[:, t, b * BANK:(b + 1) * BANK], ps))
            self.meet()
        for t in range(NT):
            for half in range(2):
                mm = pe.matmul(self.bank(2 * t + half), C["ident"][:, :], self.h[:, t, half * BANK:(half + 1) * BANK],
                               start=True, stop=False, skip_group_check=True)
        self.T(mm)

        u_rows = [self.sb(f"u_rows{j}", [P, D]) for j in range(NU)]
        v_rows = [self.sb(f"v_rows{j}", [P, D]) for j in range(NU)]
        u_in = [nc.alloc_semaphore(f"u_landed{j}") for j in range(NU)]
        v_in = [nc.alloc_semaphore(f"v_landed{j}") for j in range(NU)]
        dots, added = Counter(nc.alloc_semaphore("dots_done")), Counter(nc.alloc_semaphore("rows_added"))
        w = self.sb("pick_from", [P, 2 * KEYS])
        w2 = self.sb("pick_rest", [P, 2 * KEYS])
        best = self.sb("best", [P, 2, TOPK])
        where = self.sb("where", [P, 2, TOPK], U32)
        wheref = self.sb("wheref", [P, 2, TOPK])
        top = [self.sb(f"top{t}", [P, TOPK]) for t in range(NT)]
        ci = self.sb("ci", [P, TOPK], U32)
        part = self.sb("part", [P, 2, TOPK], U32)
        partf = self.sb("partf", [P, 2, TOPK])
        hot = self.sb("hot", [P, 2, TOPK, TOPK])
        half_index = self.sb("half_index", [P, 2, TOPK])
        index = [self.sb(f"index{t}", [P, TOPK], I32) for t in range(NT)]
        gate = [self.sb(f"gate{t}", [P, TOPK]) for t in range(NT)]
        soft = self.sb("soft", [P, NT, 4])
        act_in = [self.sb(f"act_in{t}", [P, TOPK]) for t in range(NT)]
        coef = [self.sb(f"coef{t}", [P, TOPK]) for t in range(NT)]
        diag = self.sb("diag", [P, TOPK, P])
        for j in range(NU):
            dots.mark(dve.memset(w[:, j:j + 1], 0.0))
        for j in range(TOPK):
            added.mark(dve.memset(w[:, NU + j:NU + j + 1], 0.0))
        wait(dve, dots.now(), added.now())

        def v(ins):
            m = self.V(ins)
            wait(dve, m)
            return m

        def apart(engine):
            engine.nop(nofuse=True)

        after_index = [0] * NT

        def top16(values, rest, val, idx):
            apart(dve)
            v(dve.max(val[:, 0:8], values))
            apart(dve)
            self.V(dve.max_index(idx[:, 0:8], val[:, 0:8], values))
            v(dve.match_replace(rest, val[:, 0:8], values, NEG))
            apart(dve)
            v(dve.max(val[:, 8:16], rest))
            apart(dve)
            v(dve.max_index(idx[:, 8:16], val[:, 8:16], rest))

        def choose(i, t, free):
            v(dve.tensor_copy(w[:, :], sc[:, t, bass.ds(i * (2 * KEYS), 2 * KEYS)]))
            for j in range(2):
                f = slice(j * KEYS, (j + 1) * KEYS)
                top16(w[:, f], w2[:, f], best[:, j, :], where[:, j, :])
            v(dve.tensor_copy(wheref[:, :, :], where[:, :, :]))
            v(dve.tensor_tensor(w[:, :].rearrange("p (a b) -> p a b", a=TOPK), best[:, 0, :, None].to_broadcast([P, TOPK, TOPK]),
                                best[:, 1, None, :].to_broadcast([P, TOPK, TOPK]), ALU.add))
            top16(w[:, :], w2[:, :], top[t], ci)
            self.V(dve.tensor_scalar(part[:, 0, :], ci[:, :], 4, None, ALU.logical_shift_right))
            v(dve.tensor_scalar(part[:, 1, :], ci[:, :], TOPK - 1, None, ALU.bitwise_and))
            v(dve.tensor_copy(partf[:, :, :], part[:, :, :]))
            for j in range(2):
                v(dve.tensor_tensor(hot[:, j], C["iota"][:, None, :].to_broadcast([P, TOPK, TOPK]),
                                    partf[:, j, :, None].to_broadcast([P, TOPK, TOPK]), ALU.is_equal))
                v(dve.tensor_tensor(hot[:, j], hot[:, j], wheref[:, j, None, :].to_broadcast([P, TOPK, TOPK]), ALU.mult))
            v(dve.tensor_reduce(half_index[:, :, :], hot[:, :, :, :], AX, ALU.add))
            for sem, value in free:
                dve.wait_ge(sem, value)
            v(dve.scalar_tensor_tensor(index[t][:, :], half_index[:, 0, :], float(KEYS), half_index[:, 1, :], ALU.mult, ALU.add))
            after_index[t] = self.c_dve.value
            m = v(dve.tensor_scalar(soft[:, t, 0:1], top[t][:, 0:1], -1.0, None, ALU.mult))
            wait(act, m)
            m = self.A(act.activation(gate[t][:, :], top[t][:, :], ACT.Exp, bias=soft[:, t, 0:1], accum_out=soft[:, t, 1:2]))
            wait(dve, m)
            v(dve.reciprocal(soft[:, t, 2:3], soft[:, t, 1:2]))
            return v(dve.tensor_scalar(gate[t][:, :], gate[t][:, :], soft[:, t, 2:3], None, ALU.mult))

        def row_landed(i, t, k):
            return i * (NT * TOPK // NU * 16) + (t * (TOPK // NU) + k // NU + 1) * 16

        def read_before(c, base, i, t, k, back):
            return i * (NT * TOPK) + (base + t * TOPK + k + 1 - back)

        def unit(i, t, ready, following):
            wait(pool, ready)
            for rows, sems, counter, base, table in (
                    (u_rows, u_in, dots, NU, self.ins["expert_u"]), (v_rows, v_in, added, TOPK, self.ins["expert_v"])):
                for k in range(TOPK):
                    pool.wait_ge(counter.sem, read_before(counter, base, i, t, k, NU))
                    apart(pool)
                    pool.indirect_dma_start(rows[k % NU][:, :], None, table,
                                            bass.IndirectOffsetOnAxis(ap=index[t][:, k:k + 1], axis=0)).then_inc(sems[k % NU], 16)
            for k in range(TOPK):
                dve.wait_ge(u_in[k % NU], row_landed(i, t, k))
                dots.mark(dve.tensor_tensor_reduce(u_rows[k % NU][:, :], u_rows[k % NU][:, :], xb[:, t, :], 1.0, 0.0,
                                                   ALU.mult, ALU.add, act_in[t][:, k:k + 1]))
            wait(act, dots.now())
            m = self.A(act.activation(coef[t][:, :], act_in[t][:, :], ACT.Gelu))
            wait(dve, m)
            m = self.V(dve.tensor_tensor(coef[t][:, :], coef[t][:, :], gate[t][:, :], ALU.mult))
            wait(act, m)
            wait(dve, m)
            for k in range(TOPK):
                act.wait_ge(added.sem, read_before(added, TOPK, i, t, k, TOPK))
                d = self.A(act.activation(diag[:, k, :], C["ident"][:, :], ACT.Copy, scale=coef[t][:, k:k + 1]))
                wait(pe, d)
                pe.wait_ge(v_in[k % NU], row_landed(i, t, k))
                for half in range(2):
                    mm = pe.matmul(self.bank(2 * t + half), diag[:, k, :], v_rows[k % NU][:, half * BANK:(half + 1) * BANK],
                                   start=False, stop=False, skip_group_check=True)
                added.mark(mm)
            if following:
                free = [(v_in[j], row_landed(i, t, TOPK - NU + j)) for j in range(NU)]
                return choose(i + 1, t, free)

        for t in range(NT):
            choose(0, t, [])
        back = [self.c_dve.value - x for t, x in enumerate(after_index)]
        per = self.unit_counts(dots, added)

        def units(i, following):
            start, turn = self.c_dve.value, self.c_dve.loop
            for t in range(NT):
                unit(i, t, Mark(self.c_dve, start - back[t], turn), following)

        with loop(nc, PEER_H - 1, [ENG.PE, ENG.DVE, ENG.Activation, ENG.Pool], per) as i:
            units(i, True)
        units(PEER_H - 1, False)
        wait(dve, added.now())
        for t in range(NT):
            for half in range(2):
                self.V(dve.tensor_copy(self.h[:, t, half * BANK:(half + 1) * BANK], self.bank(2 * t + half)))

    def unit_counts(self, dots, added):
        return {dots: NT * TOPK, added: NT * TOPK, self.c_dve: 31 * NT, self.c_act: 18 * NT}

    def store(self):
        self.meet()
        wait(self.sp, *self.everything())
        done = Counter(self.nc.alloc_semaphore("stored"), 16)
        for t in range(NT):
            last = done.mark(self.sp.dma_start(self.out.rearrange("o (t p) d -> t p (o d)", p=P)[t], self.h[:, t, :]))
        wait(self.sp, last)

    def build(self):
        self.setup()
        self.stick_breaking()
        self.mlp(self.C["g_mlp0"], "0")
        self.retention()
        self.mlp(self.C["g_mlp1"], "1")
        self.final_norm()
        self.mixer()
        self.experts()
        self.store()


def program(nc, ins, out, where):
    with nc.allow_non_contiguous_dma(reason="layouts"):
        Program(nc, ins, out, where).build()


def host_arrays(a):
    weights, small = weight_stream(a)
    arrays = {"x": a["x"], "meta": a["meta_tokens_2"], "expert_u": a["expert_u_2"][0],
              "expert_v": a["expert_v_2"][0], "weights": weights}
    every = {**shape_constants(), **vectors(a), "small": small}
    groups = {"first": FIRST_BLOCK, "peer": PEER_ONLY}
    groups["always"] = [n for n in every if n not in FIRST_BLOCK and n not in PEER_ONLY]
    where = {}
    for group, names in groups.items():
        arrays["constants_" + group], where[group] = pack({n: every[n] for n in names})
    return {name: np.ascontiguousarray(v) for name, v in arrays.items()}, where


def kernel(**inputs):
    import concourse.bacc as bacc
    from concourse.bass_utils import run_bass_kernel_spmd

    arrays, where = host_arrays({k: np.asarray(v) for k, v in inputs.items()})
    nc = bacc.Bacc("TRN2", target_bir_lowering=False, num_devices=1)
    ins = {name: nc.dram_tensor(name, v.shape, mybir.dt.from_np(v.dtype), kind="ExternalInput").ap()
           for name, v in arrays.items()}
    out = nc.dram_tensor("out", (1, S, D), F32, kind="ExternalOutput").ap()
    program(nc, ins, out, where)
    r = run_bass_kernel_spmd(nc, [arrays], core_ids=[0])
    return r.results[0]["out"]
```
